# Optimizing a Trainium2 kernel written in Bass

```python
import jax, jax.numpy as jnp
from jax import lax
import numpy as np

D_MODEL = 1024
BATCH = 1
SEQ = 256
DEPTH = 2

SSD_EXPAND = 2
SSD_D_INNER = SSD_EXPAND * D_MODEL
SSD_HEAD_DIM = 64
SSD_HEADS = SSD_D_INNER // SSD_HEAD_DIM
SSD_GROUPS = 4
SSD_HEADS_PER_GROUP = SSD_HEADS // SSD_GROUPS
SSD_STATE = 128
SSD_CONV = 4
SSD_CHUNK = 128
SSD_CONV_CH = SSD_D_INNER + 2 * SSD_GROUPS * SSD_STATE
ATTN_HEADS = 16
ATTN_KV_HEADS = 2
ATTN_HEAD_DIM = 64
ATTN_WIDTH = ATTN_HEADS * ATTN_HEAD_DIM
Q_BLOCK = 128
TOPK_MAX = 256
IDX_HEADS = 8
IDX_DIM = 64
ROPE_THETA = 10000.0
MEM_LEN = 256
XATTN_HEADS = 4
XATTN_HEAD_DIM = D_MODEL // XATTN_HEADS
MOE_GROUPS = 4
MOE_EXPERTS_PER_GROUP = 8
MOE_EXPERTS = MOE_GROUPS * MOE_EXPERTS_PER_GROUP
MOE_D_FF = 256
MOE_TOPK_IN_GROUP = 2
RMS_EPS = 1e-6

IN_WIDTHS = (SSD_D_INNER, SSD_CONV_CH, SSD_HEADS, ATTN_WIDTH, ATTN_KV_HEADS * ATTN_HEAD_DIM,
             ATTN_KV_HEADS * ATTN_HEAD_DIM, IDX_HEADS * IDX_DIM, IDX_DIM, IDX_HEADS, D_MODEL, D_MODEL)
D_IN_PROJ = sum(IN_WIDTHS)

kernel_name = 'hybrid_ssd_dsa_hmoe_block'

F32 = jnp.float32

def rms_norm(x, g):
    xf = x.astype(F32)
    y = xf * lax.rsqrt(jnp.mean(xf * xf, axis=-1, keepdims=True) + RMS_EPS)
    return (y * g.astype(F32)).astype(x.dtype)

def rope_tables(seq, dim):
    inv = 1.0 / (ROPE_THETA ** (jnp.arange(0, dim, 2, dtype=F32) / dim))
    ang = jnp.arange(seq, dtype=F32)[:, None] * inv[None, :]
    return jnp.cos(ang), jnp.sin(ang)

def apply_rope(x, cos, sin):
    x1, x2 = jnp.split(x.astype(F32), 2, axis=-1)
    c = cos[None, :, None, :]
    s = sin[None, :, None, :]
    return jnp.concatenate([x1 * c - x2 * s, x1 * s + x2 * c], axis=-1).astype(x.dtype)

def ssd_branch(z, xbc, dt_raw, conv_w, conv_b, dt_bias, a_log, d_skip, norm_g):
    Bsz, S, _ = xbc.shape
    G, HG, P, N, L = SSD_GROUPS, SSD_HEADS_PER_GROUP, SSD_HEAD_DIM, SSD_STATE, SSD_CHUNK
    xbc = lax.conv_general_dilated(
        xbc, conv_w[:, None, :].astype(xbc.dtype), window_strides=(1,),
        padding=[(SSD_CONV - 1, 0)], dimension_numbers=('NWC', 'WIO', 'NWC'),
        feature_group_count=SSD_CONV_CH) + conv_b.astype(xbc.dtype)
    xbc = jax.nn.silu(xbc)
    xs, bm, cm = jnp.split(xbc, [SSD_D_INNER, SSD_D_INNER + G * N], axis=-1)
    xs = xs.reshape(Bsz, S, G, HG, P)
    bm = bm.reshape(Bsz, S, G, N)
    cm = cm.reshape(Bsz, S, G, N)
    dt = jax.nn.softplus(dt_raw.astype(F32) + dt_bias.astype(F32)).reshape(Bsz, S, G, HG)
    a_neg = -jnp.exp(a_log.astype(F32)).reshape(G, HG)
    nc = S // L

    def to_chunks(t):
        return jnp.moveaxis(t.reshape((Bsz, nc, L) + t.shape[2:]), 1, 0)

    causal = jnp.tril(jnp.ones((L, L), dtype=bool))[None, :, :, None, None]

    def step(state, inp):
        xc, bc, cc, dtc = inp
        xc, bc, cc = xc.astype(F32), bc.astype(F32), cc.astype(F32)
        acum = jnp.cumsum(dtc * a_neg, axis=1)
        seg = acum[:, :, None] - acum[:, None, :]
        decay = jnp.exp(jnp.where(causal, seg, -jnp.inf))
        xdt = xc * dtc[..., None]
        cb = jnp.einsum('btgn,bsgn->btsg', cc, bc)
        y_diag = jnp.einsum('btsg,btsgh,bsghp->btghp', cb, decay, xdt)
        y_off = jnp.einsum('btgn,bghpn->btghp', cc, state) * jnp.exp(acum)[..., None]
        tail = jnp.exp(acum[:, -1:] - acum)
        new_state = (state * jnp.exp(acum[:, -1])[..., None, None]
                     + jnp.einsum('bsgh,bsghp,bsgn->bghpn', tail, xdt, bc))
        return new_state, y_diag + y_off

    state0 = jnp.zeros((Bsz, G, HG, P, N), F32)
    _, ys = lax.scan(step, state0, (to_chunks(xs), to_chunks(bm), to_chunks(cm), to_chunks(dt)))
    y = jnp.moveaxis(ys, 0, 1).reshape(Bsz, S, G, HG, P)
    y = y + d_skip.astype(F32).reshape(G, HG)[None, None, :, :, None] * xs.astype(F32)
    y = y.reshape(Bsz, S, SSD_D_INNER) * jax.nn.silu(z.astype(F32))
    y = y.reshape(Bsz, S, SSD_GROUPS, SSD_D_INNER // SSD_GROUPS)
    y = y * lax.rsqrt(jnp.mean(y * y, axis=-1, keepdims=True) + RMS_EPS)
    y = y.reshape(Bsz, S, SSD_D_INNER) * norm_g.astype(F32)
    return y.astype(z.dtype)

def dsa_branch(q, k, v, qi, ki, wi):
    Bsz, S = q.shape[:2]
    topk = min(TOPK_MAX, S // 4)
    nb = S // Q_BLOCK
    rep = ATTN_HEADS // ATTN_KV_HEADS
    idx_scale = (IDX_DIM ** -0.5) * (IDX_HEADS ** -0.5)
    attn_scale = ATTN_HEAD_DIM ** -0.5
    key_pos = jnp.arange(S)
    ki32 = ki.astype(F32)

    def block(bi):
        q0 = bi * Q_BLOCK
        qb = lax.dynamic_slice_in_dim(q, q0, Q_BLOCK, axis=1)
        qib = lax.dynamic_slice_in_dim(qi, q0, Q_BLOCK, axis=1)
        wib = lax.dynamic_slice_in_dim(wi, q0, Q_BLOCK, axis=1)
        qpos = q0 + jnp.arange(Q_BLOCK)
        admissible = key_pos[None, :] <= qpos[:, None]
        rel = jax.nn.relu(jnp.einsum('bqhd,bsd->bqhs', qib.astype(F32), ki32))
        iscore = jnp.einsum('bqh,bqhs->bqs', wib.astype(F32) * idx_scale, rel)
        iscore = jnp.where(admissible[None], iscore, -jnp.inf)
        _, sel = lax.top_k(iscore, topk)
        valid = sel <= qpos[None, :, None]
        kg = jax.vmap(lambda kb, ib: kb[ib])(k, sel)
        vg = jax.vmap(lambda vb, ib: vb[ib])(v, sel)
        qg = qb.reshape(Bsz, Q_BLOCK, ATTN_KV_HEADS, rep, ATTN_HEAD_DIM).astype(F32)
        s = jnp.einsum('bqgrd,bqkgd->bqgrk', qg, kg.astype(F32)) * attn_scale
        s = jnp.where(valid[:, :, None, None, :], s, -jnp.inf)
        p = jax.nn.softmax(s, axis=-1)
        o = jnp.einsum('bqgrk,bqkgd->bqgrd', p, vg.astype(F32))
        return o.reshape(Bsz, Q_BLOCK, ATTN_WIDTH).astype(q.dtype)

    out = lax.map(block, jnp.arange(nb))
    return jnp.moveaxis(out, 0, 1).reshape(Bsz, S, ATTN_WIDTH)

def hybrid_mixer(hn, w_in, conv_w, conv_b, dt_bias, a_log, d_skip, ssd_norm, w_ssd_o, w_attn_o, w_out):
    Bsz, S, _ = hn.shape
    proj = hn @ w_in
    splits = [int(p) for p in np.cumsum(IN_WIDTHS)[:-1]]
    z, xbc, dt_raw, q, k, v, qi, ki, wi, g_ssd, g_attn = jnp.split(proj, splits, axis=-1)
    y_ssd = ssd_branch(z, xbc, dt_raw, conv_w, conv_b, dt_bias, a_log, d_skip, ssd_norm)
    cos_a, sin_a = rope_tables(S, ATTN_HEAD_DIM)
    cos_i, sin_i = rope_tables(S, IDX_DIM)
    q = apply_rope(q.reshape(Bsz, S, ATTN_HEADS, ATTN_HEAD_DIM), cos_a, sin_a)
    k = apply_rope(k.reshape(Bsz, S, ATTN_KV_HEADS, ATTN_HEAD_DIM), cos_a, sin_a)
    v = v.reshape(Bsz, S, ATTN_KV_HEADS, ATTN_HEAD_DIM)
    qi = apply_rope(qi.reshape(Bsz, S, IDX_HEADS, IDX_DIM), cos_i, sin_i)
    ki = apply_rope(ki[:, :, None, :], cos_i, sin_i)[:, :, 0, :]
    y_attn = dsa_branch(q, k, v, qi, ki, wi)
    merged = (jax.nn.sigmoid(g_ssd) * (y_ssd @ w_ssd_o)
              + jax.nn.sigmoid(g_attn) * (y_attn @ w_attn_o))
    return merged @ w_out

def cross_attention(hn, mn, w_cq, w_ckv, w_co):
    Bsz, S, _ = hn.shape
    M = mn.shape[1]
    q = (hn @ w_cq).reshape(Bsz, S, XATTN_HEADS, XATTN_HEAD_DIM)
    k, v = jnp.split(mn @ w_ckv, 2, axis=-1)
    k = k.reshape(Bsz, M, XATTN_HEADS, XATTN_HEAD_DIM)
    v = v.reshape(Bsz, M, XATTN_HEADS, XATTN_HEAD_DIM)
    s = jnp.einsum('bshd,bmhd->bhsm', q.astype(F32), k.astype(F32)) * (XATTN_HEAD_DIM ** -0.5)
    p = jax.nn.softmax(s, axis=-1)
    o = jnp.einsum('bhsm,bmhd->bshd', p, v.astype(F32)).reshape(Bsz, S, D_MODEL)
    return o.astype(hn.dtype) @ w_co

def hier_moe(hn, w_group, b_group, w_router, b_router, w_gate_e, w_up_e, w_down_e):
    Bsz, S, D = hn.shape
    t = hn.reshape(-1, D)
    n_tok = t.shape[0]
    g_logits = (t @ w_group).astype(F32) + b_group.astype(F32)
    g_prob = jax.nn.softmax(g_logits, axis=-1)
    g_sel = jnp.argmax(g_logits, axis=-1)
    g_w = jnp.take_along_axis(g_prob, g_sel[:, None], axis=-1)
    e_logits = ((t @ w_router).astype(F32) + b_router.astype(F32)).reshape(
        n_tok, MOE_GROUPS, MOE_EXPERTS_PER_GROUP)
    e_in_group = jnp.take_along_axis(e_logits, g_sel[:, None, None], axis=1)[:, 0]
    top_v, top_i = lax.top_k(e_in_group, MOE_TOPK_IN_GROUP)
    top_w = jax.nn.softmax(top_v, axis=-1) * g_w
    within = jnp.einsum('nk,nke->ne', top_w,
                        jax.nn.one_hot(top_i, MOE_EXPERTS_PER_GROUP, dtype=F32))
    combine = jax.nn.one_hot(g_sel, MOE_GROUPS, dtype=F32)[:, :, None] * within[:, None, :]
    out = jnp.zeros((n_tok, D), F32)
    for g in range(MOE_GROUPS):
        hid = (jax.nn.silu(jnp.einsum('nd,edf->nef', t, w_gate_e[g]))
               * jnp.einsum('nd,edf->nef', t, w_up_e[g]))
        hid = hid * combine[:, g, :, None].astype(hid.dtype)
        out = out + jnp.einsum('nef,efd->nd', hid, w_down_e[g]).astype(F32)
    return out.astype(hn.dtype).reshape(Bsz, S, D)

def setup_inputs(seed: int = 0) -> dict:
    key = jax.random.key(seed)
    ks = iter(jax.random.split(key, 40))

    def nrm(shape, scale):
        return jax.random.normal(next(ks), shape, F32) * scale

    def gain(shape):
        return 1.0 + nrm(shape, 0.02)

    D, L_ = D_MODEL, DEPTH
    dt0 = jnp.exp(jax.random.uniform(next(ks), (L_, SSD_HEADS), F32)
                  * (np.log(0.1) - np.log(1e-3)).astype(np.float32) + np.float32(np.log(1e-3)))
    dt_bias = dt0 + jnp.log(-jnp.expm1(-dt0))
    a_log = jnp.log(jax.random.uniform(next(ks), (L_, SSD_HEADS), F32, 1.0, 16.0))
    return {
        'x': nrm((BATCH, SEQ, D), 1.0),
        'mem': nrm((BATCH, MEM_LEN, D), 1.0),
        'norm_mix': gain((L_, D)),
        'w_in': nrm((L_, D, D_IN_PROJ), D ** -0.5),
        'conv_w': nrm((L_, SSD_CONV, SSD_CONV_CH), 0.5),
        'conv_b': nrm((L_, SSD_CONV_CH), 0.02),
        'dt_bias': dt_bias,
        'a_log': a_log,
        'd_skip': gain((L_, SSD_HEADS)),
        'ssd_norm': gain((L_, SSD_D_INNER)),
        'w_ssd_o': nrm((L_, SSD_D_INNER, D), SSD_D_INNER ** -0.5),
        'w_attn_o': nrm((L_, ATTN_WIDTH, D), ATTN_WIDTH ** -0.5),
        'w_out': nrm((L_, D, D), D ** -0.5),
        'norm_xattn': gain((L_, D)),
        'norm_mem': gain((L_, D)),
        'w_cq': nrm((L_, D, D), D ** -0.5),
        'w_ckv': nrm((L_, D, 2 * D), D ** -0.5),
        'w_co': nrm((L_, D, D), D ** -0.5),
        'norm_ffn': gain((L_, D)),
        'w_group': nrm((L_, D, MOE_GROUPS), D ** -0.5),
        'b_group': nrm((L_, MOE_GROUPS), 0.01),
        'w_router': nrm((L_, D, MOE_EXPERTS), D ** -0.5),
        'b_router': nrm((L_, MOE_EXPERTS), 0.01),
        'w_gate_e': nrm((L_, MOE_GROUPS, MOE_EXPERTS_PER_GROUP, D, MOE_D_FF), D ** -0.5),
        'w_up_e': nrm((L_, MOE_GROUPS, MOE_EXPERTS_PER_GROUP, D, MOE_D_FF), D ** -0.5),
        'w_down_e': nrm((L_, MOE_GROUPS, MOE_EXPERTS_PER_GROUP, MOE_D_FF, D), MOE_D_FF ** -0.5),
        'norm_final': gain((D,)),
    }

def reference(x, mem, norm_mix, w_in, conv_w, conv_b, dt_bias, a_log, d_skip, ssd_norm,
              w_ssd_o, w_attn_o, w_out, norm_xattn, norm_mem, w_cq, w_ckv, w_co, norm_ffn,
              w_group, b_group, w_router, b_router, w_gate_e, w_up_e, w_down_e, norm_final):
    h = x
    for l in range(DEPTH):
        hn = rms_norm(h, norm_mix[l])
        h = h + hybrid_mixer(hn, w_in[l], conv_w[l], conv_b[l], dt_bias[l], a_log[l], d_skip[l],
                             ssd_norm[l], w_ssd_o[l], w_attn_o[l], w_out[l])
        hn = rms_norm(h, norm_xattn[l])
        mn = rms_norm(mem, norm_mem[l])
        h = h + cross_attention(hn, mn, w_cq[l], w_ckv[l], w_co[l])
        hn = rms_norm(h, norm_ffn[l])
        h = h + hier_moe(hn, w_group[l], b_group[l], w_router[l], b_router[l],
                         w_gate_e[l], w_up_e[l], w_down_e[l])
    return rms_norm(h, norm_final)


_drawn_inputs = setup_inputs


def setup_inputs(seed=0):
    import zlib

    import numpy as np

    out = dict(_drawn_inputs(seed))
    spreads = {}
    factors = {'norm_xattn': 3.751,
     'norm_mem': 3.71,
     'b_router': 2.798,
     'norm_final': 21.92,
     'b_group': 5.451,
     'norm_ffn': 3.015}
    for name, (base, spread) in spreads.items():
        noise = np.random.default_rng([zlib.crc32(name.encode()), seed]).standard_normal(out[name].shape)
        drawn = base * np.exp(spread * noise) if base else spread * noise
        out[name] = __import__('jax').numpy.asarray(drawn.astype(out[name].dtype))
    for name, factor in factors.items():
        out[name] = (out[name] * factor).astype(out[name].dtype)
    return out
```

```python
import math
from contextlib import ExitStack

import concourse.bass as bass
from concourse import mybir

F32 = mybir.dt.float32
I32 = mybir.dt.int32
ALU = mybir.AluOpType
ACT = mybir.ActivationFunctionType
AX_X = mybir.AxisListType.X

P = 128
NEG = -1.0e30
TAKEN = -3.0e38
EPS = 1e-6

DEPTH, SEQ, D = 2, 256, 1024
TT = SEQ // P
KC = D // P
DI = 2 * D
SH, SP_, SG, SN = 32, 64, 4, 128
HG = SH // SG
CH = DI + 2 * SG * SN
CC = CH // P
TAPS = 4
AH, AKV, HD = 16, 2, 64
IH = 8
TOPK = SEQ // 4
XH, XD = 4, 256
G, E, F = 4, 8, 256
NCOL = 512
IDX_SCALE = HD ** -0.5 * IH ** -0.5

Z0 = 0
XBC0 = Z0 + DI
DT0 = XBC0 + CH
Q0 = DT0 + SH
K0 = Q0 + AH * HD
QI0 = K0 + 2 * AKV * HD
KI0 = QI0 + IH * HD
GS0 = KI0 + HD + IH
GA0 = GS0 + D

C_ID, C_TRI, C_TRIS, C_ONE, C_IOTA, C_CAUS, C_COS, C_SIN, C_PRIO, C_GI, C_MH = (
    0, 128, 256, 384, 512, 640, 768, 896, 1024, 1032, 1036)
C_W = 1044
P_CW, P_CB, P_NM, P_NX, P_NE, P_NF, P_SN, P_DTB, P_AL, P_DS, P_BR = (
    0, 96, 120, 128, 136, 144, 152, 168, 200, 232, 264)
P_W = 300

(R_LG, R_GM, R_OH, R_EQ, R_GD, R_GE, R_T2, R_PK, R_EI, R_V1, R_V2, R_O1, R_O2, R_DL, R_TW, R_GS, R_DN, R_WI, R_RK,
 R_CN, R_OW, R_FA, R_KY, R_GF) = (
    0, 72, 74, 82, 98, 106, 114, 116, 180, 196, 198, 200, 216, 232, 234, 236, 238, 240, 256,
    264, 268, 270, 278, 288)

ATT = [(0, r, i) for r in range(2) for i in range(2)] + [(1, r, i) for r in range(2) for i in range(4)]
SSD = [(t, g) for t in range(TT) for g in range(SG)]


def make_order():
    o = [("norm", 0)] + [("hT", 0, i) for i in range(4)]
    o += [("small",), ("kv",), ("qi",), ("xbc", 0), ("acum",), ("kT",), ("kiT",), ("qiT", 0), ("qiT", 1), ("xbc", 1)]
    o += [("idx", 0, r, 0) for r in range(2)] + [("topk", 0), ("xbc", 2)]
    o += [("idx", 1, r, i) for r in range(2) for i in range(2)] + [("topk", 1), ("xbc", 3), ("xbc", 4), ("xbc", 5)]
    o += [("q", 0), ("q", 1)] + [("xT", i) for i in range(8)] + [("bT",), ("cb", 0), ("cb", 1)]
    o += [("qT", i) for i in range(4)]
    for n, (t, g) in enumerate(SSD):
        o += [("decay", n)]
        if n:
            o += [("ssd", n - 1)]
        if n % 2 == 0:
            o += [("z", n // 2)]
    o += [("ssd", len(SSD) - 1)]
    for n in range(len(ATT) + 2):
        if n < len(ATT):
            o += [("score", n)]
        if 1 <= n <= len(ATT):
            o += [("probT", n - 1)]
        if n >= 2:
            o += [("pv", n - 2)]
        if n == 3:
            o += [("gate", 0, 0)]
        if n == 7:
            o += [("gate", 0, 1)]
    o += [("ynorm",)] + [("yT", i) for i in range(8)]
    o += [("ssdo", 0), ("ssdo", 1), ("gate", 1, 0), ("gate", 1, 1)]
    o += [("aT", i) for i in range(4)] + [("atto", 0), ("atto", 1)]
    o += [("mgT", i) for i in range(4)] + [("wo", 0), ("wo", 1)]
    o += [("memT", i) for i in range(4)] + [("ck", 0), ("ck", 1), ("cv", 0), ("cv", 1)]
    o += [("norm", 1)] + [("hT", 1, i) for i in range(4)] + [("cq", 0), ("cq", 1)]
    for n in range(6):
        if n < 4:
            o += [("xscore", n)]
        if 1 <= n <= 4:
            o += [("xprobT", n - 1)]
        if n >= 2:
            o += [("xpv", n - 2)]
    o += [("xoT", i) for i in range(4)] + [("co", 0), ("co", 1)]
    o += [("norm", 2)] + [("hT", 2, i) for i in range(4)] + [("router",), ("rank",)]
    return o


ORDER = make_order()
IDX = [st for st in ORDER if st[0] == "idx"]

JOBS_OF = {
    "hT": (1, "dve"), "small": (2, "dve"), "kv": (2, "dve"), "qi": (2, "dve"), "xbc": (2, "dve"),
    "acum": (1, "dve"), "kT": (1, "dve"), "kiT": (1, "dve"), "qiT": (1, "act"), "idx": (1, "act"), "q": (2, "dve"),
    "xT": (1, "act"), "bT": (1, "act"), "cb": (1, "dve"), "qT": (1, "act"), "decay": (2, "dve"),
    "z": (2, "act"), "score": (1, "dve"), "probT": (1, "act"), "pv": (1, "dve"), "gate": (2, "act"),
    "yT": (1, "dve"), "ssdo": (2, "dve"), "aT": (1, "act"), "atto": (2, "dve"), "mgT": (1, "act"),
    "wo": (2, "dve"), "memT": (1, "dve"), "ck": (2, "act"), "cv": (2, "act"), "cq": (2, "act"),
    "xscore": (1, "act"), "xprobT": (1, "act"), "xpv": (1, "dve"), "xoT": (1, "act"), "co": (2, "dve"),
    "router": (1, "dve"), "rank": (1, "dve"),
}


def ssd_jobs(n):
    return [("dve"), ("act" if SSD[n][0] == 0 else "dve")]


def make_jobs():
    jobs = []
    for st in ORDER:
        if st[0] == "ssd":
            jobs += [(st, i, own) for i, own in enumerate(ssd_jobs(st[1]))]
        elif st[0] in JOBS_OF:
            n, own = JOBS_OF[st[0]]
            jobs += [(st, i, own) for i in range(n)]
    return jobs


JOBS = make_jobs()
JOB = {(st, i): k for k, (st, i, _) in enumerate(JOBS)}
OWNER = [own for _, _, own in JOBS]
RANK = [sum(o == OWNER[k] for o in OWNER[:k + 1]) for k in range(len(JOBS))]
DRAINS = {own: OWNER.count(own) for own in ("dve", "act")}
NJ = len(JOBS)

CHUNKED = {"small": 1, "kv": 1, "qi": 1, "xbc": 1, "q": 1, "z": 1, "gate": 1, "ssdo": 2, "atto": 1, "wo": 1,
           "ck": 1, "cv": 1, "cq": 1, "co": 1, "router": 1}
CHUNKS = [(st, i) for st in ORDER if st[0] in CHUNKED for i in range(CHUNKED[st[0]])]
CHUNK = {c: k for k, c in enumerate(CHUNKS)}
W_SLOTS = 4

FIRST_BLOCK = 2
D_SLOTS = 2
NORMS = 5
NT = G + 1
NCH = len(CHUNKS)
PER_LAYER = NCH + NT * E
assert NCH % W_SLOTS == 0 and E % W_SLOTS == 0 and E % D_SLOTS == 0

V_LAYER, V_TILE = 198, 1
A_LAYER = 2


def last_job(c):
    (st, i) = CHUNKS[c]
    return JOB[(st, 1 if JOBS_OF[st[0]][0] == 2 else 0)]


def bc(ap, axis, n):
    ap = ap.unsqueeze(axis)
    shape = list(ap.shape)
    shape[axis] = n
    return ap.to_broadcast(shape)


class Steps:

    def __init__(self, eng, sem):
        self.eng, self.sem, self.base, self.n = eng, sem, 0, 0

    def at(self, base):
        self.base, self.n = base, 0

    def link(self, ins):
        self.n += 1
        ins.then_inc(self.sem, 1)
        self.eng.wait_ge(self.sem, self.base + self.n)


def trunk(nc, x, mem, w_in, w_ssd_o, w_attn_o, w_out, w_cq, w_ckv, w_co, w_group, w_router,
          w_gate, w_up, w_down, params, consts, gain_final, out):
    with ExitStack() as ctx:
        def sb(name, shape, dt=F32):
            return ctx.enter_context(nc.sbuf_tensor(name, shape, dt))

        def sem(name):
            return ctx.enter_context(nc.semaphore(name))

        wring = sb("wring", [P, W_SLOTS, KC, NCOL])
        h = sb("h", [P, TT, D])
        xn = sb("xn", [P, TT, D])
        hT = sb("hT", [P, KC, SEQ])
        big = sb("big", [P, CC * SEQ])
        xs = sb("xs", [P, TT, DI])
        gate = sb("gate", [P, TT, D])
        qbuf = sb("qbuf", [P, TT, D])
        qT = sb("qT", [P, KC, SEQ])
        scr = sb("scr", [P, 4096])
        att = sb("att", [P, 2048])
        kT = sb("kT", [P, AKV + 1, SEQ])
        qiT = sb("qiT", [P, IH // 2, SEQ])
        ktok = sb("ktok", [P, TT, AKV + 1, 2, HD])
        vtok = sb("vtok", [P, TT, AKV * HD])
        pen = sb("pen", [P, TT, SEQ])
        btok = sb("btok", [P, SG * SN])
        cst = sb("cst", [P, C_W])
        prm = sb("prm", [P, P_W])
        dtb = sb("dtb", [P, TT, SH])
        dta = sb("dta", [P, TT, SH])
        acum = sb("acum", [P, 3, SH])
        eac = sb("eac", [P, SH])
        tail = sb("tail", [P, SH])
        tmp32 = sb("tmp32", [P, 2, TT * SH])
        wis = sb("wis", [P, TT, IH])
        st_ = sb("sums", [P, 24])
        mx = sb("mx", [P, 4, 4])
        nmx = sb("nmx", [P, 4, 4])
        sm = sb("sm", [P, 4, 4])
        rs = sb("rs", [P, 4, 4])
        prm_ffn = sb("prm_ffn", [P, KC])
        top8 = sb("top8", [P, 8])
        rt = sb("rt", [P, 292])
        gsel = sb("gsel", [1, 1], I32)

        ident = cst[:, C_ID:C_ID + P]
        tri = cst[:, C_TRI:C_TRI + P]
        tris = cst[:, C_TRIS:C_TRIS + P]
        ones = cst[:, C_ONE:C_ONE + P]
        iota = cst[:, C_IOTA:C_IOTA + P]
        caus = cst[:, C_CAUS:C_CAUS + P]

        def cols(buf, a, *shape):
            v = buf[:, a:a + math.prod(shape)]
            names = "abc"[:len(shape)]
            if len(shape) == 1:
                return v
            return v.rearrange(f"p ({' '.join(names)}) -> p {' '.join(names)}",
                               **{n: s for n, s in zip(names, shape)})

        xbcT = cols(big, 0, CC, SEQ)
        zt = cols(big, 0, TT, DI)
        yT = cols(big, 0, 2 * KC, SEQ)
        memx = cols(big, 0, TT, D)
        memT = cols(big, 2048, KC, SEQ)
        xg = cols(big, 0, KC, P)
        yg = cols(big, 1024, D)
        hid = cols(big, 2048, 2, F)
        hidT = cols(big, 2560, 2, F)
        sil = cols(big, 3072, 2, F)
        sel = cols(big, 3584, TT, P)
        selT = cols(big, 3840, TT * P)
        cmb = cols(big, 4096, E)
        ropeA = cols(scr, 0, NCOL)
        ropeB = cols(scr, 512, NCOL)
        conv = cols(scr, 1024, 2, 2, SEQ)
        rel = cols(scr, 2048, 2, NCOL)
        isc = cols(scr, 3072, SEQ)
        ex32 = cols(scr, 3328, TT * SH)
        mm_ = cols(scr, 0, 2, HG * P)
        state = cols(scr, 2048, SG, NCOL)
        ckT = cols(scr, 0, KC, SEQ)
        cv = cols(scr, 2048, TT, D)
        xdt = cols(att, 0, 2, NCOL)
        xdtt = cols(att, 1024, NCOL)
        ytmp = cols(att, 1536, NCOL)
        sco = cols(att, 0, 2, NCOL)
        pT = cols(att, 1024, 2, NCOL)
        cbm = cols(qiT[:, :, :].rearrange("p a b -> p (a b)"), 0, TT, SG * P)
        dring = cols(xs[:, :, :].rearrange("p a b -> p (a b)"), 0, D_SLOTS, 2 * D)

        bank = [ctx.enter_context(nc.psum_tensor(f"bank{b}", [P, NCOL], F32)) for b in range(8)]

        cst_in = sem("cst_in")
        prm_in = sem("prm_in")
        prm_used = sem("prm_used")
        w_in_sem = [sem(f"chunk_in{s}") for s in range(W_SLOTS)]
        d_in_sem = [sem(f"down_in{s}") for s in range(D_SLOTS)]
        mem_in = sem("mem_in")
        fin_in = sem("fin_in")
        filled_s = sem("bank_filled")
        drained_s = {"dve": sem("drained_by_dve"), "act": sem("drained_by_act")}
        v_step = sem("dve_step")
        a_step = sem("act_step")
        p_step = sem("pool_step")
        norm_rdy = sem("xn_ready")
        ka_rdy = sem("keys_roped")
        dup_rdy = sem("keys_doubled")
        conv0_rdy = sem("conv_started")
        conv_rdy = sem("conv_summed")
        silu_rdy = sem("conv_silu")
        dt_abs = sem("dt_abs")
        dt_log = sem("dt_log")
        dt_rdy = sem("dt_ready")
        ac_rdy = sem("acum_ready")
        eac_rdy = sem("exp_acum_ready")
        rel_used = sem("rel_used")
        x_scaled = sem("x_scaled")
        seg_rdy = sem("segments_ready")
        dec_rdy = sem("decay_ready")
        m_rdy = sem("decayed_scores_ready")
        y_rdy = sem("y_gated")
        yn_rdy = sem("y_normed")
        sc_rdy = sem("score_max_ready")
        pr_rdy = sem("probs_ready")
        mem_rdy = sem("mem_normed")
        var_rdy = sem("mean_square_ready")
        rstd_rdy = sem("rstd_ready")
        ssq_rdy = sem("y_squares_ready")
        rt_in = sem("group_logits_ready")
        rt_exp = sem("group_exp_ready")
        r2_in = sem("top2_diff_ready")
        r2_exp = sem("top2_exp_ready")
        oh_rdy = sem("onehot_ready")
        keys_rdy = sem("slots_ready")
        sel_rdy = sem("selection_ready")
        gat_s = sem("gathered")
        xg_rdy = sem("gathered_x_ready")
        gu_s = sem("gate_up_filled")
        sil_s = sem("silu_done")
        hid_s = sem("hidden_ready")
        hT_s = sem("hidden_transposed")
        hTc_s = sem("hidden_copied")
        dn_s = sem("down_done")
        yg_s = sem("expert_sum_ready")
        sct_s = sem("scattered")
        add_s = sem("h_added")
        fin_s = sem("final_ready")
        out_s = sem("stored")

        def filled(eng, l, job):
            eng.wait_ge(filled_s, l * NJ + job + 1)

        def drained(eng, l, job):
            eng.wait_ge(drained_s[OWNER[job]], l * DRAINS[OWNER[job]] + RANK[job])

        def settle(eng):
            eng.nop(nofuse=True)

        def drain_inc(ins, job):
            ins.then_inc(drained_s[OWNER[job]], 1)

        block = ctx.enter_context(nc.Block())

        @block.sync
        def _(sp):
            sp.nop().then_inc(gu_s, W_SLOTS)
            sp.nop().then_inc(dn_s, D_SLOTS)

            def rows(w, a, b):
                return w.rearrange("(c p) n -> p c n", p=P)[:, :, a:b]

            def chunk(l, c):
                st, part = CHUNKS[c]
                kind = st[0]
                if c < W_SLOTS:
                    sp.wait_ge(gu_s, l * NT * E + c + 1)
                else:
                    filled(sp, l, last_job(c - W_SLOTS))
                settle(sp)
                slot = wring[:, c % W_SLOTS, :, :]

                def load(dst, src):
                    sp.dma_start(dst, src).then_inc(w_in_sem[c % W_SLOTS], 16)

                def halves(src):
                    load(slot[:, 0:KC // 2, :], src[:, 0:KC // 2, :])
                    load(slot[:, KC // 2:KC, :], src[:, KC // 2:KC, :])

                if kind == "small":
                    load(slot[:, :, 0:SH], rows(w_in[l], DT0, DT0 + SH))
                    load(slot[:, :, SH:SH + HD + IH], rows(w_in[l], KI0, GS0))
                elif kind == "kv":
                    load(slot[:, 0:4, 0:256], rows(w_in[l], K0, QI0)[:, 0:4, :])
                    load(slot[:, 4:8, 0:256], rows(w_in[l], K0, QI0)[:, 4:8, :])
                elif kind == "router":
                    load(slot[:, :, 0:G], rows(w_group[l], 0, G))
                    load(slot[:, :, G:G + G * E], rows(w_router[l], 0, G * E))
                elif kind == "ssdo":
                    n = st[1] * NCOL
                    halves(rows(w_ssd_o[l][part * D:(part + 1) * D, :], n, n + NCOL))
                else:
                    w, a = {
                        "qi": (w_in, QI0), "xbc": (w_in, XBC0), "q": (w_in, Q0), "z": (w_in, Z0),
                        "gate": (w_in, GS0 if st[1:2] == (0,) else GA0), "atto": (w_attn_o, 0),
                        "wo": (w_out, 0), "ck": (w_ckv, 0), "cv": (w_ckv, D), "cq": (w_cq, 0), "co": (w_co, 0),
                    }[kind]
                    a += NCOL * (st[-1] if len(st) > 1 else 0)
                    halves(rows(w[l], a, a + NCOL))

            def experts(l, t, g):
                for e in range(E):
                    k = NCH + e
                    s = k % W_SLOTS
                    if e < W_SLOTS:
                        filled(sp, l, last_job(NCH - W_SLOTS + e))
                        settle(sp)
                    sp.wait_ge(gu_s, (l * NT + t) * E + e + 1)
                    settle(sp)
                    sp.dma_start(wring[:, s, :, 0:F], rows(w_gate[l, g, e], 0, F)).then_inc(w_in_sem[s], 16)
                    sp.dma_start(wring[:, s, :, F:2 * F], rows(w_up[l, g, e], 0, F)).then_inc(w_in_sem[s], 16)
                    sp.wait_ge(dn_s, (l * NT + t) * E + e + 1)
                    settle(sp)
                    sp.dma_start(dring[:, e % D_SLOTS, :].rearrange("p (c n) -> p c n", n=D),
                                 rows(w_down[l, g, e], 0, D)).then_inc(d_in_sem[e % D_SLOTS], 16)

            with sp.Fori(0, DEPTH) as l:
                for c in range(NCH):
                    chunk(l, c)
                with sp.Fori(0, G) as g:
                    experts(l, g, g)
                sp.wait_ge(keys_rdy, l + 1)
                settle(sp)
                over = nc.values_load(gsel[0:1, 0:1], engines=[mybir.EngineType.SP], min_val=0, max_val=G - 1)
                experts(l, G, over)
            sp.wait_ge(fin_s, TT)
            sp.dma_start(out.rearrange("(t p) d -> p t d", p=P), xn[:, :, :]).then_inc(out_s, 16)
            sp.wait_ge(out_s, 16)

        @block.gpsimd
        def _(pool):
            pool.dma_start(cst[:, :], consts).then_inc(cst_in, 16)
            pool.dma_start(h[:, :, :], x.rearrange("(t p) d -> p t d", p=P)).then_inc(cst_in, 16)
            pool.nop().then_inc(prm_used, 1)
            def power(at, r):
                pool.wait_ge(var_rdy, at)
                nc.gpsimd.tensor_tensor(r, r, cst[:, C_MH:C_MH + r.shape[1]], ALU.pow).then_inc(rstd_rdy, 1)

            pool.wait_ge(cst_in, 32)
            with pool.Fori(0, DEPTH) as l:
                pool.wait_ge(prm_used, l + 1)
                settle(pool)
                pool.dma_start(prm[:, :], params[l]).then_inc(prm_in, 16)
                pool.wait_ge(prm_in, l * 16 + 16)
                power(l * NORMS + 1, st_[:, 18:20])
                pool.wait_ge(ka_rdy, l + 1)
                settle(pool)
                nc.gpsimd.tensor_copy(ktok[:, :, :, 1, :], ktok[:, :, :, 0, :]).then_inc(dup_rdy, 1)
                pool.wait_ge(eac_rdy, l + 1)
                for n, (t, g) in enumerate(SSD):
                    if n == 0:
                        drained(pool, l, JOB[(("xT", 7), 0)])
                    xsg = xs[:, t, g * NCOL:(g + 1) * NCOL].rearrange("p (h d) -> p h d", d=SP_)
                    if n >= 2:
                        filled(pool, l, JOB[(("ssd", n - 2), 1)])
                    dst = xdt[:, n % 2, :].rearrange("p (h d) -> p h d", d=SP_)
                    nc.gpsimd.tensor_tensor(dst, xsg, bc(dtb[:, t, g * HG:(g + 1) * HG], 2, SP_),
                                            ALU.mult).then_inc(p_step, 1)
                    pool.wait_ge(p_step, l * len(SSD) + (n + 1))
                    if t == 0:
                        if n >= 1:
                            filled(pool, l, JOB[(("ssd", n - 1), 1)])
                        nc.gpsimd.tensor_tensor(xdtt[:, :].rearrange("p (h d) -> p h d", d=SP_), dst,
                                                bc(tail[:, g * HG:(g + 1) * HG], 2, SP_), ALU.mult)
                    nc.gpsimd.tensor_tensor(xsg, xsg, bc(prm[:, P_DS + g * HG:P_DS + (g + 1) * HG], 2, SP_),
                                            ALU.mult).then_inc(x_scaled, 1)
                power(l * NORMS + 2, st_[:, 8:16])
                filled(pool, l, JOB[(("ssdo", 1), 1)])
                settle(pool)
                pool.dma_start(memx, mem.rearrange("(t p) d -> p t d", p=P)).then_inc(mem_in, 16)
                for k in (3, 4, 5):
                    power(l * NORMS + k, st_[:, 18:20])
            power(DEPTH * NORMS + 1, st_[:, 18:20])
            pool.wait_ge(yg_s, DEPTH * NT * 2)
            pool.dma_start(gate[:, 0, :], gain_final).then_inc(fin_in, 16)
            pool.wait_ge(fin_in, 16)

        @block.tensor
        def _(pe):
            def transposes(l, job, blocks):
                free(l, job)
                b = bank[job % 8]
                for i, src in enumerate(blocks):
                    ins = nc.tensor.transpose(b[:, i * P:(i + 1) * P], src, ident)
                ins.then_inc(filled_s, 1)

            def free(l, job):
                if job >= 8:
                    drained(pe, l, job - 8)

            def chunk_in(l, c):
                pe.wait_ge(w_in_sem[c % W_SLOTS], (l * (PER_LAYER // W_SLOTS) + (c // W_SLOTS + 1)) * 32)

            def by_token(l, st, src, width=NCOL):
                c = CHUNK[(st, 0)]
                chunk_in(l, c)
                for t in range(TT):
                    job = JOB[(st, t)]
                    free(l, job)
                    for i in range(KC):
                        k = (FIRST_BLOCK + i) % KC
                        ins = nc.tensor.matmul(bank[job % 8][:, 0:width], src[:, k, t * P:(t + 1) * P],
                                               wring[:, c % W_SLOTS, k, 0:width], start=i == 0, stop=i == KC - 1)
                    ins.then_inc(filled_s, 1)

            def by_channel(l, st, src):
                c = CHUNK[(st, 0)]
                chunk_in(l, c)
                for j in range(2):
                    job = JOB[(st, j)]
                    free(l, job)
                    for i in range(2):
                        m = (2 * j + i) * P
                        for k in range(KC):
                            ins = nc.tensor.matmul(bank[job % 8][:, i * SEQ:(i + 1) * SEQ],
                                                   wring[:, c % W_SLOTS, k, m:m + P], src[:, k, :],
                                                   start=k == 0, stop=k == KC - 1)
                    ins.then_inc(filled_s, 1)

            def pairs(src, i):
                return [src[:, t, (2 * i + j) * P:(2 * i + j + 1) * P] for j in range(2) for t in range(TT)]

            def stage(l, st):
                kind = st[0]
                if kind == "hT":
                    pe.wait_ge(norm_rdy, l * 3 + st[1] + 1)
                    transposes(l, JOB[(st, 0)], pairs(xn, st[2]))
                elif kind in ("small", "kv", "qi", "q", "z", "gate"):
                    if kind == "small":
                        drained(pe, l, JOB[(("hT", 0, 3), 0)])
                    by_token(l, st, hT, {"small": SH + HD + IH, "kv": 2 * AKV * HD}.get(kind, NCOL))
                elif kind == "xbc":
                    by_channel(l, st, hT)
                elif kind == "acum":
                    pe.wait_ge(dt_rdy, l + 1)
                    job = JOB[(st, 0)]
                    free(l, job)
                    b = bank[job % 8]
                    for t in range(TT):
                        nc.tensor.matmul(b[:, t * SH:(t + 1) * SH], tri, dta[:, t, :], start=True, stop=True)
                    nc.tensor.matmul(b[:, 2 * SH:3 * SH], ones, dta[:, 0, :],
                                     start=True, stop=True).then_inc(filled_s, 1)
                elif kind == "kT":
                    pe.wait_ge(dup_rdy, l + 1)
                    job = JOB[(st, 0)]
                    free(l, job)
                    b = bank[job % 8]
                    for i in range(2):
                        for t in range(TT):
                            src = ktok[:, t, i, :, :].rearrange("p a d -> p (a d)")
                            ins = nc.tensor.transpose(b[:, (2 * i + t) * P:(2 * i + t + 1) * P], src, ident)
                    ins.then_inc(filled_s, 1)
                elif kind == "kiT":
                    job = JOB[(st, 0)]
                    free(l, job)
                    b = bank[job % 8]
                    for t in range(TT):
                        src = ktok[:, t, 2, :, :].rearrange("p a d -> p (a d)")
                        ins = nc.tensor.transpose(b[:, t * P:(t + 1) * P], src, ident)
                    ins.then_inc(filled_s, 1)
                elif kind == "qiT":
                    if st[1] == 0:
                        drained(pe, l, JOB[(("qi",), 1)])
                    transposes(l, JOB[(st, 0)], pairs(qbuf, st[1]))
                elif kind == "idx":
                    _, t, r, i = st
                    drained(pe, l, JOB[(("kiT",), 0)])
                    drained(pe, l, JOB[(("qiT", 1), 0)])
                    job = JOB[(st, 0)]
                    free(l, job)
                    nk = (t + 1) * P
                    for j in range(NCOL // nk):
                        pair = i * (NCOL // nk) + j
                        ins = nc.tensor.matmul(bank[job % 8][:, j * nk:(j + 1) * nk],
                                               qiT[r * HD:(r + 1) * HD, pair, t * P:(t + 1) * P],
                                               kT[r * HD:(r + 1) * HD, 2, 0:nk], start=True, stop=True)
                    ins.then_inc(filled_s, 1)
                elif kind == "xT":
                    t, q = divmod(st[1], 4)
                    pe.wait_ge(silu_rdy, l * 12 + (2 * q + 2))
                    transposes(l, JOB[(st, 0)], [xbcT[:, 4 * q + i, t * P:(t + 1) * P] for i in range(4)])
                elif kind == "bT":
                    pe.wait_ge(silu_rdy, l * 12 + 12)
                    transposes(l, JOB[(st, 0)], [xbcT[:, 2 * KC + g, 0:P] for g in range(SG)])
                elif kind == "cb":
                    job = JOB[(st, 0)]
                    free(l, job)
                    ts = slice(st[1] * P, (st[1] + 1) * P)
                    for g in range(SG):
                        ins = nc.tensor.matmul(bank[job % 8][:, g * P:(g + 1) * P], xbcT[:, 2 * KC + g, ts],
                                               xbcT[:, 2 * KC + SG + g, ts], start=True, stop=True)
                    ins.then_inc(filled_s, 1)
                elif kind == "qT":
                    drained(pe, l, JOB[(("q", 1), 1)])
                    transposes(l, JOB[(st, 0)], pairs(qbuf, st[1]))
                elif kind == "decay":
                    t, g = SSD[st[1]]
                    for j in range(2):
                        job = JOB[(st, j)]
                        free(l, job)
                        for i in range(4):
                            hd = g * HG + 4 * j + i
                            ins = nc.tensor.matmul(bank[job % 8][:, i * P:(i + 1) * P],
                                                   dta[:, t, hd:hd + 1].to_broadcast([P, P]), tri,
                                                   start=True, stop=True)
                        ins.then_inc(filled_s, 1)
                elif kind == "ssd":
                    n = st[1]
                    t, g = SSD[n]
                    pe.wait_ge(x_scaled, l * len(SSD) + (n + 1))
                    pe.wait_ge(m_rdy, l * len(SSD) + (n + 1))
                    job = JOB[(st, 0)]
                    free(l, job)
                    for i in range(HG):
                        ins = nc.tensor.matmul(bank[job % 8][:, i * SP_:(i + 1) * SP_],
                                               mm_[:, n % 2, i * P:(i + 1) * P],
                                               xdt[:, n % 2, i * SP_:(i + 1) * SP_], start=True, stop=True)
                    ins.then_inc(filled_s, 1)
                    job = JOB[(st, 1)]
                    free(l, job)
                    if t == 0:
                        drained(pe, l, JOB[(("bT",), 0)])
                        ins = nc.tensor.matmul(bank[job % 8][:, :], btok[:, g * SN:(g + 1) * SN], xdtt[:, :],
                                               start=True, stop=True)
                    else:
                        drained(pe, l, JOB[(("ssd", g), 1)])
                        ins = nc.tensor.matmul(bank[job % 8][:, :], xbcT[:, 2 * KC + SG + g, P:2 * P],
                                               state[:, g, :], start=True, stop=True)
                    ins.then_inc(filled_s, 1)
                elif kind == "score":
                    t, r, i = ATT[st[1]]
                    drained(pe, l, JOB[(("qT", 3), 0)])
                    drained(pe, l, JOB[(("kT",), 0)])
                    job = JOB[(st, 0)]
                    free(l, job)
                    nk = (t + 1) * P
                    nh = NCOL // nk
                    for j in range(nh):
                        pair = i * nh + j
                        ins = nc.tensor.matmul(bank[job % 8][:, j * nk:(j + 1) * nk],
                                               qT[r * HD:(r + 1) * HD, pair, t * P:(t + 1) * P],
                                               kT[r * HD:(r + 1) * HD, pair // 4, 0:nk], start=True, stop=True)
                    ins.then_inc(filled_s, 1)
                elif kind in ("probT", "xprobT"):
                    n = st[1] + (len(ATT) if kind == "xprobT" else 0)
                    pe.wait_ge(pr_rdy, l * (len(ATT) + 4) + (n + 1))
                    src = sco[:, st[1] % 2, :]
                    transposes(l, JOB[(st, 0)], [src[:, i * P:(i + 1) * P] for i in range(4)])
                elif kind == "pv":
                    n = st[1]
                    t, r, i = ATT[n]
                    drained(pe, l, JOB[(("probT", n), 0)])
                    job = JOB[(st, 0)]
                    free(l, job)
                    nk = t + 1
                    nh = 4 // nk
                    for j in range(nh):
                        grp = (i * nh + j) // 4
                        for s in range(nk):
                            ins = nc.tensor.matmul(bank[job % 8][:, j * HD:(j + 1) * HD],
                                                   pT[:, n % 2, (j * nk + s) * P:(j * nk + s + 1) * P],
                                                   vtok[:, s, grp * HD:(grp + 1) * HD],
                                                   start=s == 0, stop=s == nk - 1)
                    ins.then_inc(filled_s, 1)
                elif kind == "yT":
                    pe.wait_ge(yn_rdy, l + 1)
                    transposes(l, JOB[(st, 0)], pairs(xs, st[1]))
                elif kind == "ssdo":
                    drained(pe, l, JOB[(("yT", 7), 0)])
                    jobs = [JOB[(st, t)] for t in range(TT)]
                    for half in range(2):
                        c = CHUNK[(st, half)]
                        chunk_in(l, c)
                        for t in range(TT):
                            if half == 0:
                                free(l, jobs[t])
                            for k in range(KC):
                                ins = nc.tensor.matmul(bank[jobs[t] % 8][:, :],
                                                       yT[:, half * KC + k, t * P:(t + 1) * P],
                                                       wring[:, c % W_SLOTS, k, :],
                                                       start=half == 0 and k == 0, stop=half == 1 and k == KC - 1)
                            if half == 1:
                                ins.then_inc(filled_s, 1)
                elif kind == "aT":
                    drained(pe, l, JOB[(("pv", len(ATT) - 1), 0)])
                    transposes(l, JOB[(st, 0)], pairs(qbuf, st[1]))
                elif kind == "atto":
                    drained(pe, l, JOB[(("aT", 3), 0)])
                    by_token(l, st, qT)
                elif kind == "mgT":
                    drained(pe, l, JOB[(("atto", 1), 1)])
                    transposes(l, JOB[(st, 0)], pairs(xn, st[1]))
                elif kind == "wo":
                    drained(pe, l, JOB[(("mgT", 3), 0)])
                    by_token(l, st, hT)
                elif kind == "memT":
                    pe.wait_ge(mem_rdy, l + 1)
                    transposes(l, JOB[(st, 0)], pairs(memx, st[1]))
                elif kind == "ck":
                    drained(pe, l, JOB[(("memT", 3), 0)])
                    by_channel(l, st, memT)
                elif kind == "cv":
                    by_token(l, st, memT)
                elif kind == "cq":
                    drained(pe, l, JOB[(("hT", 1, 3), 0)])
                    by_channel(l, st, hT)
                elif kind == "xscore":
                    t, pr = divmod(st[1], 2)
                    drained(pe, l, JOB[(("cq", 1), 1)])
                    job = JOB[(st, 0)]
                    free(l, job)
                    for j in range(2):
                        for k in range(2):
                            blk = 2 * (2 * pr + j) + k
                            ins = nc.tensor.matmul(bank[job % 8][:, j * SEQ:(j + 1) * SEQ],
                                                   qT[:, blk, t * P:(t + 1) * P], ckT[:, blk, :],
                                                   start=k == 0, stop=k == 1)
                    ins.then_inc(filled_s, 1)
                elif kind == "xpv":
                    n = st[1]
                    t, pr = divmod(n, 2)
                    drained(pe, l, JOB[(("xprobT", n), 0)])
                    job = JOB[(st, 0)]
                    free(l, job)
                    for j in range(2):
                        hd = 2 * pr + j
                        for s in range(2):
                            ins = nc.tensor.matmul(bank[job % 8][:, j * XD:(j + 1) * XD],
                                                   pT[:, n % 2, (2 * j + s) * P:(2 * j + s + 1) * P],
                                                   cv[:, s, hd * XD:(hd + 1) * XD], start=s == 0, stop=s == 1)
                    ins.then_inc(filled_s, 1)
                elif kind == "xoT":
                    drained(pe, l, JOB[(("xpv", 3), 0)])
                    transposes(l, JOB[(st, 0)], pairs(qbuf, st[1]))
                elif kind == "co":
                    drained(pe, l, JOB[(("xoT", 3), 0)])
                    by_token(l, st, qT)
                elif kind == "router":
                    drained(pe, l, JOB[(("hT", 2, 3), 0)])
                    c = CHUNK[(st, 0)]
                    chunk_in(l, c)
                    job = JOB[(st, 0)]
                    free(l, job)
                    for t in range(TT):
                        for k in range(KC):
                            ins = nc.tensor.matmul(bank[job % 8][:, t * 64:t * 64 + G + G * E],
                                                   hT[:, k, t * P:(t + 1) * P],
                                                   wring[:, c % W_SLOTS, k, 0:G + G * E],
                                                   start=k == 0, stop=k == KC - 1)
                    ins.then_inc(filled_s, 1)
                elif kind == "rank":
                    pe.wait_ge(oh_rdy, l + 1)
                    job = JOB[(st, 0)]
                    free(l, job)
                    b = bank[job % 8]
                    oh = cols(rt, R_OH, TT, G)
                    nc.tensor.matmul(b[:, 0:G], tris, oh[:, 0, :], start=True, stop=True)
                    nc.tensor.matmul(b[:, 8:8 + G], tris, oh[:, 1, :], start=True, stop=False)
                    nc.tensor.matmul(b[:, 8:8 + G], ones, oh[:, 0, :], start=False, stop=True)
                    nc.tensor.matmul(b[:, 16:16 + G], ones, oh[:, 0, :], start=True, stop=False)
                    nc.tensor.matmul(b[:, 16:16 + G], ones, oh[:, 1, :], start=False,
                                     stop=True).then_inc(filled_s, 1)

            def expert_tile(l, t):
                u = l * NT + t
                pe.wait_ge(sel_rdy, u + 1)
                for c in range(KC):
                    for k in range(TT):
                        ins = nc.tensor.matmul(bank[6 + c // 4][:, (c % 4) * P:(c % 4 + 1) * P],
                                               xn[:, k, c * P:(c + 1) * P], sel[:, k, :], start=k == 0, stop=k == TT - 1)
                    if c % 4 == 3:
                        ins.then_inc(gat_s, 1)
                for k in range(TT):
                    nc.tensor.transpose(bank[2][:, k * P:(k + 1) * P], sel[:, k, :], ident)
                within = cols(rt, R_WI, TT, E)
                for k in range(TT):
                    ins = nc.tensor.matmul(bank[3][:, 0:E], sel[:, k, :], within[:, k, :],
                                           start=k == 0, stop=k == TT - 1)
                ins.then_inc(gat_s, 1)
                pe.wait_ge(xg_rdy, u + 1)

                def gate_up(e):
                    c = NCH + e
                    pe.wait_ge(w_in_sem[c % W_SLOTS],
                               (l * (PER_LAYER // W_SLOTS) + t * (E // W_SLOTS) + (c // W_SLOTS + 1)) * 32)
                    if e >= 2:
                        pe.wait_ge(hid_s, u * E + (e - 1))
                    for k in range(KC):
                        ins = nc.tensor.matmul(bank[e % 2][:, :], xg[:, k, :], wring[:, c % W_SLOTS, k, :],
                                               start=k == 0, stop=k == KC - 1)
                    ins.then_inc(gu_s, 1)

                gate_up(0)
                for e in range(E):
                    if e + 1 < E:
                        gate_up(e + 1)
                    pe.wait_ge(hid_s, u * E + (e + 1))
                    if e >= 2:
                        pe.wait_ge(hTc_s, u * E + (e - 1))
                    for k in range(2):
                        ins = nc.tensor.transpose(bank[2 + e % 2][:, k * P:(k + 1) * P],
                                                  hid[:, e % 2, k * P:(k + 1) * P], ident)
                    ins.then_inc(hT_s, 1)
                    pe.wait_ge(hTc_s, u * E + (e + 1))
                    pe.wait_ge(d_in_sem[e % D_SLOTS], (u * (E // D_SLOTS) + (e // D_SLOTS + 1)) * 16)
                    for n in range(2):
                        for k in range(2):
                            ins = nc.tensor.matmul(bank[4 + n][:, :], hidT[:, e % 2, k * P:(k + 1) * P],
                                                   dring[:, e % D_SLOTS, k * D + n * NCOL:k * D + (n + 1) * NCOL],
                                                   start=e == 0 and k == 0, stop=e == E - 1 and k == 1)
                    ins.then_inc(dn_s, 1)
                pe.wait_ge(yg_s, u * 2 + 2)
                for k in range(TT):
                    for n in range(2):
                        if k:
                            pe.wait_ge(add_s, u * 4 + (n + 1))
                        nc.tensor.matmul(bank[6 + n][:, :], selT[:, k * P:(k + 1) * P],
                                         yg[:, n * NCOL:(n + 1) * NCOL], start=True, stop=True).then_inc(sct_s, 1)

            pe.wait_ge(cst_in, 32)
            with pe.Fori(0, DEPTH) as l:
                for st in ORDER:
                    stage(l, st)
                drained(pe, l, max(k for k in range(NJ) if OWNER[k] == "dve"))
                drained(pe, l, max(k for k in range(NJ) if OWNER[k] == "act"))
                settle(pe)
                with pe.Fori(0, G) as t:
                    expert_tile(l, t)
                expert_tile(l, G)

        @block.scalar
        def _(act):
            steps = Steps(act, a_step)

            def stage(l, st):
                kind = st[0]
                job = JOB.get((st, 0))
                if kind == "xbc":
                    for j in range(2):
                        m = 2 * st[1] + j
                        filled(act, l, JOB[(st, j)])
                        if m >= 2:
                            act.wait_ge(silu_rdy, l * 12 + (m - 1))
                        for i in range(2):
                            ch = 2 * m + i
                            ins = nc.scalar.activation(conv[:, m % 2, i, :], bank[JOB[(st, j)] % 8][:, i * SEQ:(i + 1) * SEQ],
                                                       ACT.Identity, bias=prm[:, P_CB + ch:P_CB + ch + 1],
                                                       scale=prm[:, P_CW + 3 * CC + ch:P_CW + 3 * CC + ch + 1])
                        ins.then_inc(conv0_rdy, 1)
                    for j in range(2):
                        m = 2 * st[1] + j
                        act.wait_ge(conv_rdy, l * 12 + (m + 1))
                        nc.scalar.activation(xbcT[:, 2 * m:2 * m + 2, :], conv[:, m % 2, :, :],
                                             ACT.Silu).then_inc(silu_rdy, 1)
                elif kind == "acum":
                    act.wait_ge(dt_abs, l + 1)
                    steps.link(nc.scalar.activation(ex32, tmp32[:, 0, :], ACT.Exp, scale=-1.0))
                    steps.link(nc.scalar.activation(tmp32[:, 0, :], ex32, ACT.Ln, bias=1.0))
                    nc.scalar.activation(eac[:, :], prm[:, P_AL:P_AL + SH], ACT.Exp).then_inc(dt_log, 1)
                    act.wait_ge(ac_rdy, l + 1)
                    nc.scalar.activation(eac[:, :], acum[:, 1, :], ACT.Exp)
                    nc.scalar.activation(tail[:, :], tail[:, :], ACT.Exp).then_inc(eac_rdy, 1)
                elif kind in ("qiT", "xT", "qT", "aT", "mgT", "xoT", "bT"):
                    filled(act, l, job)
                    b = bank[job % 8][:, :]
                    if kind == "bT":
                        dst = btok[:, :]
                    elif kind == "xT":
                        t, q = divmod(st[1], 4)
                        dst = xs[:, t, q * NCOL:(q + 1) * NCOL]
                    else:
                        if kind == "mgT" and st[1] == 0:
                            filled(act, l, JOB[(("gate", 1, 1), 1)])
                        to = {"qiT": qiT, "qT": qT, "aT": qT, "mgT": hT, "xoT": qT}[kind]
                        dst = to[:, 2 * st[1]:2 * st[1] + 2, :].rearrange("p c t -> p (c t)")
                    drain_inc(nc.scalar.activation(dst, b, ACT.Copy), job)
                elif kind == "idx":
                    filled(act, l, job)
                    n = IDX.index(st)
                    if n >= 2:
                        act.wait_ge(rel_used, l * len(IDX) + (n - 1))
                    drain_inc(nc.scalar.activation(rel[:, n % 2, :], bank[job % 8][:, :], ACT.Relu), job)
                elif kind in ("z", "gate", "cv"):
                    for t in range(TT):
                        job = JOB[(st, t)]
                        filled(act, l, job)
                        n = st[-1] * NCOL
                        if kind == "gate" and st[1] == 1:
                            drained(act, l, JOB[(("ssdo", 1), 1)])
                        dst = {"z": zt, "gate": gate, "cv": cv}[kind][:, t, n:n + NCOL]
                        func = {"z": ACT.Silu, "gate": ACT.Sigmoid, "cv": ACT.Copy}[kind]
                        drain_inc(nc.scalar.activation(dst, bank[job % 8][:, :], func), job)
                elif kind in ("ck", "cq"):
                    to = {"ck": ckT, "cq": qT}[kind]
                    for j in range(2):
                        job = JOB[(st, j)]
                        filled(act, l, job)
                        blk = 4 * st[1] + 2 * j
                        drain_inc(nc.scalar.activation(to[:, blk:blk + 2, :].rearrange("p c t -> p (c t)"),
                                                       bank[job % 8][:, :], ACT.Copy), job)
                elif kind == "decay":
                    n = st[1]
                    act.wait_ge(seg_rdy, l * len(SSD) + (n + 1))
                    nc.scalar.activation(mm_[:, n % 2, :], mm_[:, n % 2, :], ACT.Exp).then_inc(dec_rdy, 1)
                elif kind == "ssd":
                    t, g = SSD[st[1]]
                    if t == 0:
                        job = JOB[(st, 1)]
                        filled(act, l, job)
                        drain_inc(nc.scalar.activation(state[:, g, :], bank[job % 8][:, :], ACT.Copy), job)
                elif kind == "ynorm":
                    for t in range(TT):
                        for g in range(SG):
                            act.wait_ge(y_rdy, l * len(SSD) + (t * SG + g + 1))
                            ins = nc.scalar.activation(zt[:, t, g * NCOL:(g + 1) * NCOL], xs[:, t, g * NCOL:(g + 1) * NCOL],
                                                       ACT.Square, accum_out=st_[:, t * SG + g:t * SG + g + 1])
                    ins.then_inc(ssq_rdy, 1)
                elif kind == "score":
                    n = st[1]
                    t, r, i = ATT[n]
                    nk = (t + 1) * P
                    act.wait_ge(sc_rdy, l * (len(ATT) + 4) + (n + 1))
                    for j in range(NCOL // nk):
                        ins = nc.scalar.activation(sco[:, n % 2, j * nk:(j + 1) * nk], sco[:, n % 2, j * nk:(j + 1) * nk],
                                                   ACT.Exp, bias=nmx[:, n % 4, j:j + 1], scale=HD ** -0.5,
                                                   accum_out=sm[:, n % 4, j:j + 1])
                    ins.then_inc(pr_rdy, 1)
                elif kind == "xscore":
                    n = st[1]
                    act.wait_ge(sc_rdy, l * (len(ATT) + 4) + (len(ATT) + n + 1))
                    if n >= 2:
                        filled(act, l, JOB[(("xprobT", n - 2), 0)])
                    for j in range(2):
                        ins = nc.scalar.activation(sco[:, n % 2, j * SEQ:(j + 1) * SEQ], bank[job % 8][:, j * SEQ:(j + 1) * SEQ],
                                                   ACT.Exp, bias=nmx[:, n % 4, j:j + 1], scale=XD ** -0.5,
                                                   accum_out=sm[:, n % 4, j:j + 1])
                    ins.then_inc(pr_rdy, 1)
                    act.wait_ge(pr_rdy, l * (len(ATT) + 4) + (len(ATT) + n + 1))
                    drain_inc(act.nop(), job)
                elif kind in ("probT", "xprobT"):
                    filled(act, l, job)
                    n = st[1]
                    if n >= 2:
                        filled(act, l, JOB[("pv" if kind == "probT" else "xpv", n - 2), 0])
                    drain_inc(nc.scalar.activation(pT[:, n % 2, :], bank[job % 8][:, :], ACT.Copy), job)
                elif kind == "router":
                    act.wait_ge(rt_in, l + 1)
                    gd = cols(rt, R_GD, TT * G)
                    nc.scalar.activation(cols(rt, R_GE, TT * G), gd, ACT.Exp).then_inc(rt_exp, 1)
                    act.wait_ge(r2_in, l + 1)
                    nc.scalar.activation(cols(rt, R_TW, TT), cols(rt, R_DL, TT), ACT.Exp).then_inc(r2_exp, 1)

            def expert_tile(l, t):
                u = l * NT + t

                def silu(e):
                    act.wait_ge(gu_s, u * E + (W_SLOTS + e + 1))
                    if e >= 2:
                        act.wait_ge(hid_s, u * E + (e - 1))
                    nc.scalar.activation(sil[:, e % 2, :], bank[e % 2][:, 0:F], ACT.Silu).then_inc(sil_s, 1)

                silu(0)
                for e in range(E):
                    if e + 1 < E:
                        silu(e + 1)
                    act.wait_ge(hT_s, u * E + (e + 1))
                    if e >= 2:
                        act.wait_ge(dn_s, u * E + (D_SLOTS + e - 1))
                    nc.scalar.activation(hidT[:, e % 2, :], bank[2 + e % 2][:, 0:F], ACT.Copy).then_inc(hTc_s, 1)
                act.wait_ge(dn_s, u * E + (D_SLOTS + E))
                for n in range(2):
                    nc.scalar.activation(yg[:, n * NCOL:(n + 1) * NCOL], bank[4 + n][:, :],
                                         ACT.Copy).then_inc(yg_s, 1)

            with act.Fori(0, DEPTH) as l:
                act.wait_ge(prm_in, l * 16 + 16)
                steps.at(l * A_LAYER)
                for st in ORDER:
                    stage(l, st)
                assert steps.n == A_LAYER, f"A_LAYER = {steps.n}"
                with act.Fori(0, G) as t:
                    expert_tile(l, t)
                expert_tile(l, G)

        @block.vector
        def _(dve):
            steps = Steps(dve, v_step)
            link = steps.link
            V = nc.vector

            def rms(at, ss, r, n):
                V.tensor_scalar(r, ss, 1.0 / n, EPS, ALU.mult, ALU.add).then_inc(var_rdy, 1)
                dve.wait_ge(rstd_rdy, at)

            def normalise(at, src, dst, squares):
                for t in range(TT):
                    ins = V.scalar_tensor_tensor(squares[:, t, :], src[:, t, :], 1.0, src[:, t, :], ALU.mult, ALU.mult,
                                                 accum_out=st_[:, 16 + t:17 + t])
                link(ins)
                rms(at, st_[:, 16:18], st_[:, 18:20], D)
                for t in range(TT):
                    ins = V.tensor_scalar(dst[:, t, :], src[:, t, :], st_[:, 18 + t:19 + t], None, ALU.mult)
                return ins

            def rope(src, nh, t, dst):
                a = ropeA[:, 0:nh * HD].rearrange("p (h d) -> p h d", d=HD)
                b = ropeB[:, 0:nh * HD].rearrange("p (h d) -> p h d", d=HD)
                s = src.rearrange("p (h d) -> p h d", d=HD)
                cos = bc(cst[:, C_COS + t * HD:C_COS + (t + 1) * HD], 1, nh)
                sin = bc(cst[:, C_SIN + t * HD:C_SIN + (t + 1) * HD], 1, nh)
                V.tensor_tensor(a, s, cos, ALU.mult)
                link(V.tensor_tensor(b, s, sin, ALU.mult))
                hf = HD // 2
                V.tensor_tensor(dst[:, :, 0:hf], a[:, :, 0:hf], b[:, :, hf:HD], ALU.subtract)
                return V.tensor_tensor(dst[:, :, hf:HD], a[:, :, hf:HD], b[:, :, 0:hf], ALU.add)

            def first_max(src, prio, m, eq, oh, n):
                link(V.tensor_reduce(m, src, AX_X, ALU.max))
                link(V.tensor_tensor(eq, src, bc(m, 2, n), ALU.is_equal))
                link(V.tensor_tensor(eq, eq, bc(prio, 1, TT), ALU.mult))
                link(V.tensor_reduce(cols(rt, R_T2, TT), eq, AX_X, ALU.max))
                link(V.tensor_tensor(oh, eq, bc(cols(rt, R_T2, TT), 2, n), ALU.is_equal))

            def stage(l, st):
                kind = st[0]
                job = JOB.get((st, 0))
                b = bank[job % 8][:, :] if job is not None else None
                if kind == "norm":
                    if st[1] == 1:
                        drained(dve, l, JOB[(("wo", 1), 1)])
                    elif st[1] == 2:
                        drained(dve, l, JOB[(("co", 1), 1)])
                    normalise(l * NORMS + (1, 4, 5)[st[1]], h, xn, xn).then_inc(norm_rdy, 1)
                elif kind in ("hT", "memT", "yT"):
                    filled(dve, l, job)
                    i = st[-1]
                    to, gain = {"hT": (hT, (P_NM, P_NX, P_NF)[st[1] if kind == "hT" else 0]),
                                "memT": (memT, P_NE), "yT": (yT, P_SN)}[kind]
                    for j in range(2):
                        ins = V.tensor_scalar(to[:, 2 * i + j, :], b[:, j * SEQ:(j + 1) * SEQ],
                                              prm[:, gain + 2 * i + j:gain + 2 * i + j + 1], None, ALU.mult)
                    drain_inc(ins, job)
                elif kind == "small":
                    for t in range(TT):
                        job = JOB[(st, t)]
                        b = bank[job % 8]
                        filled(dve, l, job)
                        V.tensor_tensor(dtb[:, t, :], b[:, 0:SH], prm[:, P_DTB:P_DTB + SH], ALU.add)
                        V.tensor_scalar(wis[:, t, :], b[:, SH + HD:SH + HD + IH], IDX_SCALE, None, ALU.mult)
                        link(rope(b[:, SH:SH + HD], 1, t, ktok[:, t, 2:3, 0, :]))
                        drain_inc(dve.nop(), job)
                    dts = dtb[:, :, :].rearrange("p t h -> p (t h)")
                    V.scalar_tensor_tensor(tmp32[:, 0, :], dts, -1.0, dts, ALU.mult, ALU.max).then_inc(dt_abs, 1)
                    link(V.tensor_scalar(tmp32[:, 1, :], dts, 0.0, None, ALU.max))
                elif kind == "kv":
                    for t in range(TT):
                        job = JOB[(st, t)]
                        b = bank[job % 8]
                        filled(dve, l, job)
                        V.tensor_copy(vtok[:, t, :], b[:, AKV * HD:2 * AKV * HD])
                        link(rope(b[:, 0:AKV * HD], AKV, t, ktok[:, t, 0:AKV, 0, :]))
                        drain_inc(dve.nop(), job)
                    dve.nop().then_inc(ka_rdy, 1)
                elif kind in ("qi", "q"):
                    for t in range(TT):
                        job = JOB[(st, t)]
                        filled(dve, l, job)
                        n = NCOL * st[1] if kind == "q" else 0
                        if kind == "q" and st[1] == 0 and t == 0:
                            filled(dve, l, JOB[(("qiT", 1), 0)])
                        dst = qbuf[:, t, n:n + NCOL].rearrange("p (h d) -> p h d", d=HD)
                        link(rope(bank[job % 8][:, :], NCOL // HD, t, dst))
                        drain_inc(dve.nop(), job)
                elif kind == "xbc":
                    for j in range(2):
                        m = 2 * st[1] + j
                        job = JOB[(st, j)]
                        b = bank[job % 8]
                        dve.wait_ge(conv0_rdy, l * 12 + (m + 1))
                        for k in range(1, TAPS):
                            for i in range(2):
                                ch = 2 * m + i
                                w = P_CW + (TAPS - 1 - k) * CC + ch
                                ins = V.scalar_tensor_tensor(conv[:, m % 2, i, k:SEQ], b[:, i * SEQ:(i + 1) * SEQ - k],
                                                             prm[:, w:w + 1], conv[:, m % 2, i, k:SEQ], ALU.mult, ALU.add)
                            if k < TAPS - 1:
                                link(ins)
                            else:
                                ins.then_inc(conv_rdy, 1)
                                dve.wait_ge(conv_rdy, l * 12 + (m + 1))
                                drain_inc(dve.nop(), job)
                elif kind == "acum":
                    dve.wait_ge(dt_log, l + 1)
                    dts = dtb[:, :, :].rearrange("p t h -> p (t h)")
                    link(V.tensor_tensor(dts, tmp32[:, 0, :], tmp32[:, 1, :], ALU.add))
                    V.scalar_tensor_tensor(dta[:, :, :], dtb[:, :, :], -1.0, bc(eac[:, :], 1, TT),
                                           ALU.mult, ALU.mult).then_inc(dt_rdy, 1)
                    filled(dve, l, job)
                    link(V.tensor_copy(acum[:, :, :].rearrange("p t h -> p (t h)"), b[:, 0:3 * SH]))
                    drain_inc(dve.nop(), job)
                    V.tensor_tensor(tail[:, :], acum[:, 2, :], acum[:, 0, :], ALU.subtract).then_inc(ac_rdy, 1)
                elif kind in ("kT", "kiT"):
                    filled(dve, l, job)
                    if kind == "kT":
                        dst = kT[:, 0:AKV, :]
                        src = b.rearrange("p (a t) -> p a t", a=AKV)
                    else:
                        dst, src = kT[:, AKV, :], b[:, 0:SEQ]
                    drain_inc(V.tensor_copy(dst, src), job)
                elif kind == "idx":
                    _, t, r, i = st
                    nk = (t + 1) * P
                    n = IDX.index(st)
                    drained(dve, l, job)
                    for j in range(NCOL // nk):
                        hd = 2 * (i * (NCOL // nk) + j) + r
                        src = rel[:, n % 2, j * nk:(j + 1) * nk]
                        if r == 0 and i == 0 and j == 0:
                            ins = V.tensor_scalar(isc[:, 0:nk], src, wis[:, t, hd:hd + 1], None, ALU.mult)
                        else:
                            ins = V.scalar_tensor_tensor(isc[:, 0:nk], src, wis[:, t, hd:hd + 1], isc[:, 0:nk],
                                                         ALU.mult, ALU.add)
                        link(ins)
                    dve.nop().then_inc(rel_used, 1)
                elif kind == "topk":
                    t = st[1]
                    nk = (t + 1) * P
                    s = isc[:, 0:nk]
                    link(V.tensor_tensor(isc[:, t * P:nk], isc[:, t * P:nk], caus, ALU.add))
                    for _ in range(TOPK // 8):
                        settle(dve)
                        link(V.max(top8[:, :], s))
                        settle(dve)
                        link(V.match_replace(s, top8[:, :], s, TAKEN))
                    link(V.tensor_scalar(pen[:, t, 0:nk], s, TAKEN / 2, NEG, ALU.is_gt, ALU.mult))
                    link(V.tensor_tensor(pen[:, t, t * P:nk], pen[:, t, t * P:nk], caus, ALU.add))
                elif kind == "cb":
                    filled(dve, l, job)
                    if st[1] == 0:
                        filled(dve, l, JOB[(IDX[-1], 0)])
                    drain_inc(V.tensor_tensor(cbm[:, st[1], :].rearrange("p (g t) -> p g t", g=SG),
                                              b.rearrange("p (g t) -> p g t", g=SG), bc(tri, 1, SG), ALU.mult), job)
                elif kind == "decay":
                    n = st[1]
                    t, g = SSD[n]
                    if n == 0:
                        dve.wait_ge(silu_rdy, l * 12 + 12)
                    if n >= 2:
                        filled(dve, l, JOB[(("ssd", n - 2), 0)])
                    for j in range(2):
                        job = JOB[(st, j)]
                        filled(dve, l, job)
                        for i in range(4):
                            hd = 4 * j + i
                            ins = V.tensor_scalar(mm_[:, n % 2, hd * P:(hd + 1) * P], bank[job % 8][:, i * P:(i + 1) * P],
                                                  acum[:, t, g * HG + hd:g * HG + hd + 1], 0.0, ALU.subtract, ALU.min)
                        drain_inc(ins, job)
                    drained(dve, l, job)
                    dve.nop().then_inc(seg_rdy, 1)
                    dve.wait_ge(dec_rdy, l * len(SSD) + (n + 1))
                    m3 = mm_[:, n % 2, :].rearrange("p (h t) -> p h t", h=HG)
                    V.tensor_tensor(m3, m3, bc(cbm[:, t, g * P:(g + 1) * P], 1, HG), ALU.mult).then_inc(m_rdy, 1)
                elif kind == "ssd":
                    n = st[1]
                    t, g = SSD[n]
                    y = xs[:, t, g * NCOL:(g + 1) * NCOL]
                    filled(dve, l, job)
                    dve.wait_ge(x_scaled, l * len(SSD) + (n + 1))
                    link(V.tensor_tensor(y, b, y, ALU.add))
                    drain_inc(dve.nop(), job)
                    if t == 1:
                        job = JOB[(st, 1)]
                        filled(dve, l, job)
                        link(V.tensor_tensor(ytmp.rearrange("p (h d) -> p h d", d=SP_),
                                             bank[job % 8][:, :].rearrange("p (h d) -> p h d", d=SP_),
                                             bc(eac[:, g * HG:(g + 1) * HG], 2, SP_), ALU.mult))
                        drain_inc(dve.nop(), job)
                        link(V.tensor_tensor(y, y, ytmp, ALU.add))
                elif kind == "ynorm":
                    drained(dve, l, JOB[(("z", 3), 1)])
                    for t in range(TT):
                        for g in range(SG):
                            y = xs[:, t, g * NCOL:(g + 1) * NCOL]
                            V.tensor_tensor(y, y, zt[:, t, g * NCOL:(g + 1) * NCOL], ALU.mult).then_inc(y_rdy, 1)
                    dve.wait_ge(ssq_rdy, l + 1)
                    rms(l * NORMS + 2, st_[:, 0:8], st_[:, 8:16], NCOL)
                    for t in range(TT):
                        for g in range(SG):
                            y = xs[:, t, g * NCOL:(g + 1) * NCOL]
                            ins = V.tensor_scalar(y, y, st_[:, 8 + t * SG + g:9 + t * SG + g], None, ALU.mult)
                    ins.then_inc(yn_rdy, 1)
                elif kind == "score":
                    n = st[1]
                    t, r, i = ATT[n]
                    nk = (t + 1) * P
                    nh = NCOL // nk
                    filled(dve, l, job)
                    if n == 0:
                        filled(dve, l, JOB[(("ssd", len(SSD) - 1), 1)])
                    if n >= 2:
                        filled(dve, l, JOB[(("probT", n - 2), 0)])
                    s3 = sco[:, n % 2, :].rearrange("p (h s) -> p h s", h=nh)
                    link(V.tensor_tensor(s3, b.rearrange("p (h s) -> p h s", h=nh), bc(pen[:, t, 0:nk], 1, nh), ALU.add))
                    drain_inc(dve.nop(), job)
                    link(V.tensor_reduce(mx[:, n % 4, 0:nh], s3, AX_X, ALU.max))
                    V.tensor_scalar(nmx[:, n % 4, 0:nh], mx[:, n % 4, 0:nh], -(HD ** -0.5), None,
                                    ALU.mult).then_inc(sc_rdy, 1)
                elif kind == "xscore":
                    n = st[1]
                    filled(dve, l, job)
                    if n >= 2:
                        dve.wait_ge(pr_rdy, l * (len(ATT) + 4) + (len(ATT) + n - 1))
                    link(V.tensor_reduce(mx[:, n % 4, 0:2], b.rearrange("p (h s) -> p h s", h=2), AX_X, ALU.max))
                    V.tensor_scalar(nmx[:, n % 4, 0:2], mx[:, n % 4, 0:2], -(XD ** -0.5), None,
                                    ALU.mult).then_inc(sc_rdy, 1)
                elif kind in ("pv", "xpv"):
                    n = st[1]
                    if kind == "pv":
                        t, r, i = ATT[n]
                        nh, w = 4 // (t + 1), HD
                        dst = qbuf[:, t, :].rearrange("p (a r d) -> p a r d", r=2, d=HD)[:, i * nh:(i + 1) * nh, r, :]
                    else:
                        t, pr = divmod(n, 2)
                        nh, w = 2, XD
                        dst = qbuf[:, t, pr * NCOL:(pr + 1) * NCOL].rearrange("p (a d) -> p a d", a=2)
                    filled(dve, l, job)
                    link(V.reciprocal(rs[:, n % 4, 0:nh], sm[:, n % 4, 0:nh]))
                    drain_inc(V.tensor_tensor(dst, b[:, 0:nh * w].rearrange("p (h d) -> p h d", h=nh),
                                              bc(rs[:, n % 4, 0:nh], 2, w), ALU.mult), job)
                elif kind == "ssdo":
                    n = st[1] * NCOL
                    for t in range(TT):
                        job = JOB[(st, t)]
                        filled(dve, l, job)
                        drained(dve, l, JOB[(("gate", 0, 1), 1)])
                        drain_inc(V.tensor_tensor(xn[:, t, n:n + NCOL], bank[job % 8][:, :], gate[:, t, n:n + NCOL], ALU.mult), job)
                elif kind == "atto":
                    n = st[1] * NCOL
                    for t in range(TT):
                        job = JOB[(st, t)]
                        filled(dve, l, job)
                        drained(dve, l, JOB[(("gate", 1, 1), 1)])
                        g_ = gate[:, t, n:n + NCOL]
                        link(V.tensor_tensor(g_, bank[job % 8][:, :], g_, ALU.mult))
                        drain_inc(V.tensor_tensor(xn[:, t, n:n + NCOL], xn[:, t, n:n + NCOL], g_, ALU.add), job)
                elif kind in ("wo", "co"):
                    n = st[1] * NCOL
                    if kind == "wo" and st[1] == 0:
                        dve.wait_ge(mem_in, l * 16 + 16)
                        normalise(l * NORMS + 3, memx, memx, cols(big, 2048, TT, D)).then_inc(mem_rdy, 1)
                    for t in range(TT):
                        job = JOB[(st, t)]
                        filled(dve, l, job)
                        drain_inc(V.tensor_tensor(h[:, t, n:n + NCOL], bank[job % 8][:, :], h[:, t, n:n + NCOL], ALU.add), job)
                elif kind == "router":
                    route(l, st, job, b)
                elif kind == "rank":
                    rank(l, job, b)

            def route(l, st, job, b):
                lg = cols(rt, R_LG, TT, G + G * E)
                filled(dve, l, job)
                link(V.tensor_tensor(lg, b.rearrange("p (a n) -> p a n", n=64)[:, 0:TT, 0:G + G * E],
                                     bc(prm[:, P_BR:P_BR + G + G * E], 1, TT), ALU.add))
                drain_inc(dve.nop(), job)
                dve.nop().then_inc(prm_used, 1)
                gm, oh = cols(rt, R_GM, TT), cols(rt, R_OH, TT, G)
                eq4 = cols(rt, R_EQ, TT, G)
                gd = cols(rt, R_GD, TT, G)
                prio = cst[:, C_PRIO:C_PRIO + E]
                first_max(lg[:, :, 0:G], prio[:, 0:G], gm, eq4, oh, G)
                dve.nop().then_inc(oh_rdy, 1)
                V.tensor_tensor(gd, lg[:, :, 0:G], bc(gm, 2, G), ALU.subtract).then_inc(rt_in, 1)
                lge = lg[:, :, G:G + G * E].rearrange("p t (g e) -> p t g e", g=G)
                pick = rt[:, R_PK:R_PK + TT * G * E].rearrange("p (t g e) -> p t g e", t=TT, g=G)
                for t in range(TT):
                    ins = V.tensor_tensor(pick[:, t], lge[:, t], bc(oh[:, t, :], 2, E), ALU.mult)
                link(ins)
                ein = cols(rt, R_EI, TT, E)
                for t in range(TT):
                    ins = V.tensor_reduce(ein[:, t, :], pick[:, t].rearrange("p g e -> p e g"), AX_X, ALU.add)
                link(ins)
                v1, v2 = cols(rt, R_V1, TT), cols(rt, R_V2, TT)
                oh1, oh2 = cols(rt, R_O1, TT, E), cols(rt, R_O2, TT, E)
                eq8 = cols(rt, R_EQ, TT, E)
                first_max(ein, prio, v1, eq8, oh1, E)
                link(V.scalar_tensor_tensor(ein, oh1, TAKEN, ein, ALU.mult, ALU.add))
                first_max(ein, prio, v2, eq8, oh2, E)
                V.tensor_tensor(cols(rt, R_DL, TT), v2, v1, ALU.subtract).then_inc(r2_in, 1)
                dve.wait_ge(rt_exp, l + 1)
                gs = cols(rt, R_GS, TT)
                link(V.tensor_reduce(gs, cols(rt, R_GE, TT, G), AX_X, ALU.add))
                dve.wait_ge(r2_exp, l + 1)
                tw, den = cols(rt, R_TW, TT), cols(rt, R_DN, TT)
                link(V.scalar_tensor_tensor(den, tw, 1.0, gs, ALU.add, ALU.mult))
                link(V.reciprocal(den, den))
                link(V.tensor_tensor(tw, tw, den, ALU.mult))
                wi_ = cols(rt, R_WI, TT, E)
                V.tensor_tensor(oh2, oh2, bc(tw, 2, E), ALU.mult)
                link(V.tensor_tensor(wi_, oh1, bc(den, 2, E), ALU.mult))
                link(V.tensor_tensor(wi_, wi_, oh2, ALU.add))

            def rank(l, job, b):
                filled(dve, l, job)
                oh = cols(rt, R_OH, TT, G)
                rk = cols(rt, R_RK, TT, G)
                V.tensor_tensor(rk, b.rearrange("p (a n) -> p a n", n=8)[:, 0:TT, 0:G], oh, ALU.mult)
                cnt = cols(rt, R_CN, G)
                link(V.tensor_scalar(cnt, b[:, 16:16 + G], P + 0.5, None, ALU.is_ge))
                drain_inc(dve.nop(), job)
                own, far = cols(rt, R_OW, TT), cols(rt, R_FA, TT, G)
                V.tensor_tensor(cnt, cnt, cst[:, C_GI:C_GI + G], ALU.mult)
                V.tensor_scalar(far, oh, -4.0 * SEQ, 4.0 * SEQ, ALU.mult, ALU.add)
                link(V.tensor_reduce(own, rk, AX_X, ALU.add))
                key = cols(rt, R_KY, NT, TT)
                V.tensor_tensor(key[:, 0:G, :].rearrange("p g t -> p t g"), far, bc(own, 2, G), ALU.add)
                V.tensor_scalar(key[:, G, :], own, -float(P), None, ALU.add)
                link(V.tensor_reduce(cols(rt, R_GF, 1), cnt, AX_X, ALU.add))
                V.tensor_copy(gsel[0:1, 0:1], rt[0:1, R_GF:R_GF + 1]).then_inc(keys_rdy, 1)
                dve.wait_ge(keys_rdy, l + 1)

            def expert_tile(l, t):
                u = l * NT + t
                for k in range(TT):
                    ins = V.tensor_scalar(sel[:, k, :], iota, rt[:, bass.ds(R_KY + t * TT + k, 1)], None, ALU.is_equal)
                ins.then_inc(sel_rdy, 1)
                for c in range(KC):
                    if c % 4 == 0:
                        dve.wait_ge(gat_s, u * 3 + (c // 4 + 1))
                    ins = V.tensor_scalar(xg[:, c, :], bank[6 + c // 4][:, (c % 4) * P:(c % 4 + 1) * P],
                                          prm_ffn[:, c:c + 1], None, ALU.mult)
                dve.wait_ge(gat_s, u * 3 + 3)
                V.tensor_copy(selT, bank[2][:, 0:TT * P])
                link(V.tensor_copy(cmb, bank[3][:, 0:E]))
                dve.nop().then_inc(xg_rdy, 1)
                for e in range(E):
                    dve.wait_ge(sil_s, u * E + (e + 1))
                    if e >= 2:
                        dve.wait_ge(hT_s, u * E + (e - 1))
                    V.scalar_tensor_tensor(hid[:, e % 2, :], sil[:, e % 2, :], cmb[:, e:e + 1], bank[e % 2][:, F:2 * F],
                                           ALU.mult, ALU.mult).then_inc(hid_s, 1)
                for k in range(TT):
                    for n in range(2):
                        dve.wait_ge(sct_s, u * 4 + (2 * k + n + 1))
                        hh = h[:, k, n * NCOL:(n + 1) * NCOL]
                        V.tensor_tensor(hh, bank[6 + n][:, :], hh, ALU.add).then_inc(add_s, 1)
                dve.wait_ge(add_s, u * 4 + 4)

            dve.wait_ge(cst_in, 32)
            with dve.Fori(0, DEPTH) as l:
                steps.at(l * (V_LAYER + NT * V_TILE))
                dve.wait_ge(prm_in, l * 16 + 16)
                for st in ORDER:
                    if st[0] == "router":
                        link(V.tensor_copy(prm_ffn[:, :], prm[:, P_NF:P_NF + KC]))
                    stage(l, st)
                assert steps.n == V_LAYER, f"V_LAYER = {steps.n}"
                settle(dve)
                with dve.Fori(0, G) as t:
                    steps.at(l * (V_LAYER + NT * V_TILE) + t * V_TILE + V_LAYER)
                    expert_tile(l, t)
                    assert steps.n == V_TILE, f"V_TILE = {steps.n}"
                steps.at(l * (V_LAYER + NT * V_TILE) + (G * V_TILE + V_LAYER))
                expert_tile(l, G)
            steps.at(DEPTH * (V_LAYER + NT * V_TILE))
            link(normalise(DEPTH * NORMS + 1, h, xn, xn))
            dve.wait_ge(fin_in, 16)
            for t in range(TT):
                V.tensor_tensor(xn[:, t, :], xn[:, t, :], gate[:, 0, :], ALU.mult).then_inc(fin_s, 1)


_NAMES = ["x", "mem", "w_in", "w_ssd_o", "w_attn_o", "w_out", "w_cq", "w_ckv", "w_co", "w_group", "w_router",
          "w_gate_e", "w_up_e", "w_down_e"]


def constants():
    import numpy as np
    i = np.arange(P)
    c = np.zeros((P, C_W), np.float32)
    c[:, C_ID:C_ID + P] = np.eye(P)
    c[:, C_TRI:C_TRI + P] = i[:, None] <= i[None, :]
    c[:, C_TRIS:C_TRIS + P] = i[:, None] < i[None, :]
    c[:, C_ONE:C_ONE + P] = 1.0
    c[:, C_IOTA:C_IOTA + P] = i[None, :]
    c[:, C_CAUS:C_CAUS + P] = np.where(i[None, :] <= i[:, None], 0.0, NEG)
    inv = (1.0 / (np.float32(10000.0) ** (np.arange(0, HD, 2, dtype=np.float32) / np.float32(HD)))).astype(np.float32)
    for t in range(TT):
        ang = (t * P + i).astype(np.float32)[:, None] * inv[None, :]
        c[:, C_COS + t * HD:C_COS + (t + 1) * HD] = np.tile(np.cos(ang), (1, 2))
        c[:, C_SIN + t * HD:C_SIN + (t + 1) * HD] = np.tile(np.sin(ang), (1, 2))
    c[:, C_PRIO:C_PRIO + E] = E - np.arange(E)
    c[:, C_GI:C_GI + G] = np.arange(G)
    c[:, C_MH:C_MH + E] = -0.5
    return c


def small_params(a):
    import numpy as np

    def by_block(v):
        return np.moveaxis(v.reshape(DEPTH, -1, P), 2, 1)

    def repeated(v):
        return np.broadcast_to(v[:, None, :], (DEPTH, P, v.shape[-1]))

    parts = [by_block(a[n].reshape(DEPTH, -1)) for n in
             ("conv_w", "conv_b", "norm_mix", "norm_xattn", "norm_mem", "norm_ffn", "ssd_norm")]
    parts += [repeated(a[n]) for n in ("dt_bias", "a_log", "d_skip", "b_group", "b_router")]
    return np.ascontiguousarray(np.concatenate(parts, axis=2))


def kernel(**inputs):
    import numpy as np
    import concourse.bacc as _bacc
    from concourse.bass_utils import run_bass_kernel_spmd as _run

    a = {k: np.asarray(v) for k, v in inputs.items()}
    arrays = {n: np.ascontiguousarray(a[n]) for n in _NAMES}
    arrays["x"] = arrays["x"].reshape(SEQ, D)
    arrays["mem"] = arrays["mem"].reshape(SEQ, D)
    arrays["params"] = small_params(a)
    arrays["consts"] = constants()
    arrays["gain_final"] = np.ascontiguousarray(np.broadcast_to(a["norm_final"][None, :], (P, D)))
    nc = _bacc.Bacc("TRN2", target_bir_lowering=False, num_devices=1)
    args = [nc.dram_tensor(f"in_{n}", v.shape, F32, kind="ExternalInput").ap() for n, v in arrays.items()]
    out = nc.dram_tensor("out_0", (SEQ, D), F32, kind="ExternalOutput").ap()
    trunk(nc, *args, out)
    r = _run(nc, [{f"in_{n}": v for n, v in arrays.items()}], core_ids=[0])
    return r.results[0]["out_0"].reshape(1, SEQ, D)
```

```python
import math
from contextlib import ExitStack

import concourse.bass as bass
from concourse import mybir

F32 = mybir.dt.float32
I32 = mybir.dt.int32
ALU = mybir.AluOpType
ACT = mybir.ActivationFunctionType
AX_X = mybir.AxisListType.X

P = 128
NEG = -1.0e30
TAKEN = -3.0e38
EPS = 1e-6

DEPTH, SEQ, D = 2, 256, 1024
TT = SEQ // P
KC = D // P
DI = 2 * D
SH, SP_, SG, SN = 32, 64, 4, 128
HG = SH // SG
CH = DI + 2 * SG * SN
CC = CH // P
TAPS = 4
AH, AKV, HD = 16, 2, 64
IH = 8
TOPK = SEQ // 4
XH, XD = 4, 256
G, E, F = 4, 8, 256
NCOL = 512
IDX_SCALE = HD ** -0.5 * IH ** -0.5

Z0 = 0
XBC0 = Z0 + DI
DT0 = XBC0 + CH
Q0 = DT0 + SH
K0 = Q0 + AH * HD
QI0 = K0 + 2 * AKV * HD
KI0 = QI0 + IH * HD
GS0 = KI0 + HD + IH
GA0 = GS0 + D

C_ID, C_TRI, C_TRIS, C_ONE, C_IOTA, C_CAUS, C_COS, C_SIN, C_PRIO, C_FULL, C_MH = (
    0, 128, 256, 384, 512, 640, 768, 896, 1024, 1032, 1040)
C_W = 1048
P_CW, P_CB, P_NM, P_NX, P_NE, P_NF, P_SN, P_DTB, P_AL, P_DS, P_BR = (
    0, 96, 120, 128, 136, 144, 152, 168, 200, 232, 264)
P_W = 300

(R_LG, R_GM, R_OH, R_EQ, R_GD, R_GE, R_T2, R_PK, R_EI, R_V1, R_V2, R_O1, R_O2, R_DL, R_TW, R_GS, R_DN, R_WI,
 R_US, R_KY, R_CN, R_CR, R_NR, R_PS, R_TG, R_KT, R_W) = (
    0, 72, 74, 82, 98, 106, 114, 116, 180, 196, 198, 200, 216, 232, 234, 236, 238, 240,
    256, 320, 384, 388, 420, 424, 428, 432, 448)

ATT = [(0, r, i) for r in range(2) for i in range(2)] + [(1, r, i) for r in range(2) for i in range(4)]
SSD = [(t, g) for t in range(TT) for g in range(SG)]


def make_order():
    o = [("norm", 0)] + [("hT", 0, i) for i in range(4)]
    o += [("small",), ("kv",), ("dt",), ("qi",), ("acum",), ("kT",), ("kiT",), ("xbc", 0), ("qiT", 0), ("qiT", 1), ("xbc", 1)]
    o += [("idx", 0, r, 0) for r in range(2)] + [("topk", 0), ("xbc", 2)]
    o += [("idx", 1, r, i) for r in range(2) for i in range(2)] + [("topk", 1), ("xbc", 3), ("xbc", 4), ("xbc", 5)]
    o += [("q", 0)] + [("xT", i) for i in range(4)] + [("bT",), ("q", 1)] + [("xT", i) for i in range(4, 8)]
    o += [("cb", 0), ("cb", 1)]
    for n, (t, g) in enumerate(SSD):
        o += [("decay", n)]
        if n:
            o += [("ssd", n - 1)]
        if n % 2 == 0:
            o += [("z", n // 2)]
        if n in (1, 3):
            o += [("qT", n - 1), ("qT", n)]
    o += [("ssd", len(SSD) - 1)]
    for n in range(len(ATT) + 2):
        if n < len(ATT):
            o += [("score", n)]
        if 1 <= n <= len(ATT):
            o += [("probT", n - 1)]
        if n >= 2:
            o += [("pv", n - 2)]
        if n == 3:
            o += [("gate", 0, 0)]
        if n == 7:
            o += [("gate", 0, 1)]
        if n < len(SSD):
            o += [("ygate", n)]
        if n == len(SSD):
            o += [("ynorm",)]
        if 9 <= n < 13:
            o += [("yT", 2 * n - 18), ("yT", 2 * n - 17)]
    o += [("ssdo", 0), ("ssdo", 1), ("gate", 1, 0), ("gate", 1, 1)]
    o += [("aT", i) for i in range(4)] + [("atto", 0), ("atto", 1)]
    o += [("mgT", i) for i in range(4)] + [("wo", 0), ("wo", 1)]
    o += [("memT", i) for i in range(4)] + [("ck", 0), ("ck", 1), ("cv", 0), ("cv", 1)]
    o += [("norm", 1)] + [("hT", 1, i) for i in range(4)] + [("cq", 0), ("cq", 1)]
    for n in range(6):
        if n < 4:
            o += [("xscore", n)]
        if 1 <= n <= 4:
            o += [("xprobT", n - 1)]
        if n >= 2:
            o += [("xpv", n - 2)]
    o += [("xoT", i) for i in range(4)] + [("co", 0), ("co", 1)]
    o += [("norm", 2)] + [("hT", 2, i) for i in range(4)] + [("router",), ("rank",)]
    return o


ORDER = make_order()
IDX = [st for st in ORDER if st[0] == "idx"]

JOBS_OF = {
    "hT": (1, "dve"), "small": (2, "dve"), "kv": (2, "dve"), "qi": (2, "dve"), "xbc": (2, "dve"),
    "acum": (1, "dve"), "kT": (1, "dve"), "kiT": (1, "dve"), "qiT": (1, "act"), "idx": (1, "act"), "q": (2, "dve"),
    "xT": (1, "act"), "bT": (1, "act"), "cb": (1, "dve"), "qT": (1, "act"), "decay": (2, "dve"),
    "z": (2, "act"), "score": (1, "dve"), "probT": (1, "act"), "pv": (1, "dve"), "gate": (2, "act"),
    "yT": (1, "dve"), "ssdo": (2, "dve"), "aT": (1, "act"), "atto": (2, "dve"), "mgT": (1, "act"),
    "wo": (2, "dve"), "memT": (1, "dve"), "ck": (2, "act"), "cv": (2, "act"), "cq": (2, "act"),
    "xscore": (1, "act"), "xprobT": (1, "act"), "xpv": (1, "dve"), "xoT": (1, "act"), "co": (2, "dve"),
    "router": (1, "dve"), "rank": (1, "dve"),
}


def ssd_jobs(n):
    return [("dve"), ("act" if SSD[n][0] == 0 else "dve")]


def make_jobs():
    jobs = []
    for st in ORDER:
        if st[0] == "ssd":
            jobs += [(st, i, own) for i, own in enumerate(ssd_jobs(st[1]))]
        elif st[0] in JOBS_OF:
            n, own = JOBS_OF[st[0]]
            jobs += [(st, i, own) for i in range(n)]
    return jobs


JOBS = make_jobs()
JOB = {(st, i): k for k, (st, i, _) in enumerate(JOBS)}
OWNER = [own for _, _, own in JOBS]
RANK = [sum(o == OWNER[k] for o in OWNER[:k + 1]) for k in range(len(JOBS))]
DRAINS = {own: OWNER.count(own) for own in ("dve", "act")}
NJ = len(JOBS)

CHUNKED = {"small": 1, "kv": 1, "qi": 1, "xbc": 1, "q": 1, "z": 1, "gate": 1, "ssdo": 2, "atto": 1, "wo": 1,
           "ck": 1, "cv": 1, "cq": 1, "co": 1}
CHUNKS = [(st, i) for st in ORDER if st[0] in CHUNKED for i in range(CHUNKED[st[0]])]
CHUNK = {c: k for k, c in enumerate(CHUNKS)}
W_SLOTS = 4

FIRST_BLOCK = 2
NORMS = 5
NCH = len(CHUNKS)
SLOT = [(c - NCH) % W_SLOTS for c in range(NCH)]
NTH = [SLOT[:c].count(SLOT[c]) for c in range(NCH)]

S = 32
BE = 4
NB = E // BE
ROUNDS = SEQ // S
GATHER = (6, 7, 0, 1)

V_LAYER = 207
A_LAYER = 2


def last_job(c):
    (st, i) = CHUNKS[c]
    return JOB[(st, 1 if JOBS_OF[st[0]][0] == 2 else 0)]


def bc(ap, axis, n):
    ap = ap.unsqueeze(axis)
    shape = list(ap.shape)
    shape[axis] = n
    return ap.to_broadcast(shape)


class Steps:

    def __init__(self, eng, sem):
        self.eng, self.sem, self.base, self.n = eng, sem, 0, 0

    def at(self, base):
        self.base, self.n = base, 0

    def link(self, ins):
        self.n += 1
        ins.then_inc(self.sem, 1)
        self.eng.wait_ge(self.sem, self.base + self.n)


def trunk(nc, x, mem, w_in, w_ssd_o, w_attn_o, w_out, w_cq, w_ckv, w_co, w_group, w_router,
          w_gate, w_up, w_down, params, consts, gain_final, out):
    with ExitStack() as ctx:
        def sb(name, shape, dt=F32):
            return ctx.enter_context(nc.sbuf_tensor(name, shape, dt))

        def sem(name):
            return ctx.enter_context(nc.semaphore(name))

        wring = sb("wring", [P, W_SLOTS, KC, NCOL])
        h = sb("h", [P, TT, D])
        xn = sb("xn", [P, TT, D])
        hT = sb("hT", [P, KC, SEQ])
        big = sb("big", [P, CC * SEQ])
        xs = sb("xs", [P, TT, DI])
        ga = sb("ga", [P, 4096])
        gate = ga[:, 0:TT * D].rearrange("p (t d) -> p t d", t=TT)
        att = ga[:, TT * D:2 * TT * D]
        qq = sb("qq", [P, 2, TT * D])
        qbuf = qq[:, 0, :].rearrange("p (t d) -> p t d", t=TT)
        qT = qq[:, 1, :].rearrange("p (c s) -> p c s", c=KC)
        scr = sb("scr", [P, 4096])
        kT = sb("kT", [P, AKV + 1, SEQ])
        qiT = sb("qiT", [P, IH // 2, SEQ])
        ktok = sb("ktok", [P, TT, AKV + 1, 2, HD])
        vtok = sb("vtok", [P, TT, AKV * HD])
        pen = sb("pen", [P, TT, SEQ])
        btok = sb("btok", [P, SG * SN])
        cst = sb("cst", [P, C_W])
        prm = sb("prm", [P, P_W])
        dtb = sb("dtb", [P, TT, SH])
        dta = sb("dta", [P, TT, SH])
        acum = sb("acum", [P, 3, SH])
        eac = sb("eac", [P, SH])
        tail = sb("tail", [P, SH])
        tmp32 = sb("tmp32", [P, 2, TT * SH])
        wis = sb("wis", [P, TT, IH])
        st_ = sb("sums", [P, 24])
        mx = sb("mx", [P, 4, 4])
        nmx = sb("nmx", [P, 4, 4])
        sm = sb("sm", [P, 4, 4])
        rs = sb("rs", [P, 4, 4])
        prm_ffn = sb("prm_ffn", [P, KC])
        top8 = sb("top8", [P, 8])
        rt = sb("rt", [P, R_W])
        itab = sb("itab", [1, 12], I32)
        ub = sb("ub", [P, 1])

        ident = cst[:, C_ID:C_ID + P]
        tri = cst[:, C_TRI:C_TRI + P]
        tris = cst[:, C_TRIS:C_TRIS + P]
        ones = cst[:, C_ONE:C_ONE + P]
        iota = cst[:, C_IOTA:C_IOTA + P]
        caus = cst[:, C_CAUS:C_CAUS + P]

        def cols(buf, a, *shape):
            v = buf[:, a:a + math.prod(shape)]
            names = "abc"[:len(shape)]
            if len(shape) == 1:
                return v
            return v.rearrange(f"p ({' '.join(names)}) -> p {' '.join(names)}",
                               **{n: s for n, s in zip(names, shape)})

        xbcT = cols(big, 0, CC, SEQ)
        zt = cols(big, 0, TT, DI)
        yT = cols(big, 0, 2 * KC, SEQ)
        memx = cols(big, 0, TT, D)
        memT = cols(big, 2048, KC, SEQ)
        xg = cols(big, 0, KC, E * S)
        sel = cols(big, 2048, TT, E * S)
        selw = cols(big, 2560, TT, E * S)
        selT = cols(big, 3072, NB, SEQ)
        sil = cols(big, 3584, NB, F)
        hid = cols(big, 4096, NB, F)
        hidT = cols(big, 4608, NB, F)
        yg = cols(big, 5120, D)
        ropeA = cols(scr, 0, NCOL)
        ropeB = cols(scr, 512, NCOL)
        conv = cols(scr, 1024, 2, 2, SEQ)
        rel = cols(scr, 2048, 2, NCOL)
        isc = cols(scr, 3072, SEQ)
        ex32 = cols(scr, 3328, TT * SH)
        mm_ = cols(scr, 0, 2, HG * P)
        state = cols(scr, 2048, SG, NCOL)
        ckT = cols(scr, 0, KC, SEQ)
        cv = cols(scr, 2048, TT, D)
        xdt = cols(att, 0, 2, NCOL)
        xdtt = cols(att, 1024, NCOL)
        ytmp = cols(att, 1536, NCOL)
        sco = cols(att, 0, 2, NCOL)
        pT = cols(att, 1024, 2, NCOL)
        cbm = cols(qiT[:, :, :].rearrange("p a b -> p (a b)"), 0, TT, SG * P)
        quad = [wring[:, 2 * i:2 * i + 2, :, :].rearrange("p s (a k) n -> p (s a) k n", a=2) for i in range(2)]
        dquad = [xs[:, :, :].rearrange("p t (a n) -> p (t a) n", a=2).rearrange("p j (k n) -> p j k n", n=NCOL),
                 scr[:, :].rearrange("p (j k n) -> p j k n", j=BE, n=NCOL),
                 qq[:, :, :].rearrange("p t (a n) -> p (t a) n", a=2).rearrange("p j (k n) -> p j k n", n=NCOL),
                 ga[:, :].rearrange("p (j k n) -> p j k n", j=BE, n=NCOL)]
        rw = btok[:, :].rearrange("p (k n) -> p k n", k=KC)[:, :, 0:G + G * E]

        bank = [ctx.enter_context(nc.psum_tensor(f"bank{b}", [P, NCOL], F32)) for b in range(8)]

        cst_in = sem("cst_in")
        prm_in = sem("prm_in")
        prm_used = sem("prm_used")
        w_in_sem = [sem(f"chunk_in{s}") for s in range(W_SLOTS)]
        quad_in = [sem(f"gate_up_in{i}") for i in range(2)]
        d_in_sem = [sem(f"down_in{i}") for i in range(2 * NB)]
        mem_in = sem("mem_in")
        router_in = sem("router_in")
        fin_in = sem("fin_in")
        filled_s = sem("bank_filled")
        drained_s = {"dve": sem("drained_by_dve"), "act": sem("drained_by_act")}
        v_step = sem("dve_step")
        a_step = sem("act_step")
        p_step = sem("pool_step")
        norm_rdy = sem("xn_ready")
        ka_rdy = sem("keys_roped")
        dup_rdy = sem("keys_doubled")
        conv0_rdy = sem("conv_started")
        conv_rdy = sem("conv_summed")
        silu_rdy = sem("conv_silu")
        dt_abs = sem("dt_abs")
        dt_log = sem("dt_log")
        dt_rdy = sem("dt_ready")
        ac_rdy = sem("acum_ready")
        eac_rdy = sem("exp_acum_ready")
        rel_used = sem("rel_used")
        x_scaled = sem("x_scaled")
        seg_rdy = sem("segments_ready")
        dec_rdy = sem("decay_ready")
        m_rdy = sem("decayed_scores_ready")
        y_rdy = sem("y_gated")
        yn_rdy = sem("y_normed")
        sc_rdy = sem("score_max_ready")
        pr_rdy = sem("probs_ready")
        mem_rdy = sem("mem_normed")
        var_rdy = sem("mean_square_ready")
        rstd_rdy = sem("rstd_ready")
        ssq_rdy = sem("y_squares_ready")
        rt_in = sem("group_logits_ready")
        rt_exp = sem("group_exp_ready")
        r2_in = sem("top2_diff_ready")
        r2_exp = sem("top2_exp_ready")
        oh_rdy = sem("onehot_ready")
        keys_rdy = sem("slots_ready")
        kt_rdy = sem("pass_keys_ready")
        sel_rdy = sem("selection_ready")
        gat_s = sem("gathered")
        xg_rdy = sem("gathered_x_ready")
        gu_s = sem("gate_up_quad_used")
        sil_s = sem("silu_done")
        hid_s = sem("hidden_ready")
        hT_s = sem("hidden_transposed")
        hTc_s = sem("hidden_copied")
        dn_s = sem("down_quad_used")
        yg_s = sem("expert_sum_ready")
        sct_s = sem("scattered")
        add_s = sem("h_added")
        fin_s = sem("final_ready")
        out_s = sem("stored")

        def filled(eng, l, job):
            eng.wait_ge(filled_s, l * NJ + job + 1)

        def drained(eng, l, job):
            eng.wait_ge(drained_s[OWNER[job]], l * DRAINS[OWNER[job]] + RANK[job])

        def settle(eng):
            eng.nop(nofuse=True)

        def drain_inc(ins, job):
            ins.then_inc(drained_s[OWNER[job]], 1)

        PE, AC, VE, SP = (mybir.EngineType.PE, mybir.EngineType.Activation, mybir.EngineType.DVE, mybir.EngineType.SP)

        def number(engine, at, most):
            return nc.values_load(itab[0:1, at], engines=[engine], min_val=0, max_val=most)

        def passes_before(eng, engine, l):
            eng.wait_ge(keys_rdy, l + 1)
            settle(eng)
            return number(engine, slice(8, 9), DEPTH * (G + ROUNDS))

        def more_passes(eng, engine, l, run):
            eng.wait_ge(keys_rdy, l + 2)
            settle(eng)
            more = number(engine, slice(9, 10), ROUNDS)
            with eng.If(more > 0):
                with eng.Fori(0, G) as g:
                    rounds = number(engine, bass.ds(g, 1), ROUNDS)
                    first = number(engine, bass.ds(g + G, 1), DEPTH * (G + ROUNDS))
                    with eng.If(rounds > 1):
                        with eng.Fori(1, rounds) as r_:
                            run(first + r_, g)

        block = ctx.enter_context(nc.Block())

        @block.sync
        def _(sp):
            sp.dma_start(h[:, :, :], x.rearrange("(t p) d -> p t d", p=P)).then_inc(cst_in, 16)
            sp.dma_start(cst[:, :], consts).then_inc(cst_in, 16)
            sp.nop().then_inc(prm_used, 1)
            sp.nop().then_inc(gu_s, 2)
            sp.nop().then_inc(dn_s, 2 * NB)

            def rows(w, a, b):
                return w.rearrange("(c p) n -> p c n", p=P)[:, :, a:b]

            def chunk(l, c, before):
                st, part = CHUNKS[c]
                kind = st[0]
                if c < W_SLOTS:
                    sp.wait_ge(gu_s, before * (2 * NB) + (SLOT[c] // 2 + 1))
                else:
                    filled(sp, l, last_job(c - W_SLOTS))
                settle(sp)
                slot = wring[:, SLOT[c], :, :]

                def load(dst, src):
                    sp.dma_start(dst, src).then_inc(w_in_sem[SLOT[c]], 16)

                def halves(src):
                    load(slot[:, 0:KC // 2, :], src[:, 0:KC // 2, :])
                    load(slot[:, KC // 2:KC, :], src[:, KC // 2:KC, :])

                if kind == "small":
                    load(slot[:, :, 0:SH], rows(w_in[l], DT0, DT0 + SH))
                    load(slot[:, :, SH:SH + HD + IH], rows(w_in[l], KI0, GS0))
                elif kind == "kv":
                    load(slot[:, 0:4, 0:256], rows(w_in[l], K0, QI0)[:, 0:4, :])
                    load(slot[:, 4:8, 0:256], rows(w_in[l], K0, QI0)[:, 4:8, :])
                elif kind == "ssdo":
                    n = st[1] * NCOL
                    halves(rows(w_ssd_o[l][part * D:(part + 1) * D, :], n, n + NCOL))
                else:
                    w, a = {
                        "qi": (w_in, QI0), "xbc": (w_in, XBC0), "q": (w_in, Q0), "z": (w_in, Z0),
                        "gate": (w_in, GS0 if st[1:2] == (0,) else GA0), "atto": (w_attn_o, 0),
                        "wo": (w_out, 0), "ck": (w_ckv, 0), "cv": (w_ckv, D), "cq": (w_cq, 0), "co": (w_co, 0),
                    }[kind]
                    a += NCOL * (st[-1] if len(st) > 1 else 0)
                    halves(rows(w[l], a, a + NCOL))

            def down(l, u, g, b, i):
                sp.wait_ge(dn_s, u * (2 * NB) + (2 * b + i + 1))
                settle(sp)
                for j in range(BE):
                    src = w_down[l, g, b * BE + j].rearrange("(k p) (a n) -> p a k n", p=P, a=2)
                    sp.dma_start(dquad[2 * b + i][:, j, :, :], src[:, i, :, :]).then_inc(d_in_sem[2 * b + i], 16)

            def experts(l, u, g, down_ahead=()):
                for b in range(NB):
                    for i in range(2):
                        filled(sp, l, last_job(NCH - (3 if i == 0 else 1)))
                        settle(sp)
                        sp.wait_ge(gu_s, u * (2 * NB) + (2 * b + i + 1))
                        settle(sp)
                        for j in range(BE):
                            for w, a in ((w_gate, 0), (w_up, F)):
                                src = w[l, g, b * BE + j].rearrange("(a k p) n -> p a k n", p=P, a=2)
                                sp.dma_start(quad[i][:, j, :, a:a + F], src[:, i, :, :]).then_inc(quad_in[i], 16)
                    for i in range(2):
                        if (b, i) not in down_ahead:
                            down(l, u, g, b, i)

            with sp.Fori(0, DEPTH) as l:
                sp.wait_ge(prm_used, l + 1)
                settle(sp)
                sp.dma_start(prm[:, :], params[l]).then_inc(prm_in, 16)
                before = passes_before(sp, SP, l)
                for c in range(NCH):
                    chunk(l, c, before)
                    if c == CHUNK[(("ssdo", 1), 1)]:
                        filled(sp, l, JOB[(("ssd", SG - 1), 1)])
                        settle(sp)
                        sp.dma_start(rw[:, :, 0:G], rows(w_group[l], 0, G)).then_inc(router_in, 16)
                        sp.dma_start(rw[:, :, G:G + G * E], rows(w_router[l], 0, G * E)).then_inc(router_in, 16)
                    if c == CHUNK[(("wo", 1), 0)]:
                        filled(sp, l, JOB[(("yT", 7), 0)])
                        settle(sp)
                        down(l, before, 0, 0, 0)
                filled(sp, l, JOB[(("xpv", 3), 0)])
                settle(sp)
                down(l, before, 0, 0, 1)
                down(l, before, 0, 1, 1)
                experts(l, before, 0, down_ahead=[(0, 0), (0, 1), (1, 1)])
                with sp.Fori(1, G) as g:
                    experts(l, before + g, g)
                more_passes(sp, SP, l, lambda u, g: experts(l, u, g))
            sp.wait_ge(fin_s, TT)
            sp.dma_start(out.rearrange("(t p) d -> p t d", p=P), xn[:, :, :]).then_inc(out_s, 16)
            sp.wait_ge(out_s, 16)

        @block.gpsimd
        def _(pool):
            def power(at, r):
                pool.wait_ge(var_rdy, at)
                nc.gpsimd.tensor_tensor(r, r, cst[:, C_MH:C_MH + r.shape[1]], ALU.pow).then_inc(rstd_rdy, 1)

            pool.wait_ge(cst_in, 32)
            with pool.Fori(0, DEPTH) as l:
                pool.wait_ge(prm_in, l * 16 + 16)
                power(l * NORMS + 1, st_[:, 18:20])
                pool.wait_ge(ka_rdy, l + 1)
                settle(pool)
                nc.gpsimd.tensor_copy(ktok[:, :, :, 1, :], ktok[:, :, :, 0, :]).then_inc(dup_rdy, 1)
                pool.wait_ge(eac_rdy, l + 1)
                for n, (t, g) in enumerate(SSD):
                    if n == 0:
                        drained(pool, l, JOB[(("xT", 7), 0)])
                    xsg = xs[:, t, g * NCOL:(g + 1) * NCOL].rearrange("p (h d) -> p h d", d=SP_)
                    if n >= 2:
                        filled(pool, l, JOB[(("ssd", n - 2), 1)])
                    dst = xdt[:, n % 2, :].rearrange("p (h d) -> p h d", d=SP_)
                    nc.gpsimd.tensor_tensor(dst, xsg, bc(dtb[:, t, g * HG:(g + 1) * HG], 2, SP_),
                                            ALU.mult).then_inc(p_step, 1)
                    pool.wait_ge(p_step, l * len(SSD) + (n + 1))
                    if t == 0:
                        if n >= 1:
                            filled(pool, l, JOB[(("ssd", n - 1), 1)])
                        nc.gpsimd.tensor_tensor(xdtt[:, :].rearrange("p (h d) -> p h d", d=SP_), dst,
                                                bc(tail[:, g * HG:(g + 1) * HG], 2, SP_), ALU.mult)
                    nc.gpsimd.tensor_tensor(xsg, xsg, bc(prm[:, P_DS + g * HG:P_DS + (g + 1) * HG], 2, SP_),
                                            ALU.mult).then_inc(x_scaled, 1)
                power(l * NORMS + 2, st_[:, 8:16])
                filled(pool, l, JOB[(("ssdo", 1), 1)])
                settle(pool)
                pool.dma_start(memx, mem.rearrange("(t p) d -> p t d", p=P)).then_inc(mem_in, 16)
                for k in (3, 4, 5):
                    power(l * NORMS + k, st_[:, 18:20])
            power(DEPTH * NORMS + 1, st_[:, 18:20])
            pool.wait_ge(norm_rdy, DEPTH * 3 + 1)
            pool.dma_start(gate[:, 0, :], gain_final).then_inc(fin_in, 16)
            pool.wait_ge(fin_in, 16)

        @block.tensor
        def _(pe):
            def transposes(l, job, blocks):
                free(l, job)
                b = bank[job % 8]
                for i, src in enumerate(blocks):
                    ins = nc.tensor.transpose(b[:, i * P:(i + 1) * P], src, ident)
                ins.then_inc(filled_s, 1)

            def free(l, job):
                if job >= 8:
                    drained(pe, l, job - 8)

            def chunk_in(l, c):
                pe.wait_ge(w_in_sem[SLOT[c]], (l * SLOT.count(SLOT[c]) + (NTH[c] + 1)) * 32)

            def by_token(l, st, src, width=NCOL):
                c = CHUNK[(st, 0)]
                chunk_in(l, c)
                for t in range(TT):
                    job = JOB[(st, t)]
                    free(l, job)
                    for i in range(KC):
                        k = (FIRST_BLOCK + i) % KC
                        ins = nc.tensor.matmul(bank[job % 8][:, 0:width], src[:, k, t * P:(t + 1) * P],
                                               wring[:, SLOT[c], k, 0:width], start=i == 0, stop=i == KC - 1)
                    ins.then_inc(filled_s, 1)

            def by_channel(l, st, src):
                c = CHUNK[(st, 0)]
                chunk_in(l, c)
                for j in range(2):
                    job = JOB[(st, j)]
                    free(l, job)
                    for i in range(2):
                        m = (2 * j + i) * P
                        for k in range(KC):
                            ins = nc.tensor.matmul(bank[job % 8][:, i * SEQ:(i + 1) * SEQ],
                                                   wring[:, SLOT[c], k, m:m + P], src[:, k, :],
                                                   start=k == 0, stop=k == KC - 1)
                    ins.then_inc(filled_s, 1)

            def pairs(src, i):
                return [src[:, t, (2 * i + j) * P:(2 * i + j + 1) * P] for j in range(2) for t in range(TT)]

            def stage(l, st):
                kind = st[0]
                if kind == "hT":
                    pe.wait_ge(norm_rdy, l * 3 + st[1] + 1)
                    transposes(l, JOB[(st, 0)], pairs(xn, st[2]))
                elif kind in ("small", "kv", "qi", "q", "z", "gate"):
                    if kind == "small":
                        drained(pe, l, JOB[(("hT", 0, 3), 0)])
                    by_token(l, st, hT, {"small": SH + HD + IH, "kv": 2 * AKV * HD}.get(kind, NCOL))
                elif kind == "xbc":
                    by_channel(l, st, hT)
                elif kind == "acum":
                    pe.wait_ge(dt_rdy, l + 1)
                    job = JOB[(st, 0)]
                    free(l, job)
                    b = bank[job % 8]
                    for t in range(TT):
                        nc.tensor.matmul(b[:, t * SH:(t + 1) * SH], tri, dta[:, t, :], start=True, stop=True)
                    nc.tensor.matmul(b[:, 2 * SH:3 * SH], ones, dta[:, 0, :],
                                     start=True, stop=True).then_inc(filled_s, 1)
                elif kind == "kT":
                    pe.wait_ge(dup_rdy, l + 1)
                    job = JOB[(st, 0)]
                    free(l, job)
                    b = bank[job % 8]
                    for i in range(2):
                        for t in range(TT):
                            src = ktok[:, t, i, :, :].rearrange("p a d -> p (a d)")
                            ins = nc.tensor.transpose(b[:, (2 * i + t) * P:(2 * i + t + 1) * P], src, ident)
                    ins.then_inc(filled_s, 1)
                elif kind == "kiT":
                    job = JOB[(st, 0)]
                    free(l, job)
                    b = bank[job % 8]
                    for t in range(TT):
                        src = ktok[:, t, 2, :, :].rearrange("p a d -> p (a d)")
                        ins = nc.tensor.transpose(b[:, t * P:(t + 1) * P], src, ident)
                    ins.then_inc(filled_s, 1)
                elif kind == "qiT":
                    if st[1] == 0:
                        drained(pe, l, JOB[(("qi",), 1)])
                    transposes(l, JOB[(st, 0)], pairs(qbuf, st[1]))
                elif kind == "idx":
                    _, t, r, i = st
                    drained(pe, l, JOB[(("kiT",), 0)])
                    drained(pe, l, JOB[(("qiT", 1), 0)])
                    job = JOB[(st, 0)]
                    free(l, job)
                    nk = (t + 1) * P
                    for j in range(NCOL // nk):
                        pair = i * (NCOL // nk) + j
                        ins = nc.tensor.matmul(bank[job % 8][:, j * nk:(j + 1) * nk],
                                               qiT[r * HD:(r + 1) * HD, pair, t * P:(t + 1) * P],
                                               kT[r * HD:(r + 1) * HD, 2, 0:nk], start=True, stop=True)
                    ins.then_inc(filled_s, 1)
                elif kind == "xT":
                    t, q = divmod(st[1], 4)
                    pe.wait_ge(silu_rdy, l * 12 + (2 * q + 2))
                    transposes(l, JOB[(st, 0)], [xbcT[:, 4 * q + i, t * P:(t + 1) * P] for i in range(4)])
                elif kind == "bT":
                    pe.wait_ge(silu_rdy, l * 12 + 12)
                    transposes(l, JOB[(st, 0)], [xbcT[:, 2 * KC + g, 0:P] for g in range(SG)])
                elif kind == "cb":
                    job = JOB[(st, 0)]
                    free(l, job)
                    ts = slice(st[1] * P, (st[1] + 1) * P)
                    for g in range(SG):
                        ins = nc.tensor.matmul(bank[job % 8][:, g * P:(g + 1) * P], xbcT[:, 2 * KC + g, ts],
                                               xbcT[:, 2 * KC + SG + g, ts], start=True, stop=True)
                    ins.then_inc(filled_s, 1)
                elif kind == "qT":
                    drained(pe, l, JOB[(("q", 1), 1)])
                    transposes(l, JOB[(st, 0)], pairs(qbuf, st[1]))
                elif kind == "decay":
                    t, g = SSD[st[1]]
                    for j in range(2):
                        job = JOB[(st, j)]
                        free(l, job)
                        for i in range(4):
                            hd = g * HG + 4 * j + i
                            ins = nc.tensor.matmul(bank[job % 8][:, i * P:(i + 1) * P],
                                                   dta[:, t, hd:hd + 1].to_broadcast([P, P]), tri,
                                                   start=True, stop=True)
                        ins.then_inc(filled_s, 1)
                elif kind == "ssd":
                    n = st[1]
                    t, g = SSD[n]
                    pe.wait_ge(x_scaled, l * len(SSD) + (n + 1))
                    pe.wait_ge(m_rdy, l * len(SSD) + (n + 1))
                    job = JOB[(st, 0)]
                    free(l, job)
                    for i in range(HG):
                        ins = nc.tensor.matmul(bank[job % 8][:, i * SP_:(i + 1) * SP_],
                                               mm_[:, n % 2, i * P:(i + 1) * P],
                                               xdt[:, n % 2, i * SP_:(i + 1) * SP_], start=True, stop=True)
                    ins.then_inc(filled_s, 1)
                    job = JOB[(st, 1)]
                    free(l, job)
                    if t == 0:
                        drained(pe, l, JOB[(("bT",), 0)])
                        ins = nc.tensor.matmul(bank[job % 8][:, :], btok[:, g * SN:(g + 1) * SN], xdtt[:, :],
                                               start=True, stop=True)
                    else:
                        drained(pe, l, JOB[(("ssd", g), 1)])
                        ins = nc.tensor.matmul(bank[job % 8][:, :], xbcT[:, 2 * KC + SG + g, P:2 * P],
                                               state[:, g, :], start=True, stop=True)
                    ins.then_inc(filled_s, 1)
                elif kind == "score":
                    t, r, i = ATT[st[1]]
                    drained(pe, l, JOB[(("qT", 3), 0)])
                    drained(pe, l, JOB[(("kT",), 0)])
                    job = JOB[(st, 0)]
                    free(l, job)
                    nk = (t + 1) * P
                    nh = NCOL // nk
                    for j in range(nh):
                        pair = i * nh + j
                        ins = nc.tensor.matmul(bank[job % 8][:, j * nk:(j + 1) * nk],
                                               qT[r * HD:(r + 1) * HD, pair, t * P:(t + 1) * P],
                                               kT[r * HD:(r + 1) * HD, pair // 4, 0:nk], start=True, stop=True)
                    ins.then_inc(filled_s, 1)
                elif kind in ("probT", "xprobT"):
                    n = st[1] + (len(ATT) if kind == "xprobT" else 0)
                    pe.wait_ge(pr_rdy, l * (len(ATT) + 4) + (n + 1))
                    src = sco[:, st[1] % 2, :]
                    transposes(l, JOB[(st, 0)], [src[:, i * P:(i + 1) * P] for i in range(4)])
                elif kind == "pv":
                    n = st[1]
                    t, r, i = ATT[n]
                    drained(pe, l, JOB[(("probT", n), 0)])
                    job = JOB[(st, 0)]
                    free(l, job)
                    nk = t + 1
                    nh = 4 // nk
                    for j in range(nh):
                        grp = (i * nh + j) // 4
                        for s in range(nk):
                            ins = nc.tensor.matmul(bank[job % 8][:, j * HD:(j + 1) * HD],
                                                   pT[:, n % 2, (j * nk + s) * P:(j * nk + s + 1) * P],
                                                   vtok[:, s, grp * HD:(grp + 1) * HD],
                                                   start=s == 0, stop=s == nk - 1)
                    ins.then_inc(filled_s, 1)
                elif kind == "yT":
                    pe.wait_ge(yn_rdy, l + 1)
                    transposes(l, JOB[(st, 0)], pairs(xs, st[1]))
                elif kind == "ssdo":
                    drained(pe, l, JOB[(("yT", 7), 0)])
                    jobs = [JOB[(st, t)] for t in range(TT)]
                    for half in range(2):
                        c = CHUNK[(st, half)]
                        chunk_in(l, c)
                        for t in range(TT):
                            if half == 0:
                                free(l, jobs[t])
                            for k in range(KC):
                                ins = nc.tensor.matmul(bank[jobs[t] % 8][:, :],
                                                       yT[:, half * KC + k, t * P:(t + 1) * P],
                                                       wring[:, SLOT[c], k, :],
                                                       start=half == 0 and k == 0, stop=half == 1 and k == KC - 1)
                            if half == 1:
                                ins.then_inc(filled_s, 1)
                elif kind == "aT":
                    drained(pe, l, JOB[(("pv", len(ATT) - 1), 0)])
                    transposes(l, JOB[(st, 0)], pairs(qbuf, st[1]))
                elif kind == "atto":
                    drained(pe, l, JOB[(("aT", 3), 0)])
                    by_token(l, st, qT)
                elif kind == "mgT":
                    drained(pe, l, JOB[(("atto", 1), 1)])
                    transposes(l, JOB[(st, 0)], pairs(xn, st[1]))
                elif kind == "wo":
                    drained(pe, l, JOB[(("mgT", 3), 0)])
                    by_token(l, st, hT)
                elif kind == "memT":
                    pe.wait_ge(mem_rdy, l + 1)
                    transposes(l, JOB[(st, 0)], pairs(memx, st[1]))
                elif kind == "ck":
                    drained(pe, l, JOB[(("memT", 3), 0)])
                    by_channel(l, st, memT)
                elif kind == "cv":
                    by_token(l, st, memT)
                elif kind == "cq":
                    drained(pe, l, JOB[(("hT", 1, 3), 0)])
                    by_channel(l, st, hT)
                elif kind == "xscore":
                    t, pr = divmod(st[1], 2)
                    drained(pe, l, JOB[(("cq", 1), 1)])
                    job = JOB[(st, 0)]
                    free(l, job)
                    for j in range(2):
                        for k in range(2):
                            blk = 2 * (2 * pr + j) + k
                            ins = nc.tensor.matmul(bank[job % 8][:, j * SEQ:(j + 1) * SEQ],
                                                   qT[:, blk, t * P:(t + 1) * P], ckT[:, blk, :],
                                                   start=k == 0, stop=k == 1)
                    ins.then_inc(filled_s, 1)
                elif kind == "xpv":
                    n = st[1]
                    t, pr = divmod(n, 2)
                    drained(pe, l, JOB[(("xprobT", n), 0)])
                    job = JOB[(st, 0)]
                    free(l, job)
                    for j in range(2):
                        hd = 2 * pr + j
                        for s in range(2):
                            ins = nc.tensor.matmul(bank[job % 8][:, j * XD:(j + 1) * XD],
                                                   pT[:, n % 2, (2 * j + s) * P:(2 * j + s + 1) * P],
                                                   cv[:, s, hd * XD:(hd + 1) * XD], start=s == 0, stop=s == 1)
                    ins.then_inc(filled_s, 1)
                elif kind == "xoT":
                    drained(pe, l, JOB[(("xpv", 3), 0)])
                    transposes(l, JOB[(st, 0)], pairs(qbuf, st[1]))
                elif kind == "co":
                    drained(pe, l, JOB[(("xoT", 3), 0)])
                    by_token(l, st, qT)
                elif kind == "router":
                    drained(pe, l, JOB[(("hT", 2, 3), 0)])
                    pe.wait_ge(router_in, l * 32 + 32)
                    job = JOB[(st, 0)]
                    free(l, job)
                    for t in range(TT):
                        for k in range(KC):
                            ins = nc.tensor.matmul(bank[job % 8][:, t * 64:t * 64 + G + G * E],
                                                   hT[:, k, t * P:(t + 1) * P], rw[:, k, :],
                                                   start=k == 0, stop=k == KC - 1)
                    ins.then_inc(filled_s, 1)
                elif kind == "rank":
                    pe.wait_ge(oh_rdy, l + 1)
                    job = JOB[(st, 0)]
                    free(l, job)
                    b = bank[job % 8]
                    us = cols(rt, R_US, TT, G * E)
                    w = G * E
                    nc.tensor.matmul(b[:, 0:w], tris, us[:, 0, :], start=True, stop=True)
                    nc.tensor.matmul(b[:, w:2 * w], tris, us[:, 1, :], start=True, stop=False)
                    nc.tensor.matmul(b[:, w:2 * w], ones, us[:, 0, :], start=False, stop=True)
                    nc.tensor.matmul(b[:, 2 * w:3 * w], ones, us[:, 0, :], start=True, stop=False)
                    nc.tensor.matmul(b[:, 2 * w:3 * w], ones, us[:, 1, :], start=False,
                                     stop=True).then_inc(filled_s, 1)

            def expert_pass(u):
                pe.wait_ge(sel_rdy, u * 2 + 1)
                for c in range(KC):
                    b = bank[GATHER[c // 2]]
                    for k in range(TT):
                        ins = nc.tensor.matmul(b[:, (c % 2) * E * S:(c % 2 + 1) * E * S], xn[:, k, c * P:(c + 1) * P],
                                               sel[:, k, :], start=k == 0, stop=k == TT - 1)
                    if c % 2:
                        ins.then_inc(gat_s, 1)
                pe.wait_ge(sel_rdy, u * 2 + 2)
                for b in range(NB):
                    for k in range(TT):
                        ins = nc.tensor.transpose(bank[2][:, b * SEQ + k * P:b * SEQ + (k + 1) * P],
                                                  selw[:, k, b * P:(b + 1) * P], ident)
                ins.then_inc(gat_s, 1)
                pe.wait_ge(xg_rdy, u * 2 + 2)
                for b in range(NB):
                    for i in range(2):
                        pe.wait_ge(quad_in[i], (u * NB + (b + 1)) * (2 * BE * 16))
                        for k in range(KC // 2):
                            for j in range(BE):
                                e = (b * BE + j) * S
                                ins = nc.tensor.matmul(bank[b][j * S:(j + 1) * S, :], xg[:, i * (KC // 2) + k, e:e + S],
                                                       quad[i][:, j, k, :], start=i == 0 and k == 0,
                                                       stop=i == 1 and k == KC // 2 - 1)
                        ins.then_inc(gu_s, 1)
                    pe.wait_ge(hid_s, u * NB + (b + 1))
                    for k in range(2):
                        ins = nc.tensor.transpose(bank[3][:, k * P:(k + 1) * P], hid[:, b, k * P:(k + 1) * P], ident)
                    ins.then_inc(hT_s, 1)
                    pe.wait_ge(hTc_s, u * NB + (b + 1))
                    for n in range(2):
                        pe.wait_ge(d_in_sem[2 * b + n], (u + 1) * (BE * 16))
                        for k in range(2):
                            for j in range(BE):
                                ins = nc.tensor.matmul(bank[4 + n][j * S:(j + 1) * S, :],
                                                       hidT[:, b, k * P + j * S:k * P + (j + 1) * S],
                                                       dquad[2 * b + n][:, j, k, :], start=k == 0, stop=k == 1)
                        ins.then_inc(dn_s, 1)
                    for k in range(TT):
                        for n in range(2):
                            if k == 0:
                                pe.wait_ge(yg_s, u * (2 * NB) + (2 * b + n + 1))
                            if b or k:
                                pe.wait_ge(add_s, u * (4 * NB) + (4 * b + 2 * k + n - 1))
                            nc.tensor.matmul(bank[6 + n][:, :], selT[:, b, k * P:(k + 1) * P],
                                             yg[:, n * NCOL:(n + 1) * NCOL], start=True, stop=True).then_inc(sct_s, 1)

            pe.wait_ge(cst_in, 32)
            with pe.Fori(0, DEPTH) as l:
                before = passes_before(pe, PE, l)
                for st in ORDER:
                    stage(l, st)
                drained(pe, l, max(k for k in range(NJ) if OWNER[k] == "dve"))
                drained(pe, l, max(k for k in range(NJ) if OWNER[k] == "act"))
                settle(pe)
                with pe.Fori(0, G) as g:
                    expert_pass(before + g)
                more_passes(pe, PE, l, lambda u, g: expert_pass(u))

        @block.scalar
        def _(act):
            steps = Steps(act, a_step)

            def stage(l, st):
                kind = st[0]
                job = JOB.get((st, 0))
                if kind == "xbc":
                    for j in range(2):
                        m = 2 * st[1] + j
                        filled(act, l, JOB[(st, j)])
                        if m >= 2:
                            act.wait_ge(silu_rdy, l * 12 + (m - 1))
                        for i in range(2):
                            ch = 2 * m + i
                            ins = nc.scalar.activation(conv[:, m % 2, i, :], bank[JOB[(st, j)] % 8][:, i * SEQ:(i + 1) * SEQ],
                                                       ACT.Identity, bias=prm[:, P_CB + ch:P_CB + ch + 1],
                                                       scale=prm[:, P_CW + 3 * CC + ch:P_CW + 3 * CC + ch + 1])
                        ins.then_inc(conv0_rdy, 1)
                    for j in range(2):
                        m = 2 * st[1] + j
                        act.wait_ge(conv_rdy, l * 12 + (m + 1))
                        nc.scalar.activation(xbcT[:, 2 * m:2 * m + 2, :], conv[:, m % 2, :, :],
                                             ACT.Silu).then_inc(silu_rdy, 1)
                elif kind == "dt":
                    act.wait_ge(dt_abs, l + 1)
                    steps.link(nc.scalar.activation(ex32, tmp32[:, 0, :], ACT.Exp, scale=-1.0))
                    steps.link(nc.scalar.activation(tmp32[:, 0, :], ex32, ACT.Ln, bias=1.0))
                    nc.scalar.activation(eac[:, :], prm[:, P_AL:P_AL + SH], ACT.Exp).then_inc(dt_log, 1)
                elif kind == "acum":
                    act.wait_ge(ac_rdy, l + 1)
                    nc.scalar.activation(eac[:, :], acum[:, 1, :], ACT.Exp)
                    nc.scalar.activation(tail[:, :], tail[:, :], ACT.Exp).then_inc(eac_rdy, 1)
                elif kind in ("qiT", "xT", "qT", "aT", "mgT", "xoT", "bT"):
                    filled(act, l, job)
                    b = bank[job % 8][:, :]
                    if kind == "bT":
                        dst = btok[:, :]
                    elif kind == "xT":
                        t, q = divmod(st[1], 4)
                        dst = xs[:, t, q * NCOL:(q + 1) * NCOL]
                    else:
                        if kind == "mgT" and st[1] == 0:
                            filled(act, l, JOB[(("gate", 1, 1), 1)])
                        to = {"qiT": qiT, "qT": qT, "aT": qT, "mgT": hT, "xoT": qT}[kind]
                        dst = to[:, 2 * st[1]:2 * st[1] + 2, :].rearrange("p c t -> p (c t)")
                    drain_inc(nc.scalar.activation(dst, b, ACT.Copy), job)
                elif kind == "idx":
                    filled(act, l, job)
                    n = IDX.index(st)
                    if n >= 2:
                        act.wait_ge(rel_used, l * len(IDX) + (n - 1))
                    drain_inc(nc.scalar.activation(rel[:, n % 2, :], bank[job % 8][:, :], ACT.Relu), job)
                elif kind in ("z", "gate", "cv"):
                    for t in range(TT):
                        job = JOB[(st, t)]
                        filled(act, l, job)
                        n = st[-1] * NCOL
                        if kind == "gate" and st[1] == 1:
                            drained(act, l, JOB[(("ssdo", 1), 1)])
                        dst = {"z": zt, "gate": gate, "cv": cv}[kind][:, t, n:n + NCOL]
                        func = {"z": ACT.Silu, "gate": ACT.Sigmoid, "cv": ACT.Copy}[kind]
                        drain_inc(nc.scalar.activation(dst, bank[job % 8][:, :], func), job)
                elif kind in ("ck", "cq"):
                    to = {"ck": ckT, "cq": qT}[kind]
                    for j in range(2):
                        job = JOB[(st, j)]
                        filled(act, l, job)
                        blk = 4 * st[1] + 2 * j
                        drain_inc(nc.scalar.activation(to[:, blk:blk + 2, :].rearrange("p c t -> p (c t)"),
                                                       bank[job % 8][:, :], ACT.Copy), job)
                elif kind == "decay":
                    n = st[1]
                    act.wait_ge(seg_rdy, l * len(SSD) + (n + 1))
                    nc.scalar.activation(mm_[:, n % 2, :], mm_[:, n % 2, :], ACT.Exp).then_inc(dec_rdy, 1)
                elif kind == "ssd":
                    t, g = SSD[st[1]]
                    if t == 0:
                        job = JOB[(st, 1)]
                        filled(act, l, job)
                        drain_inc(nc.scalar.activation(state[:, g, :], bank[job % 8][:, :], ACT.Copy), job)
                elif kind == "ygate":
                    t, g = SSD[st[1]]
                    act.wait_ge(y_rdy, l * len(SSD) + (st[1] + 1))
                    nc.scalar.activation(zt[:, t, g * NCOL:(g + 1) * NCOL], xs[:, t, g * NCOL:(g + 1) * NCOL], ACT.Square,
                                         accum_out=st_[:, st[1]:st[1] + 1]).then_inc(ssq_rdy, 1)
                elif kind == "score":
                    n = st[1]
                    t, r, i = ATT[n]
                    nk = (t + 1) * P
                    act.wait_ge(sc_rdy, l * (len(ATT) + 4) + (n + 1))
                    for j in range(NCOL // nk):
                        ins = nc.scalar.activation(sco[:, n % 2, j * nk:(j + 1) * nk], sco[:, n % 2, j * nk:(j + 1) * nk],
                                                   ACT.Exp, bias=nmx[:, n % 4, j:j + 1], scale=HD ** -0.5,
                                                   accum_out=sm[:, n % 4, j:j + 1])
                    ins.then_inc(pr_rdy, 1)
                elif kind == "xscore":
                    n = st[1]
                    act.wait_ge(sc_rdy, l * (len(ATT) + 4) + (len(ATT) + n + 1))
                    if n >= 2:
                        filled(act, l, JOB[(("xprobT", n - 2), 0)])
                    for j in range(2):
                        ins = nc.scalar.activation(sco[:, n % 2, j * SEQ:(j + 1) * SEQ], bank[job % 8][:, j * SEQ:(j + 1) * SEQ],
                                                   ACT.Exp, bias=nmx[:, n % 4, j:j + 1], scale=XD ** -0.5,
                                                   accum_out=sm[:, n % 4, j:j + 1])
                    ins.then_inc(pr_rdy, 1)
                    act.wait_ge(pr_rdy, l * (len(ATT) + 4) + (len(ATT) + n + 1))
                    drain_inc(act.nop(), job)
                elif kind in ("probT", "xprobT"):
                    filled(act, l, job)
                    n = st[1]
                    if n >= 2:
                        filled(act, l, JOB[("pv" if kind == "probT" else "xpv", n - 2), 0])
                    drain_inc(nc.scalar.activation(pT[:, n % 2, :], bank[job % 8][:, :], ACT.Copy), job)
                elif kind == "router":
                    act.wait_ge(rt_in, l + 1)
                    gd = cols(rt, R_GD, TT * G)
                    nc.scalar.activation(cols(rt, R_GE, TT * G), gd, ACT.Exp).then_inc(rt_exp, 1)
                    act.wait_ge(r2_in, l + 1)
                    nc.scalar.activation(cols(rt, R_TW, TT), cols(rt, R_DL, TT), ACT.Exp).then_inc(r2_exp, 1)

            def expert_pass(u):
                for i in (1, 3):
                    act.wait_ge(gat_s, u * 5 + (i + 1))
                    for c in (2 * i, 2 * i + 1):
                        ins = nc.scalar.activation(xg[:, c, :], bank[GATHER[i]][:, (c % 2) * E * S:(c % 2 + 1) * E * S],
                                                   ACT.Copy, scale=prm_ffn[:, c:c + 1])
                ins.then_inc(xg_rdy, 1)
                for b in range(NB):
                    act.wait_ge(gu_s, u * (2 * NB) + (2 * b + 2 + 2))
                    nc.scalar.activation(sil[:, b, :], bank[b][:, 0:F], ACT.Silu).then_inc(sil_s, 1)
                    act.wait_ge(hT_s, u * NB + (b + 1))
                    nc.scalar.activation(hidT[:, b, :], bank[3][:, 0:F], ACT.Copy).then_inc(hTc_s, 1)
                    for n in range(2):
                        act.wait_ge(dn_s, u * (2 * NB) + (2 * b + n + 1 + 2 * NB))
                        if b:
                            act.wait_ge(sct_s, u * (4 * NB) + (n + 3))
                        nc.scalar.activation(yg[:, n * NCOL:(n + 1) * NCOL], bank[4 + n][:, :],
                                             ACT.Copy).then_inc(yg_s, 1)

            with act.Fori(0, DEPTH) as l:
                before = passes_before(act, AC, l)
                act.wait_ge(prm_in, l * 16 + 16)
                steps.at(l * A_LAYER)
                for st in ORDER:
                    stage(l, st)
                assert steps.n == A_LAYER, f"A_LAYER = {steps.n}"
                with act.Fori(0, G) as g:
                    expert_pass(before + g)
                more_passes(act, AC, l, lambda u, g: expert_pass(u))

        @block.vector
        def _(dve):
            steps = Steps(dve, v_step)
            link = steps.link
            V = nc.vector

            def rms(at, ss, r, n):
                V.tensor_scalar(r, ss, 1.0 / n, EPS, ALU.mult, ALU.add).then_inc(var_rdy, 1)
                dve.wait_ge(rstd_rdy, at)

            def normalise(at, src, dst, squares):
                for t in range(TT):
                    ins = V.scalar_tensor_tensor(squares[:, t, :], src[:, t, :], 1.0, src[:, t, :], ALU.mult, ALU.mult,
                                                 accum_out=st_[:, 16 + t:17 + t])
                link(ins)
                rms(at, st_[:, 16:18], st_[:, 18:20], D)
                for t in range(TT):
                    ins = V.tensor_scalar(dst[:, t, :], src[:, t, :], st_[:, 18 + t:19 + t], None, ALU.mult)
                return ins

            def rope(src, nh, t, dst):
                a = ropeA[:, 0:nh * HD].rearrange("p (h d) -> p h d", d=HD)
                b = ropeB[:, 0:nh * HD].rearrange("p (h d) -> p h d", d=HD)
                s = src.rearrange("p (h d) -> p h d", d=HD)
                cos = bc(cst[:, C_COS + t * HD:C_COS + (t + 1) * HD], 1, nh)
                sin = bc(cst[:, C_SIN + t * HD:C_SIN + (t + 1) * HD], 1, nh)
                V.tensor_tensor(a, s, cos, ALU.mult)
                link(V.tensor_tensor(b, s, sin, ALU.mult))
                hf = HD // 2
                V.tensor_tensor(dst[:, :, 0:hf], a[:, :, 0:hf], b[:, :, hf:HD], ALU.subtract)
                return V.tensor_tensor(dst[:, :, hf:HD], a[:, :, hf:HD], b[:, :, 0:hf], ALU.add)

            def first_max(src, prio, m, eq, oh, n):
                link(V.tensor_reduce(m, src, AX_X, ALU.max))
                link(V.tensor_tensor(eq, src, bc(m, 2, n), ALU.is_equal))
                link(V.tensor_tensor(eq, eq, bc(prio, 1, TT), ALU.mult))
                link(V.tensor_reduce(cols(rt, R_T2, TT), eq, AX_X, ALU.max))
                link(V.tensor_tensor(oh, eq, bc(cols(rt, R_T2, TT), 2, n), ALU.is_equal))

            def stage(l, st):
                kind = st[0]
                job = JOB.get((st, 0))
                b = bank[job % 8][:, :] if job is not None else None
                if kind == "norm":
                    if st[1] == 1:
                        drained(dve, l, JOB[(("wo", 1), 1)])
                    elif st[1] == 2:
                        drained(dve, l, JOB[(("co", 1), 1)])
                    normalise(l * NORMS + (1, 4, 5)[st[1]], h, xn, xn).then_inc(norm_rdy, 1)
                elif kind in ("hT", "memT", "yT"):
                    filled(dve, l, job)
                    i = st[-1]
                    to, gain = {"hT": (hT, (P_NM, P_NX, P_NF)[st[1] if kind == "hT" else 0]),
                                "memT": (memT, P_NE), "yT": (yT, P_SN)}[kind]
                    for j in range(2):
                        ins = V.tensor_scalar(to[:, 2 * i + j, :], b[:, j * SEQ:(j + 1) * SEQ],
                                              prm[:, gain + 2 * i + j:gain + 2 * i + j + 1], None, ALU.mult)
                    drain_inc(ins, job)
                elif kind == "small":
                    for t in range(TT):
                        job = JOB[(st, t)]
                        b = bank[job % 8]
                        filled(dve, l, job)
                        V.tensor_tensor(dtb[:, t, :], b[:, 0:SH], prm[:, P_DTB:P_DTB + SH], ALU.add)
                        V.tensor_scalar(wis[:, t, :], b[:, SH + HD:SH + HD + IH], IDX_SCALE, None, ALU.mult)
                        link(rope(b[:, SH:SH + HD], 1, t, ktok[:, t, 2:3, 0, :]))
                        drain_inc(dve.nop(), job)
                    dts = dtb[:, :, :].rearrange("p t h -> p (t h)")
                    V.scalar_tensor_tensor(tmp32[:, 0, :], dts, -1.0, dts, ALU.mult, ALU.max).then_inc(dt_abs, 1)
                    link(V.tensor_scalar(tmp32[:, 1, :], dts, 0.0, None, ALU.max))
                elif kind == "kv":
                    for t in range(TT):
                        job = JOB[(st, t)]
                        b = bank[job % 8]
                        filled(dve, l, job)
                        V.tensor_copy(vtok[:, t, :], b[:, AKV * HD:2 * AKV * HD])
                        link(rope(b[:, 0:AKV * HD], AKV, t, ktok[:, t, 0:AKV, 0, :]))
                        drain_inc(dve.nop(), job)
                    dve.nop().then_inc(ka_rdy, 1)
                elif kind in ("qi", "q"):
                    for t in range(TT):
                        job = JOB[(st, t)]
                        filled(dve, l, job)
                        n = NCOL * st[1] if kind == "q" else 0
                        if kind == "q" and st[1] == 0 and t == 0:
                            filled(dve, l, JOB[(("qiT", 1), 0)])
                        dst = qbuf[:, t, n:n + NCOL].rearrange("p (h d) -> p h d", d=HD)
                        link(rope(bank[job % 8][:, :], NCOL // HD, t, dst))
                        drain_inc(dve.nop(), job)
                elif kind == "xbc":
                    for j in range(2):
                        m = 2 * st[1] + j
                        job = JOB[(st, j)]
                        b = bank[job % 8]
                        dve.wait_ge(conv0_rdy, l * 12 + (m + 1))
                        for k in range(1, TAPS):
                            for i in range(2):
                                ch = 2 * m + i
                                w = P_CW + (TAPS - 1 - k) * CC + ch
                                ins = V.scalar_tensor_tensor(conv[:, m % 2, i, k:SEQ], b[:, i * SEQ:(i + 1) * SEQ - k],
                                                             prm[:, w:w + 1], conv[:, m % 2, i, k:SEQ], ALU.mult, ALU.add)
                            if k < TAPS - 1:
                                link(ins)
                            else:
                                ins.then_inc(conv_rdy, 1)
                                dve.wait_ge(conv_rdy, l * 12 + (m + 1))
                                drain_inc(dve.nop(), job)
                elif kind == "dt":
                    dve.wait_ge(dt_log, l + 1)
                    dts = dtb[:, :, :].rearrange("p t h -> p (t h)")
                    link(V.tensor_tensor(dts, tmp32[:, 0, :], tmp32[:, 1, :], ALU.add))
                    V.scalar_tensor_tensor(dta[:, :, :], dtb[:, :, :], -1.0, bc(eac[:, :], 1, TT),
                                           ALU.mult, ALU.mult).then_inc(dt_rdy, 1)
                elif kind == "acum":
                    filled(dve, l, job)
                    link(V.tensor_copy(acum[:, :, :].rearrange("p t h -> p (t h)"), b[:, 0:3 * SH]))
                    drain_inc(dve.nop(), job)
                    V.tensor_tensor(tail[:, :], acum[:, 2, :], acum[:, 0, :], ALU.subtract).then_inc(ac_rdy, 1)
                elif kind in ("kT", "kiT"):
                    filled(dve, l, job)
                    if kind == "kT":
                        dst = kT[:, 0:AKV, :]
                        src = b.rearrange("p (a t) -> p a t", a=AKV)
                    else:
                        dst, src = kT[:, AKV, :], b[:, 0:SEQ]
                    drain_inc(V.tensor_copy(dst, src), job)
                elif kind == "idx":
                    _, t, r, i = st
                    nk = (t + 1) * P
                    n = IDX.index(st)
                    drained(dve, l, job)
                    for j in range(NCOL // nk):
                        hd = 2 * (i * (NCOL // nk) + j) + r
                        src = rel[:, n % 2, j * nk:(j + 1) * nk]
                        if r == 0 and i == 0 and j == 0:
                            ins = V.tensor_scalar(isc[:, 0:nk], src, wis[:, t, hd:hd + 1], None, ALU.mult)
                        else:
                            ins = V.scalar_tensor_tensor(isc[:, 0:nk], src, wis[:, t, hd:hd + 1], isc[:, 0:nk],
                                                         ALU.mult, ALU.add)
                        link(ins)
                    dve.nop().then_inc(rel_used, 1)
                elif kind == "topk":
                    t = st[1]
                    nk = (t + 1) * P
                    s = isc[:, 0:nk]
                    link(V.tensor_tensor(isc[:, t * P:nk], isc[:, t * P:nk], caus, ALU.add))
                    for _ in range(TOPK // 8):
                        settle(dve)
                        link(V.max(top8[:, :], s))
                        settle(dve)
                        link(V.match_replace(s, top8[:, :], s, TAKEN))
                    link(V.tensor_scalar(pen[:, t, 0:nk], s, TAKEN / 2, NEG, ALU.is_gt, ALU.mult))
                    link(V.tensor_tensor(pen[:, t, t * P:nk], pen[:, t, t * P:nk], caus, ALU.add))
                elif kind == "cb":
                    filled(dve, l, job)
                    if st[1] == 0:
                        filled(dve, l, JOB[(IDX[-1], 0)])
                    drain_inc(V.tensor_tensor(cbm[:, st[1], :].rearrange("p (g t) -> p g t", g=SG),
                                              b.rearrange("p (g t) -> p g t", g=SG), bc(tri, 1, SG), ALU.mult), job)
                elif kind == "decay":
                    n = st[1]
                    t, g = SSD[n]
                    if n == 0:
                        dve.wait_ge(silu_rdy, l * 12 + 12)
                    if n >= 2:
                        filled(dve, l, JOB[(("ssd", n - 2), 0)])
                    for j in range(2):
                        job = JOB[(st, j)]
                        filled(dve, l, job)
                        for i in range(4):
                            hd = 4 * j + i
                            ins = V.tensor_scalar(mm_[:, n % 2, hd * P:(hd + 1) * P], bank[job % 8][:, i * P:(i + 1) * P],
                                                  acum[:, t, g * HG + hd:g * HG + hd + 1], 0.0, ALU.subtract, ALU.min)
                        drain_inc(ins, job)
                    drained(dve, l, job)
                    dve.nop().then_inc(seg_rdy, 1)
                    dve.wait_ge(dec_rdy, l * len(SSD) + (n + 1))
                    m3 = mm_[:, n % 2, :].rearrange("p (h t) -> p h t", h=HG)
                    V.tensor_tensor(m3, m3, bc(cbm[:, t, g * P:(g + 1) * P], 1, HG), ALU.mult).then_inc(m_rdy, 1)
                elif kind == "ssd":
                    n = st[1]
                    t, g = SSD[n]
                    y = xs[:, t, g * NCOL:(g + 1) * NCOL]
                    filled(dve, l, job)
                    dve.wait_ge(x_scaled, l * len(SSD) + (n + 1))
                    link(V.tensor_tensor(y, b, y, ALU.add))
                    drain_inc(dve.nop(), job)
                    if t == 1:
                        job = JOB[(st, 1)]
                        filled(dve, l, job)
                        link(V.tensor_tensor(ytmp.rearrange("p (h d) -> p h d", d=SP_),
                                             bank[job % 8][:, :].rearrange("p (h d) -> p h d", d=SP_),
                                             bc(eac[:, g * HG:(g + 1) * HG], 2, SP_), ALU.mult))
                        drain_inc(dve.nop(), job)
                        link(V.tensor_tensor(y, y, ytmp, ALU.add))
                elif kind == "ygate":
                    t, g = SSD[st[1]]
                    drained(dve, l, JOB[(("z", 3), 1)])
                    y = xs[:, t, g * NCOL:(g + 1) * NCOL]
                    V.tensor_tensor(y, y, zt[:, t, g * NCOL:(g + 1) * NCOL], ALU.mult).then_inc(y_rdy, 1)
                elif kind == "ynorm":
                    dve.wait_ge(ssq_rdy, (l + 1) * len(SSD))
                    rms(l * NORMS + 2, st_[:, 0:8], st_[:, 8:16], NCOL)
                    for t in range(TT):
                        for g in range(SG):
                            y = xs[:, t, g * NCOL:(g + 1) * NCOL]
                            ins = V.tensor_scalar(y, y, st_[:, 8 + t * SG + g:9 + t * SG + g], None, ALU.mult)
                    ins.then_inc(yn_rdy, 1)
                elif kind == "score":
                    n = st[1]
                    t, r, i = ATT[n]
                    nk = (t + 1) * P
                    nh = NCOL // nk
                    filled(dve, l, job)
                    if n == 0:
                        filled(dve, l, JOB[(("ssd", len(SSD) - 1), 1)])
                    if n >= 2:
                        filled(dve, l, JOB[(("probT", n - 2), 0)])
                    s3 = sco[:, n % 2, :].rearrange("p (h s) -> p h s", h=nh)
                    link(V.tensor_tensor(s3, b.rearrange("p (h s) -> p h s", h=nh), bc(pen[:, t, 0:nk], 1, nh), ALU.add))
                    drain_inc(dve.nop(), job)
                    link(V.tensor_reduce(mx[:, n % 4, 0:nh], s3, AX_X, ALU.max))
                    V.tensor_scalar(nmx[:, n % 4, 0:nh], mx[:, n % 4, 0:nh], -(HD ** -0.5), None,
                                    ALU.mult).then_inc(sc_rdy, 1)
                elif kind == "xscore":
                    n = st[1]
                    filled(dve, l, job)
                    if n >= 2:
                        dve.wait_ge(pr_rdy, l * (len(ATT) + 4) + (len(ATT) + n - 1))
                    link(V.tensor_reduce(mx[:, n % 4, 0:2], b.rearrange("p (h s) -> p h s", h=2), AX_X, ALU.max))
                    V.tensor_scalar(nmx[:, n % 4, 0:2], mx[:, n % 4, 0:2], -(XD ** -0.5), None,
                                    ALU.mult).then_inc(sc_rdy, 1)
                elif kind in ("pv", "xpv"):
                    n = st[1]
                    if kind == "pv":
                        t, r, i = ATT[n]
                        nh, w = 4 // (t + 1), HD
                        dst = qbuf[:, t, :].rearrange("p (a r d) -> p a r d", r=2, d=HD)[:, i * nh:(i + 1) * nh, r, :]
                    else:
                        t, pr = divmod(n, 2)
                        nh, w = 2, XD
                        dst = qbuf[:, t, pr * NCOL:(pr + 1) * NCOL].rearrange("p (a d) -> p a d", a=2)
                    filled(dve, l, job)
                    link(V.reciprocal(rs[:, n % 4, 0:nh], sm[:, n % 4, 0:nh]))
                    drain_inc(V.tensor_tensor(dst, b[:, 0:nh * w].rearrange("p (h d) -> p h d", h=nh),
                                              bc(rs[:, n % 4, 0:nh], 2, w), ALU.mult), job)
                elif kind == "ssdo":
                    n = st[1] * NCOL
                    for t in range(TT):
                        job = JOB[(st, t)]
                        filled(dve, l, job)
                        drained(dve, l, JOB[(("gate", 0, 1), 1)])
                        drain_inc(V.tensor_tensor(xn[:, t, n:n + NCOL], bank[job % 8][:, :], gate[:, t, n:n + NCOL], ALU.mult), job)
                elif kind == "atto":
                    n = st[1] * NCOL
                    for t in range(TT):
                        job = JOB[(st, t)]
                        filled(dve, l, job)
                        drained(dve, l, JOB[(("gate", 1, 1), 1)])
                        g_ = gate[:, t, n:n + NCOL]
                        link(V.tensor_tensor(g_, bank[job % 8][:, :], g_, ALU.mult))
                        drain_inc(V.tensor_tensor(xn[:, t, n:n + NCOL], xn[:, t, n:n + NCOL], g_, ALU.add), job)
                elif kind in ("wo", "co"):
                    n = st[1] * NCOL
                    if kind == "wo" and st[1] == 0:
                        dve.wait_ge(mem_in, l * 16 + 16)
                        normalise(l * NORMS + 3, memx, memx, cols(big, 2048, TT, D)).then_inc(mem_rdy, 1)
                    for t in range(TT):
                        job = JOB[(st, t)]
                        filled(dve, l, job)
                        drain_inc(V.tensor_tensor(h[:, t, n:n + NCOL], bank[job % 8][:, :], h[:, t, n:n + NCOL], ALU.add), job)
                elif kind == "router":
                    route(l, st, job, b)
                elif kind == "rank":
                    rank(l, job, b)

            def route(l, st, job, b):
                lg = cols(rt, R_LG, TT, G + G * E)
                filled(dve, l, job)
                link(V.tensor_tensor(lg, b.rearrange("p (a n) -> p a n", n=64)[:, 0:TT, 0:G + G * E],
                                     bc(prm[:, P_BR:P_BR + G + G * E], 1, TT), ALU.add))
                drain_inc(dve.nop(), job)
                dve.nop().then_inc(prm_used, 1)
                gm, oh = cols(rt, R_GM, TT), cols(rt, R_OH, TT, G)
                eq4 = cols(rt, R_EQ, TT, G)
                gd = cols(rt, R_GD, TT, G)
                prio = cst[:, C_PRIO:C_PRIO + E]
                first_max(lg[:, :, 0:G], prio[:, 0:G], gm, eq4, oh, G)
                V.tensor_tensor(gd, lg[:, :, 0:G], bc(gm, 2, G), ALU.subtract).then_inc(rt_in, 1)
                lge = lg[:, :, G:G + G * E].rearrange("p t (g e) -> p t g e", g=G)
                pick = rt[:, R_PK:R_PK + TT * G * E].rearrange("p (t g e) -> p t g e", t=TT, g=G)
                for t in range(TT):
                    ins = V.tensor_tensor(pick[:, t], lge[:, t], bc(oh[:, t, :], 2, E), ALU.mult)
                link(ins)
                ein = cols(rt, R_EI, TT, E)
                for t in range(TT):
                    ins = V.tensor_reduce(ein[:, t, :], pick[:, t].rearrange("p g e -> p e g"), AX_X, ALU.add)
                link(ins)
                v1, v2 = cols(rt, R_V1, TT), cols(rt, R_V2, TT)
                oh1, oh2 = cols(rt, R_O1, TT, E), cols(rt, R_O2, TT, E)
                eq8 = cols(rt, R_EQ, TT, E)
                first_max(ein, prio, v1, eq8, oh1, E)
                link(V.scalar_tensor_tensor(ein, oh1, TAKEN, ein, ALU.mult, ALU.add))
                first_max(ein, prio, v2, eq8, oh2, E)
                V.tensor_tensor(cols(rt, R_DL, TT), v2, v1, ALU.subtract).then_inc(r2_in, 1)
                link(V.tensor_tensor(eq8, oh1, oh2, ALU.add))
                us = rt[:, R_US:R_US + TT * G * E].rearrange("p (t g e) -> p t g e", t=TT, g=G)
                for t in range(TT):
                    ins = V.tensor_tensor(us[:, t], bc(oh[:, t, :], 2, E), bc(eq8[:, t, :], 1, G), ALU.mult)
                ins.then_inc(oh_rdy, 1)
                dve.wait_ge(oh_rdy, l + 1)
                dve.wait_ge(rt_exp, l + 1)
                gs = cols(rt, R_GS, TT)
                link(V.tensor_reduce(gs, cols(rt, R_GE, TT, G), AX_X, ALU.add))
                dve.wait_ge(r2_exp, l + 1)
                tw, den = cols(rt, R_TW, TT), cols(rt, R_DN, TT)
                link(V.scalar_tensor_tensor(den, tw, 1.0, gs, ALU.add, ALU.mult))
                link(V.reciprocal(den, den))
                link(V.tensor_tensor(tw, tw, den, ALU.mult))
                wi_ = cols(rt, R_WI, TT, E)
                V.tensor_tensor(oh2, oh2, bc(tw, 2, E), ALU.mult)
                link(V.tensor_tensor(wi_, oh1, bc(den, 2, E), ALU.mult))
                link(V.tensor_tensor(wi_, wi_, oh2, ALU.add))

            def rank(l, job, b):
                filled(dve, l, job)
                us, key = cols(rt, R_US, TT * G * E), cols(rt, R_KY, TT * G * E)
                w = G * E
                link(V.tensor_scalar(key, us, -16.0 * SEQ, 16.0 * SEQ, ALU.mult, ALU.add))
                V.tensor_tensor(key, b[:, 0:TT * w], key, ALU.add)
                cnt, nr, ps, tg = cols(rt, R_CN, G), cols(rt, R_NR, G), cols(rt, R_PS, G), cols(rt, R_TG, G)
                link(V.tensor_reduce(cnt, b[:, 2 * w:3 * w].rearrange("p (g e) -> p g e", g=G), AX_X, ALU.max))
                drain_inc(dve.nop(), job)
                full = cols(rt, R_CR, G, ROUNDS)
                link(V.tensor_tensor(full, bc(cnt, 2, ROUNDS), bc(cst[:, C_FULL:C_FULL + ROUNDS], 1, G), ALU.is_gt))
                link(V.tensor_reduce(nr, full, AX_X, ALU.add))
                link(V.tensor_scalar(nr, nr, 1.0, None, ALU.max))
                link(V.tensor_scalar(ps, nr, -1.0, None, ALU.add))
                link(V.tensor_scalar(tg[:, 0:1], ub[:, :], G - 1.0, None, ALU.add))
                for g in range(1, G):
                    link(V.tensor_tensor(tg[:, g:g + 1], tg[:, g - 1:g], ps[:, g - 1:g], ALU.add))
                V.scalar_tensor_tensor(ub[:, :], ps[:, G - 1:G], 1.0, tg[:, G - 1:G], ALU.add, ALU.add)
                link(V.tensor_reduce(cnt[:, 0:1], ps, AX_X, ALU.add))
                V.tensor_copy(itab[0:1, 0:G], nr[0:1, :])
                V.tensor_copy(itab[0:1, G:2 * G], tg[0:1, :])
                V.tensor_copy(itab[0:1, 8:9], ub[0:1, :])
                V.tensor_copy(itab[0:1, 9:10], cnt[0:1, 0:1]).then_inc(keys_rdy, 1)
                dve.wait_ge(keys_rdy, l + 2)

            def expert_pass(u, g):
                kt = cols(rt, R_KT, TT, E)
                keys = cols(rt, R_KY, TT, G * E)[:, :, bass.ds(g * E, E)]
                V.tensor_copy(kt, keys).then_inc(kt_rdy, 1)
                dve.wait_ge(kt_rdy, u + 1)
                V.tensor_scalar(keys, keys, -float(S), None, ALU.add)
                within = cols(rt, R_WI, TT, E)

                def slots(m):
                    return m.rearrange("p (e s) -> p e s", e=E)

                for k in range(TT):
                    ins = V.tensor_tensor(slots(sel[:, k, :]), bc(iota[:, 0:S], 1, E), bc(kt[:, k, :], 2, S), ALU.is_equal)
                ins.then_inc(sel_rdy, 1)
                dve.wait_ge(sel_rdy, u * 2 + 1)
                for k in range(TT):
                    ins = V.tensor_tensor(slots(selw[:, k, :]), slots(sel[:, k, :]), bc(within[:, k, :], 2, S), ALU.mult)
                ins.then_inc(sel_rdy, 1)
                for i in (0, 2):
                    dve.wait_ge(gat_s, u * 5 + (i + 1))
                    for c in (2 * i, 2 * i + 1):
                        V.tensor_scalar(xg[:, c, :], bank[GATHER[i]][:, (c % 2) * E * S:(c % 2 + 1) * E * S],
                                        prm_ffn[:, c:c + 1], None, ALU.mult)
                dve.wait_ge(gat_s, u * 5 + 5)
                V.tensor_copy(selT, bank[2][:, :].rearrange("p (b s) -> p b s", b=NB)).then_inc(xg_rdy, 1)
                for b in range(NB):
                    dve.wait_ge(sil_s, u * NB + (b + 1))
                    V.tensor_tensor(hid[:, b, :], bank[b][:, F:2 * F], sil[:, b, :], ALU.mult).then_inc(hid_s, 1)
                    for k in range(TT):
                        for n in range(2):
                            dve.wait_ge(sct_s, u * (4 * NB) + (4 * b + 2 * k + n + 1))
                            if b:
                                dve.wait_ge(add_s, u * (4 * NB) + (2 * k + n + 1))
                            hh = h[:, k, n * NCOL:(n + 1) * NCOL]
                            V.tensor_tensor(hh, bank[6 + n][:, :], hh, ALU.add).then_inc(add_s, 1)
                dve.wait_ge(add_s, u * (4 * NB) + 4 * NB)

            V.memset(ub[:, :], 0.0)
            V.memset(itab[:, :], 0).then_inc(keys_rdy, 1)
            dve.wait_ge(keys_rdy, 1)
            dve.wait_ge(cst_in, 32)
            with dve.Fori(0, DEPTH) as l:
                before = passes_before(dve, VE, l)
                steps.at(l * V_LAYER)
                dve.wait_ge(prm_in, l * 16 + 16)
                for st in ORDER:
                    if st[0] == "router":
                        link(V.tensor_copy(prm_ffn[:, :], prm[:, P_NF:P_NF + KC]))
                    stage(l, st)
                assert steps.n == V_LAYER, f"V_LAYER = {steps.n}"
                settle(dve)
                with dve.Fori(0, G) as g:
                    expert_pass(before + g, g)
                more_passes(dve, VE, l, expert_pass)
            steps.at(DEPTH * V_LAYER)
            normalise(DEPTH * NORMS + 1, h, xn, xn).then_inc(norm_rdy, 1)
            dve.wait_ge(norm_rdy, DEPTH * 3 + 1)
            dve.wait_ge(fin_in, 16)
            for t in range(TT):
                V.tensor_tensor(xn[:, t, :], xn[:, t, :], gate[:, 0, :], ALU.mult).then_inc(fin_s, 1)


_NAMES = ["x", "mem", "w_in", "w_ssd_o", "w_attn_o", "w_out", "w_cq", "w_ckv", "w_co", "w_group", "w_router",
          "w_gate_e", "w_up_e", "w_down_e"]


def constants():
    import numpy as np
    i = np.arange(P)
    c = np.zeros((P, C_W), np.float32)
    c[:, C_ID:C_ID + P] = np.eye(P)
    c[:, C_TRI:C_TRI + P] = i[:, None] <= i[None, :]
    c[:, C_TRIS:C_TRIS + P] = i[:, None] < i[None, :]
    c[:, C_ONE:C_ONE + P] = 1.0
    c[:, C_IOTA:C_IOTA + P] = i[None, :]
    c[:, C_CAUS:C_CAUS + P] = np.where(i[None, :] <= i[:, None], 0.0, NEG)
    inv = (1.0 / (np.float32(10000.0) ** (np.arange(0, HD, 2, dtype=np.float32) / np.float32(HD)))).astype(np.float32)
    for t in range(TT):
        ang = (t * P + i).astype(np.float32)[:, None] * inv[None, :]
        c[:, C_COS + t * HD:C_COS + (t + 1) * HD] = np.tile(np.cos(ang), (1, 2))
        c[:, C_SIN + t * HD:C_SIN + (t + 1) * HD] = np.tile(np.sin(ang), (1, 2))
    c[:, C_PRIO:C_PRIO + E] = E - np.arange(E)
    c[:, C_FULL:C_FULL + ROUNDS] = np.arange(ROUNDS) * S
    c[:, C_MH:C_MH + E] = -0.5
    return c


def small_params(a):
    import numpy as np

    def by_block(v):
        return np.moveaxis(v.reshape(DEPTH, -1, P), 2, 1)

    def repeated(v):
        return np.broadcast_to(v[:, None, :], (DEPTH, P, v.shape[-1]))

    parts = [by_block(a[n].reshape(DEPTH, -1)) for n in
             ("conv_w", "conv_b", "norm_mix", "norm_xattn", "norm_mem", "norm_ffn", "ssd_norm")]
    parts += [repeated(a[n]) for n in ("dt_bias", "a_log", "d_skip", "b_group", "b_router")]
    return np.ascontiguousarray(np.concatenate(parts, axis=2))


def kernel(**inputs):
    import numpy as np
    import concourse.bacc as _bacc
    from concourse.bass_utils import run_bass_kernel_spmd as _run

    a = {k: np.asarray(v) for k, v in inputs.items()}
    arrays = {n: np.ascontiguousarray(a[n]) for n in _NAMES}
    arrays["x"] = arrays["x"].reshape(SEQ, D)
    arrays["mem"] = arrays["mem"].reshape(SEQ, D)
    arrays["params"] = small_params(a)
    arrays["consts"] = constants()
    arrays["gain_final"] = np.ascontiguousarray(np.broadcast_to(a["norm_final"][None, :], (P, D)))
    nc = _bacc.Bacc("TRN2", target_bir_lowering=False, num_devices=1)
    args = [nc.dram_tensor(f"in_{n}", v.shape, F32, kind="ExternalInput").ap() for n, v in arrays.items()]
    out = nc.dram_tensor("out_0", (SEQ, D), F32, kind="ExternalOutput").ap()
    trunk(nc, *args, out)
    r = _run(nc, [{f"in_{n}": v for n, v in arrays.items()}], core_ids=[0])
    return r.results[0]["out_0"].reshape(1, SEQ, D)
```

```python
import math
from contextlib import ExitStack

import concourse.bass as bass
from concourse import mybir

F32 = mybir.dt.float32
I32 = mybir.dt.int32
ALU = mybir.AluOpType
ACT = mybir.ActivationFunctionType
AX_X = mybir.AxisListType.X

P = 128
NEG = -1.0e30
TAKEN = -3.0e38
EPS = 1e-6

DEPTH, SEQ, D = 2, 256, 1024
TT = SEQ // P
KC = D // P
DI = 2 * D
SH, SP_, SG, SN = 32, 64, 4, 128
HG = SH // SG
CH = DI + 2 * SG * SN
CC = CH // P
TAPS = 4
AH, AKV, HD = 16, 2, 64
IH = 8
TOPK = SEQ // 4
XH, XD = 4, 256
G, E, F = 4, 8, 256
NCOL = 512
IDX_SCALE = HD ** -0.5 * IH ** -0.5

Z0 = 0
XBC0 = Z0 + DI
DT0 = XBC0 + CH
Q0 = DT0 + SH
K0 = Q0 + AH * HD
QI0 = K0 + 2 * AKV * HD
KI0 = QI0 + IH * HD
GS0 = KI0 + HD + IH
GA0 = GS0 + D

C_ID, C_TRI, C_TRIS, C_ONE, C_IOTA, C_CAUS, C_COS, C_SIN, C_PRIO, C_FULL, C_MH = (
    0, 128, 256, 384, 512, 640, 768, 896, 1024, 1032, 1040)
C_W = 1048
P_CW, P_CB, P_NM, P_NX, P_NE, P_NF, P_SN, P_DTB, P_AL, P_DS, P_BR, P_NFR = (
    0, 96, 120, 128, 136, 144, 152, 168, 200, 232, 264, 300)
P_W = 308

(R_LG, R_GM, R_OH, R_EQ, R_GD, R_GE, R_T2, R_PK, R_EI, R_V1, R_V2, R_O1, R_O2, R_DL, R_TW, R_GS, R_DN, R_WI,
 R_US, R_KY, R_CN, R_CR, R_NR, R_PS, R_TG, R_KT, R_W) = (
    0, 72, 74, 82, 98, 106, 114, 116, 180, 196, 198, 200, 216, 232, 234, 236, 238, 240,
    256, 320, 384, 388, 420, 424, 428, 432, 448)

ATT = [(0, r, i) for r in range(2) for i in range(2)] + [(1, r, i) for r in range(2) for i in range(4)]
SSD = [(t, g) for t in range(TT) for g in range(SG)]


def make_order():
    o = [("norm", 0)] + [("hT", 0, i) for i in range(4)]
    o += [("small",), ("kv",), ("dt",), ("qi",), ("acum",), ("kT",), ("kiT",), ("xbc", 0), ("qiT", 0), ("qiT", 1), ("xbc", 1)]
    o += [("idx", 0, r, 0) for r in range(2)] + [("topk", 0), ("xbc", 2)]
    o += [("idx", 1, r, i) for r in range(2) for i in range(2)] + [("topk", 1), ("xbc", 3), ("xbc", 4), ("xbc", 5)]
    o += [("q", 0)] + [("xT", i) for i in range(4)] + [("bT",), ("q", 1)] + [("xT", i) for i in range(4, 8)]
    o += [("cb", 0), ("cb", 1)]
    for n, (t, g) in enumerate(SSD):
        o += [("decay", n)]
        if n:
            o += [("ssd", n - 1)]
        o += [("part", ("z", n // 2), n % 2)]
        if n in (1, 3):
            o += [("qT", n - 1), ("qT", n)]
    o += [("ssd", len(SSD) - 1)]
    for n in range(len(ATT) + 2):
        if n < len(ATT):
            o += [("score", n)]
        if 1 <= n <= len(ATT):
            o += [("probT", n - 1)]
        if n >= 2:
            o += [("pv", n - 2)]
        if n in (0, 3, 6, 9):
            o += [("part", ("gate", 0, n // 6), (n // 3) % 2)]
        if n < len(SSD):
            o += [("ygate", n)]
        if n == len(SSD):
            o += [("ynorm",)]
        if 9 <= n < 13:
            o += [("yT", 2 * n - 18), ("yT", 2 * n - 17)]
    o += [("ssdo", 0), ("ssdo", 1), ("gate", 1, 0), ("gate", 1, 1)]
    o += [("aT", i) for i in range(4)] + [("atto", 0), ("atto", 1)]
    o += [("mgT", i) for i in range(4)] + [("wo", 0), ("wo", 1)]
    o += [("memT", i) for i in range(4)] + [("ck", 0), ("ck", 1), ("cv", 0), ("cv", 1)]
    o += [("norm", 1)] + [("hT", 1, i) for i in range(4)] + [("cq", 0), ("cq", 1)]
    for n in range(6):
        if n < 4:
            o += [("xscore", n)]
        if 1 <= n <= 4:
            o += [("xprobT", n - 1)]
        if n >= 2:
            o += [("xpv", n - 2)]
    o += [("xoT", i) for i in range(4)] + [("co", 0), ("co", 1)]
    o += [("norm", 2)] + [("hT", 2, i) for i in range(4)] + [("router",), ("rank",)]
    return o


ORDER = make_order()
IDX = [st for st in ORDER if st[0] == "idx"]

JOBS_OF = {
    "hT": (1, "both"), "small": (2, "dve"), "kv": (2, "dve"), "qi": (2, "dve"), "xbc": (2, "dve"),
    "acum": (1, "dve"), "kT": (1, "dve"), "kiT": (1, "dve"), "qiT": (1, "act"), "idx": (1, "act"), "q": (2, "dve"),
    "xT": (1, "act"), "bT": (1, "act"), "cb": (1, "dve"), "qT": (1, "act"), "decay": (2, "dve"),
    "z": (2, "act"), "score": (1, "dve"), "probT": (1, "act"), "pv": (1, "dve"), "gate": (2, "act"),
    "yT": (1, "both"), "ssdo": (2, "dve"), "aT": (1, "both"), "atto": (2, "dve"), "mgT": (1, "both"),
    "wo": (2, "dve"), "memT": (1, "both"), "ck": (2, "act"), "cv": (2, "act"), "cq": (2, "act"),
    "xscore": (1, "act"), "xprobT": (1, "act"), "xpv": (1, "dve"), "xoT": (1, "both"), "co": (2, "dve"),
    "router": (1, "dve"), "rank": (1, "dve"),
}


def ssd_jobs(n):
    return ["dve", "act" if SSD[n][0] == 0 else "dve"]


def make_jobs():
    jobs = []
    for st in ORDER:
        if st[0] == "part":
            jobs += [(st[1], st[2], JOBS_OF[st[1][0]][1])]
        elif st[0] == "ssd":
            jobs += [(st, i, own) for i, own in enumerate(ssd_jobs(st[1]))]
        elif st[0] in JOBS_OF:
            n, own = JOBS_OF[st[0]]
            if own == "both":
                own = ("dve", "act")[st[-1] % 2]
            jobs += [(st, i, own) for i in range(n)]
    return jobs


JOBS = make_jobs()
JOB = {(st, i): k for k, (st, i, _) in enumerate(JOBS)}
OWNER = [own for _, _, own in JOBS]
RANK = [sum(o == OWNER[k] for o in OWNER[:k + 1]) for k in range(len(JOBS))]
DRAINS = {own: OWNER.count(own) for own in ("dve", "act")}
NJ = len(JOBS)

CHUNKED = {"small": 1, "kv": 1, "qi": 1, "xbc": 1, "q": 1, "z": 1, "gate": 1, "ssdo": 2, "atto": 1, "wo": 1,
           "ck": 1, "cv": 1, "cq": 1, "co": 1}
WHOLE = [st[1] if st[0] == "part" else st for st in ORDER if st[0] != "part" or st[2] == 0]
CHUNKS = [(st, i) for st in WHOLE if st[0] in CHUNKED for i in range(CHUNKED[st[0]])]
CHUNK = {c: k for k, c in enumerate(CHUNKS)}
W_SLOTS = 4
FIRST_BLOCK = 2
FIRST_PAIR = 2
NORMS = 5
NCH = len(CHUNKS)
SLOT = [(c - NCH) % W_SLOTS for c in range(NCH)]
NTH = [SLOT[:c].count(SLOT[c]) for c in range(NCH)]

S = 32
BE = 4
NB = E // BE
ROUNDS = SEQ // S
GATHER = (6, 7, 4, 5)

V_LAYER = 215
A_LAYER = 2


def last_job(c):
    (st, i) = CHUNKS[c]
    return JOB[(st, 1 if JOBS_OF[st[0]][0] == 2 else 0)]


def bc(ap, axis, n):
    ap = ap.unsqueeze(axis)
    shape = list(ap.shape)
    shape[axis] = n
    return ap.to_broadcast(shape)


class Steps:

    def __init__(self, eng, sem):
        self.eng, self.sem, self.base, self.n = eng, sem, 0, 0

    def at(self, base):
        self.base, self.n = base, 0

    def link(self, ins):
        self.n += 1
        ins.then_inc(self.sem, 1)
        self.eng.wait_ge(self.sem, self.base + self.n)


def trunk(nc, x, mem, w_in, w_ssd_o, w_attn_o, w_out, w_cq, w_ckv, w_co, w_group, w_router,
          w_gate, w_up, w_down, params, consts, gain_final, out):
    with ExitStack() as ctx:
        def sb(name, shape, dt=F32):
            return ctx.enter_context(nc.sbuf_tensor(name, shape, dt))

        def sem(name):
            return ctx.enter_context(nc.semaphore(name))

        wring = sb("wring", [P, W_SLOTS, KC, NCOL])
        h = sb("h", [P, TT, D])
        xn = sb("xn", [P, TT, D])
        hT = sb("hT", [P, KC, SEQ])
        big = sb("big", [P, CC * SEQ])
        xs = sb("xs", [P, TT, DI])
        ga = sb("ga", [P, 4096])
        gate = ga[:, 0:TT * D].rearrange("p (t d) -> p t d", t=TT)
        att = ga[:, TT * D:2 * TT * D]
        qq = sb("qq", [P, 2, TT * D])
        qbuf = qq[:, 0, :].rearrange("p (t d) -> p t d", t=TT)
        qT = qq[:, 1, :].rearrange("p (c s) -> p c s", c=KC)
        scr = sb("scr", [P, 4096])
        kT = sb("kT", [P, AKV + 1, SEQ])
        qiT = sb("qiT", [P, IH // 2, SEQ])
        ktok = sb("ktok", [P, TT, AKV + 1, 2, HD])
        vtok = sb("vtok", [P, TT, AKV * HD])
        pen = sb("pen", [P, TT, SEQ])
        btok = sb("btok", [P, SG * SN])
        cst = sb("cst", [P, C_W])
        prm = sb("prm", [P, P_W])
        dtb = sb("dtb", [P, TT, SH])
        dta = sb("dta", [P, TT, SH])
        acum = sb("acum", [P, 3, SH])
        eac = sb("eac", [P, SH])
        tail = sb("tail", [P, SH])
        tmp32 = sb("tmp32", [P, 2, TT * SH])
        wis = sb("wis", [P, TT, IH])
        st_ = sb("sums", [P, 24])
        mx = sb("mx", [P, 4, 4])
        nmx = sb("nmx", [P, 4, 4])
        sm = sb("sm", [P, 4, 4])
        rs = sb("rs", [P, 4, 4])
        prm_ffn = sb("prm_ffn", [P, KC])
        top8 = sb("top8", [P, 8])
        rt = sb("rt", [P, R_W])
        itab = sb("itab", [1, 12], I32)
        ub = sb("ub", [P, 1])

        ident = cst[:, C_ID:C_ID + P]
        tri = cst[:, C_TRI:C_TRI + P]
        tris = cst[:, C_TRIS:C_TRIS + P]
        ones = cst[:, C_ONE:C_ONE + P]
        iota = cst[:, C_IOTA:C_IOTA + P]
        caus = cst[:, C_CAUS:C_CAUS + P]

        def cols(buf, a, *shape):
            v = buf[:, a:a + math.prod(shape)]
            names = "abc"[:len(shape)]
            if len(shape) == 1:
                return v
            return v.rearrange(f"p ({' '.join(names)}) -> p {' '.join(names)}",
                               **{n: s for n, s in zip(names, shape)})

        xbcT = cols(big, 0, CC, SEQ)
        zt = cols(big, 0, TT, DI)
        yT = cols(big, 0, 2 * KC, SEQ)
        memx = cols(big, 0, TT, D)
        memT = cols(big, 2048, KC, SEQ)
        xg = cols(big, 0, KC, E * S)
        sel = cols(big, 2048, TT, E * S)
        selw = cols(big, 2560, TT, E * S)
        selT = cols(big, 3072, NB, SEQ)
        sil = cols(big, 3584, NB, F)
        hid = cols(big, 4096, NB, F)
        hidT = cols(big, 4608, NB, F)
        yg = cols(big, 5120, D)
        ropeA = cols(scr, 0, NCOL)
        ropeB = cols(scr, 512, NCOL)
        conv = cols(scr, 1024, 2, 2, SEQ)
        rel = cols(scr, 2048, 2, NCOL)
        isc = cols(scr, 3072, SEQ)
        ex32 = cols(scr, 3328, TT * SH)
        mm_ = cols(scr, 0, 2, HG * P)
        state = cols(scr, 2048, SG, NCOL)
        ckT = cols(scr, 0, KC, SEQ)
        cv = cols(scr, 2048, TT, D)
        xdt = cols(att, 0, 2, NCOL)
        xdtt = cols(att, 1024, NCOL)
        ytmp = cols(att, 1536, NCOL)
        sco = cols(att, 0, 2, NCOL)
        pT = cols(att, 1024, 2, NCOL)
        cbm = cols(qiT[:, :, :].rearrange("p a b -> p (a b)"), 0, TT, SG * P)
        up_part = [wring[:, i, :, :].rearrange("p (w j) n -> p w j n", w=2) for i in range(W_SLOTS)]
        xn_eighth = xn[:, :, :].rearrange("p t (q c) -> p t c q", c=KC)
        dquad = [xs[:, :, :].rearrange("p t (a n) -> p (t a) n", a=2).rearrange("p j (k n) -> p j k n", n=NCOL),
                 scr[:, :].rearrange("p (j k n) -> p j k n", j=BE, n=NCOL),
                 qq[:, :, :].rearrange("p t (a n) -> p (t a) n", a=2).rearrange("p j (k n) -> p j k n", n=NCOL),
                 ga[:, :].rearrange("p (j k n) -> p j k n", j=BE, n=NCOL)]
        fgain = hT[:, 0:D // SEQ, :].rearrange("p c t -> p (c t)")
        rw = btok[:, :].rearrange("p (k n) -> p k n", k=KC)[:, :, 0:G + G * E]

        bank = [ctx.enter_context(nc.psum_tensor(f"bank{b}", [P, NCOL], F32)) for b in range(8)]

        x_in = sem("x_in")
        cst_in = sem("cst_in")
        prm_in = sem("prm_in")
        prm_used = sem("prm_used")
        w_in_sem = [sem(f"chunk_in{s}") for s in range(W_SLOTS)]
        up_part_in = [sem(f"gate_up_in{i}") for i in range(W_SLOTS)]
        d_in_sem = [sem(f"down_in{i}") for i in range(2 * NB)]
        mem_in = sem("mem_in")
        router_in = sem("router_in")
        fin_in = sem("fin_in")
        filled_s = sem("bank_filled")
        drained_s = {"dve": sem("drained_by_dve"), "act": sem("drained_by_act")}
        v_step = sem("dve_step")
        a_step = sem("act_step")
        p_step = sem("pool_step")
        h_rdy = sem("h_ready")
        sq_rdy = sem("h_squares_by_act")
        norm_rdy = sem("xn_ready")
        norm1_rdy = sem("xn_by_act")
        ka_rdy = sem("keys_roped")
        dup_rdy = sem("keys_doubled")
        conv0_rdy = sem("conv_started")
        conv_rdy = sem("conv_summed")
        silu_rdy = sem("conv_silu")
        dt_abs = sem("dt_abs")
        dt_log = sem("dt_log")
        dt_rdy = sem("dt_ready")
        ac_rdy = sem("acum_ready")
        eac_rdy = sem("exp_acum_ready")
        rel_used = sem("rel_used")
        x_scaled = sem("x_scaled")
        seg_rdy = sem("segments_ready")
        dec_rdy = sem("decay_ready")
        m_rdy = sem("decayed_scores_ready")
        y_rdy = sem("y_gated")
        yn_rdy = sem("y_normed")
        sc_rdy = sem("score_max_ready")
        pr_rdy = sem("probs_ready")
        mem_rdy = sem("mem_normed")
        var_rdy = sem("mean_square_ready")
        rstd_rdy = sem("rstd_ready")
        ssq_rdy = sem("y_squares_ready")
        rt_in = sem("group_logits_ready")
        rt_exp = sem("group_exp_ready")
        r2_in = sem("top2_diff_ready")
        r2_exp = sem("top2_exp_ready")
        oh_rdy = sem("onehot_ready")
        keys_rdy = sem("slots_ready")
        kt_rdy = sem("pass_keys_ready")
        sel_rdy = sem("selection_ready")
        gat_s = sem("gathered")
        xgv_rdy = sem("gathered_x_by_dve")
        xga_rdy = sem("gathered_x_by_act")
        st_rdy = sem("slot_weights_transposed")
        gu_s = sem("gate_up_part_used")
        sil_s = sem("silu_done")
        hid_s = sem("hidden_ready")
        hT_s = sem("hidden_transposed")
        hTc_s = sem("hidden_copied")
        dn_s = sem("down_quad_used")
        yg_s = sem("expert_sum_ready")
        sct_s = sem("scattered")
        add_s = sem("h_added")
        fin_s = sem("final_ready")
        out_s = sem("stored")

        def filled(eng, l, job):
            eng.wait_ge(filled_s, l * NJ + job + 1)

        def drained(eng, l, job):
            eng.wait_ge(drained_s[OWNER[job]], l * DRAINS[OWNER[job]] + RANK[job])

        def all_drained(eng, l, jobs):
            for own in ("dve", "act"):
                mine = [j for j in jobs if OWNER[j] == own]
                if mine:
                    drained(eng, l, max(mine))

        def settle(eng):
            eng.nop(nofuse=True)

        def drain_inc(ins, job):
            ins.then_inc(drained_s[OWNER[job]], 1)

        PE, AC, VE, SP = (mybir.EngineType.PE, mybir.EngineType.Activation, mybir.EngineType.DVE, mybir.EngineType.SP)

        def number(engine, at, most):
            return nc.values_load(itab[0:1, at], engines=[engine], min_val=0, max_val=most)

        def passes_before(eng, engine, l):
            eng.wait_ge(keys_rdy, l + 1)
            settle(eng)
            return number(engine, slice(8, 9), DEPTH * (G + ROUNDS))

        def more_passes(eng, engine, l, run):
            eng.wait_ge(keys_rdy, l + 2)
            settle(eng)
            more = number(engine, slice(9, 10), ROUNDS)
            with eng.If(more > 0):
                with eng.Fori(0, G) as g:
                    rounds = number(engine, bass.ds(g, 1), ROUNDS)
                    first = number(engine, bass.ds(g + G, 1), DEPTH * (G + ROUNDS))
                    with eng.If(rounds > 1):
                        with eng.Fori(1, rounds) as r_:
                            run(first + r_, g)

        SHARED = ("hT", "yT", "aT", "mgT", "memT", "xoT")
        TRANSPOSED = {"hT": hT, "mgT": hT, "memT": memT, "yT": yT, "aT": qT, "xoT": qT, "qT": qT, "qiT": qiT}

        def gain_of(st):
            if st[0] == "hT":
                return (P_NM, P_NX, P_NF)[st[1]]
            return {"memT": P_NE, "yT": P_SN}.get(st[0])

        block = ctx.enter_context(nc.Block())

        @block.sync
        def _(sp):
            sp.dma_start(h[:, :, :], x.rearrange("(t p) d -> p t d", p=P)).then_inc(x_in, 16)
            sp.dma_start(cst[:, :], consts).then_inc(cst_in, 16)
            sp.nop().then_inc(prm_used, 1)
            sp.nop().then_inc(gu_s, W_SLOTS)
            sp.nop().then_inc(dn_s, 2 * NB)

            def rows(w, a, b):
                return w.rearrange("(c p) n -> p c n", p=P)[:, :, a:b]

            def chunk(l, c, before):
                st, part = CHUNKS[c]
                kind = st[0]
                if c < W_SLOTS:
                    sp.wait_ge(gu_s, before * (W_SLOTS * NB) + (SLOT[c] + 1))
                else:
                    filled(sp, l, last_job(c - W_SLOTS))
                settle(sp)
                slot = wring[:, SLOT[c], :, :]

                def load(dst, src):
                    sp.dma_start(dst, src).then_inc(w_in_sem[SLOT[c]], 16)

                def halves(src):
                    load(slot[:, 0:KC // 2, :], src[:, 0:KC // 2, :])
                    load(slot[:, KC // 2:KC, :], src[:, KC // 2:KC, :])

                if kind == "small":
                    load(slot[:, :, 0:SH], rows(w_in[l], DT0, DT0 + SH))
                    load(slot[:, :, SH:SH + HD + IH], rows(w_in[l], KI0, GS0))
                elif kind == "kv":
                    load(slot[:, 0:4, 0:256], rows(w_in[l], K0, QI0)[:, 0:4, :])
                    load(slot[:, 4:8, 0:256], rows(w_in[l], K0, QI0)[:, 4:8, :])
                elif kind == "ssdo":
                    n = st[1] * NCOL
                    halves(rows(w_ssd_o[l][part * D:(part + 1) * D, :], n, n + NCOL))
                else:
                    w, a = {
                        "qi": (w_in, QI0), "xbc": (w_in, XBC0), "q": (w_in, Q0), "z": (w_in, Z0),
                        "gate": (w_in, GS0 if st[1:2] == (0,) else GA0), "atto": (w_attn_o, 0),
                        "wo": (w_out, 0), "ck": (w_ckv, 0), "cv": (w_ckv, D), "cq": (w_cq, 0), "co": (w_co, 0),
                    }[kind]
                    a += NCOL * (st[-1] if len(st) > 1 else 0)
                    halves(rows(w[l], a, a + NCOL))

            def down(l, u, g, b, i):
                sp.wait_ge(dn_s, u * (2 * NB) + (2 * b + i + 1))
                settle(sp)
                for j in range(BE):
                    src = w_down[l, g, b * BE + j].rearrange("(k p) (a n) -> p a k n", p=P, a=2)
                    sp.dma_start(dquad[2 * b + i][:, j, :, :], src[:, i, :, :]).then_inc(d_in_sem[2 * b + i], 16)

            def experts(l, u, g, down_ahead=()):
                for b in range(NB):
                    for i in range(W_SLOTS):
                        filled(sp, l, last_job(NCH - W_SLOTS + i))
                        settle(sp)
                        sp.wait_ge(gu_s, u * (W_SLOTS * NB) + (W_SLOTS * b + i + 1))
                        settle(sp)
                        for a, w in enumerate((w_gate, w_up)):
                            src = w[l, g, b * BE:(b + 1) * BE].rearrange("j (p a k) n -> p a j (k n)", p=P, a=W_SLOTS)
                            sp.dma_start(up_part[i][:, a, :, :], src[:, i]).then_inc(up_part_in[i], 16)
                    for i in range(2):
                        if (b, i) not in down_ahead:
                            down(l, u, g, b, i)

            with sp.Fori(0, DEPTH) as l:
                sp.wait_ge(prm_used, l + 1)
                settle(sp)
                sp.dma_start(prm[:, :], params[l]).then_inc(prm_in, 16)
                before = passes_before(sp, SP, l)
                for c in range(NCH):
                    chunk(l, c, before)
                    if c == CHUNK[(("ssdo", 1), 1)]:
                        filled(sp, l, JOB[(("ssd", SG - 1), 1)])
                        settle(sp)
                        sp.dma_start(rw[:, :, 0:G], rows(w_group[l], 0, G)).then_inc(router_in, 16)
                        sp.dma_start(rw[:, :, G:G + G * E], rows(w_router[l], 0, G * E)).then_inc(router_in, 16)
                    if c == CHUNK[(("wo", 1), 0)]:
                        filled(sp, l, JOB[(("yT", 7), 0)])
                        settle(sp)
                        down(l, before, 0, 0, 0)
                filled(sp, l, JOB[(("xpv", 3), 0)])
                settle(sp)
                down(l, before, 0, 0, 1)
                down(l, before, 0, 1, 1)
                experts(l, before, 0, down_ahead=[(0, 0), (0, 1), (1, 1)])
                with sp.Fori(1, G) as g:
                    experts(l, before + g, g)
                more_passes(sp, SP, l, lambda u, g: experts(l, u, g))
            for t in range(TT):
                sp.wait_ge(fin_s, t + 1)
                sp.dma_start(out[t * P:(t + 1) * P, :], xn[:, t, :]).then_inc(out_s, 16)
            sp.wait_ge(out_s, TT * 16)

        @block.gpsimd
        def _(pool):
            def power(at, r):
                pool.wait_ge(var_rdy, at)
                nc.gpsimd.tensor_tensor(r, r, cst[:, C_MH:C_MH + r.shape[1]], ALU.pow).then_inc(rstd_rdy, 1)

            pool.wait_ge(cst_in, 16)
            with pool.Fori(0, DEPTH) as l:
                pool.wait_ge(prm_in, l * 16 + 16)
                power(l * NORMS + 1, st_[:, 18:20])
                pool.wait_ge(ka_rdy, l + 1)
                settle(pool)
                nc.gpsimd.tensor_copy(ktok[:, :, :, 1, :], ktok[:, :, :, 0, :]).then_inc(dup_rdy, 1)
                pool.wait_ge(eac_rdy, l + 1)
                for n, (t, g) in enumerate(SSD):
                    if n == 0:
                        drained(pool, l, JOB[(("xT", 7), 0)])
                    xsg = xs[:, t, g * NCOL:(g + 1) * NCOL].rearrange("p (h d) -> p h d", d=SP_)
                    if n >= 2:
                        filled(pool, l, JOB[(("ssd", n - 2), 1)])
                    dst = xdt[:, n % 2, :].rearrange("p (h d) -> p h d", d=SP_)
                    nc.gpsimd.tensor_tensor(dst, xsg, bc(dtb[:, t, g * HG:(g + 1) * HG], 2, SP_),
                                            ALU.mult).then_inc(p_step, 1)
                    pool.wait_ge(p_step, l * len(SSD) + (n + 1))
                    if t == 0:
                        if n >= 1:
                            filled(pool, l, JOB[(("ssd", n - 1), 1)])
                        nc.gpsimd.tensor_tensor(xdtt[:, :].rearrange("p (h d) -> p h d", d=SP_), dst,
                                                bc(tail[:, g * HG:(g + 1) * HG], 2, SP_), ALU.mult)
                    nc.gpsimd.tensor_tensor(xsg, xsg, bc(prm[:, P_DS + g * HG:P_DS + (g + 1) * HG], 2, SP_),
                                            ALU.mult).then_inc(x_scaled, 1)
                power(l * NORMS + 2, st_[:, 8:16])
                filled(pool, l, JOB[(("ssdo", 1), 1)])
                settle(pool)
                pool.dma_start(memx, mem.rearrange("(t p) d -> p t d", p=P)).then_inc(mem_in, 16)
                for k in (3, 4, 5):
                    power(l * NORMS + k, st_[:, 18:20])
            pool.wait_ge(filled_s, (DEPTH - 1) * NJ + JOB[(("router",), 0)] + 1)
            pool.dma_start(fgain, gain_final).then_inc(fin_in, 16)
            power(DEPTH * NORMS + 1, st_[:, 18:20])
            pool.wait_ge(fin_in, 16)

        @block.tensor
        def _(pe):
            def transposes(l, job, blocks):
                free(l, job)
                b = bank[job % 8]
                for i, src in enumerate(blocks):
                    ins = nc.tensor.transpose(b[:, i * P:(i + 1) * P], src, ident)
                ins.then_inc(filled_s, 1)

            def free(l, job, also=()):
                all_drained(pe, l, list(also) + ([job - 8] if job >= 8 else []))

            def chunk_in(l, c):
                pe.wait_ge(w_in_sem[SLOT[c]], (l * SLOT.count(SLOT[c]) + (NTH[c] + 1)) * 32)

            def by_token(l, st, src, width=NCOL, made_by=None, tiles=range(TT)):
                c = CHUNK[(st, 0)]
                chunk_in(l, c)
                for t in tiles:
                    job = JOB[(st, t)]
                    src_job = {k: JOB[((*made_by, k // 2), 0)] for k in range(KC)} if made_by and t == 0 else {}
                    free(l, job, [src_job[FIRST_BLOCK]] if src_job else [])
                    for i in range(KC):
                        k = (FIRST_BLOCK + i) % KC
                        if src_job and i and k % 2 == 0:
                            drained(pe, l, src_job[k])
                        ins = nc.tensor.matmul(bank[job % 8][:, 0:width], src[:, k, t * P:(t + 1) * P],
                                               wring[:, SLOT[c], k, 0:width], start=i == 0, stop=i == KC - 1)
                    ins.then_inc(filled_s, 1)

            def by_channel(l, st, src, made_by=None):
                c = CHUNK[(st, 0)]
                chunk_in(l, c)
                for j in range(2):
                    job = JOB[(st, j)]
                    free(l, job, [JOB[((*made_by, FIRST_PAIR), 0)]] if made_by and j == 0 else [])
                    for i in range(2):
                        m = (2 * j + i) * P
                        for n in range(KC):
                            k = (2 * FIRST_PAIR + n) % KC
                            if made_by and m == 0 and n in (2, 4, 6):
                                drained(pe, l, JOB[((*made_by, k // 2), 0)])
                            ins = nc.tensor.matmul(bank[job % 8][:, i * SEQ:(i + 1) * SEQ],
                                                   wring[:, SLOT[c], k, m:m + P], src[:, k, :],
                                                   start=n == 0, stop=n == KC - 1)
                    ins.then_inc(filled_s, 1)

            def pairs(src, i):
                return [src[:, t, (2 * i + j) * P:(2 * i + j + 1) * P] for j in range(2) for t in range(TT)]

            def stage(l, st):
                kind = st[0]
                if kind == "hT":
                    pe.wait_ge(norm_rdy, l * 3 + st[1] + 1)
                    if st[1] != 1:
                        pe.wait_ge(norm1_rdy, l * 2 + (1 + st[1] // 2))
                    transposes(l, JOB[(st, 0)], pairs(xn, st[2]))
                elif kind in ("small", "kv", "qi", "q", "gate"):
                    by_token(l, st, hT, {"small": SH + HD + IH, "kv": 2 * AKV * HD}.get(kind, NCOL),
                             made_by=("hT", 0) if kind == "small" else None)
                elif kind == "part":
                    by_token(l, st[1], hT, tiles=st[2:3])
                elif kind == "xbc":
                    by_channel(l, st, hT)
                elif kind == "acum":
                    pe.wait_ge(dt_rdy, l + 1)
                    job = JOB[(st, 0)]
                    free(l, job)
                    b = bank[job % 8]
                    for t in range(TT):
                        nc.tensor.matmul(b[:, t * SH:(t + 1) * SH], tri, dta[:, t, :], start=True, stop=True)
                    nc.tensor.matmul(b[:, 2 * SH:3 * SH], ones, dta[:, 0, :],
                                     start=True, stop=True).then_inc(filled_s, 1)
                elif kind == "kT":
                    pe.wait_ge(dup_rdy, l + 1)
                    job = JOB[(st, 0)]
                    free(l, job)
                    b = bank[job % 8]
                    for i in range(2):
                        for t in range(TT):
                            src = ktok[:, t, i, :, :].rearrange("p a d -> p (a d)")
                            ins = nc.tensor.transpose(b[:, (2 * i + t) * P:(2 * i + t + 1) * P], src, ident)
                    ins.then_inc(filled_s, 1)
                elif kind == "kiT":
                    job = JOB[(st, 0)]
                    free(l, job)
                    b = bank[job % 8]
                    for t in range(TT):
                        src = ktok[:, t, 2, :, :].rearrange("p a d -> p (a d)")
                        ins = nc.tensor.transpose(b[:, t * P:(t + 1) * P], src, ident)
                    ins.then_inc(filled_s, 1)
                elif kind == "qiT":
                    if st[1] == 0:
                        drained(pe, l, JOB[(("qi",), 1)])
                    transposes(l, JOB[(st, 0)], pairs(qbuf, st[1]))
                elif kind == "idx":
                    _, t, r, i = st
                    drained(pe, l, JOB[(("kiT",), 0)])
                    drained(pe, l, JOB[(("qiT", 1), 0)])
                    job = JOB[(st, 0)]
                    free(l, job)
                    nk = (t + 1) * P
                    for j in range(NCOL // nk):
                        pair = i * (NCOL // nk) + j
                        ins = nc.tensor.matmul(bank[job % 8][:, j * nk:(j + 1) * nk],
                                               qiT[r * HD:(r + 1) * HD, pair, t * P:(t + 1) * P],
                                               kT[r * HD:(r + 1) * HD, 2, 0:nk], start=True, stop=True)
                    ins.then_inc(filled_s, 1)
                elif kind == "xT":
                    t, q = divmod(st[1], 4)
                    pe.wait_ge(silu_rdy, l * 12 + (2 * q + 2))
                    transposes(l, JOB[(st, 0)], [xbcT[:, 4 * q + i, t * P:(t + 1) * P] for i in range(4)])
                elif kind == "bT":
                    pe.wait_ge(silu_rdy, l * 12 + 12)
                    transposes(l, JOB[(st, 0)], [xbcT[:, 2 * KC + g, 0:P] for g in range(SG)])
                elif kind == "cb":
                    job = JOB[(st, 0)]
                    free(l, job)
                    ts = slice(st[1] * P, (st[1] + 1) * P)
                    for g in range(SG):
                        ins = nc.tensor.matmul(bank[job % 8][:, g * P:(g + 1) * P], xbcT[:, 2 * KC + g, ts],
                                               xbcT[:, 2 * KC + SG + g, ts], start=True, stop=True)
                    ins.then_inc(filled_s, 1)
                elif kind == "qT":
                    drained(pe, l, JOB[(("q", 1), 1)])
                    transposes(l, JOB[(st, 0)], pairs(qbuf, st[1]))
                elif kind == "decay":
                    t, g = SSD[st[1]]
                    drained(pe, l, JOB[(("acum",), 0)])
                    for j in range(2):
                        job = JOB[(st, j)]
                        free(l, job)
                        for i in range(4):
                            hd = g * HG + 4 * j + i
                            ins = nc.tensor.transpose(bank[job % 8][:, i * P:(i + 1) * P],
                                                      acum[:, t, hd:hd + 1].to_broadcast([P, P]), ident)
                        ins.then_inc(filled_s, 1)
                elif kind == "ssd":
                    n = st[1]
                    t, g = SSD[n]
                    pe.wait_ge(x_scaled, l * len(SSD) + (n + 1))
                    pe.wait_ge(m_rdy, l * len(SSD) + (n + 1))
                    job = JOB[(st, 0)]
                    free(l, job)
                    for i in range(HG):
                        ins = nc.tensor.matmul(bank[job % 8][:, i * SP_:(i + 1) * SP_],
                                               mm_[:, n % 2, i * P:(i + 1) * P],
                                               xdt[:, n % 2, i * SP_:(i + 1) * SP_], start=True, stop=True)
                    ins.then_inc(filled_s, 1)
                    job = JOB[(st, 1)]
                    free(l, job)
                    if t == 0:
                        drained(pe, l, JOB[(("bT",), 0)])
                        ins = nc.tensor.matmul(bank[job % 8][:, :], btok[:, g * SN:(g + 1) * SN], xdtt[:, :],
                                               start=True, stop=True)
                    else:
                        drained(pe, l, JOB[(("ssd", g), 1)])
                        ins = nc.tensor.matmul(bank[job % 8][:, :], xbcT[:, 2 * KC + SG + g, P:2 * P],
                                               state[:, g, :], start=True, stop=True)
                    ins.then_inc(filled_s, 1)
                elif kind == "score":
                    t, r, i = ATT[st[1]]
                    drained(pe, l, JOB[(("qT", 3), 0)])
                    drained(pe, l, JOB[(("kT",), 0)])
                    job = JOB[(st, 0)]
                    free(l, job)
                    nk = (t + 1) * P
                    nh = NCOL // nk
                    for j in range(nh):
                        pair = i * nh + j
                        ins = nc.tensor.matmul(bank[job % 8][:, j * nk:(j + 1) * nk],
                                               qT[r * HD:(r + 1) * HD, pair, t * P:(t + 1) * P],
                                               kT[r * HD:(r + 1) * HD, pair // 4, 0:nk], start=True, stop=True)
                    ins.then_inc(filled_s, 1)
                elif kind in ("probT", "xprobT"):
                    n = st[1] + (len(ATT) if kind == "xprobT" else 0)
                    pe.wait_ge(pr_rdy, l * (len(ATT) + 4) + (n + 1))
                    src = sco[:, st[1] % 2, :]
                    transposes(l, JOB[(st, 0)], [src[:, i * P:(i + 1) * P] for i in range(4)])
                elif kind == "pv":
                    n = st[1]
                    t, r, i = ATT[n]
                    drained(pe, l, JOB[(("probT", n), 0)])
                    job = JOB[(st, 0)]
                    free(l, job)
                    nk = t + 1
                    nh = 4 // nk
                    for j in range(nh):
                        grp = (i * nh + j) // 4
                        for s in range(nk):
                            ins = nc.tensor.matmul(bank[job % 8][:, j * HD:(j + 1) * HD],
                                                   pT[:, n % 2, (j * nk + s) * P:(j * nk + s + 1) * P],
                                                   vtok[:, s, grp * HD:(grp + 1) * HD],
                                                   start=s == 0, stop=s == nk - 1)
                    ins.then_inc(filled_s, 1)
                elif kind == "yT":
                    pe.wait_ge(yn_rdy, l + 1)
                    transposes(l, JOB[(st, 0)], pairs(xs, st[1]))
                elif kind == "ssdo":
                    jobs = [JOB[(st, t)] for t in range(TT)]
                    for half in range(2):
                        c = CHUNK[(st, half)]
                        chunk_in(l, c)
                        for t in range(TT):
                            if half == 0:
                                free(l, jobs[t], [JOB[(("yT", i), 0)] for i in range(8)])
                            for k in range(KC):
                                ins = nc.tensor.matmul(bank[jobs[t] % 8][:, :],
                                                       yT[:, half * KC + k, t * P:(t + 1) * P],
                                                       wring[:, SLOT[c], k, :],
                                                       start=half == 0 and k == 0, stop=half == 1 and k == KC - 1)
                            if half == 1:
                                ins.then_inc(filled_s, 1)
                elif kind == "aT":
                    drained(pe, l, JOB[(("pv", len(ATT) - 1), 0)])
                    transposes(l, JOB[(st, 0)], pairs(qbuf, st[1]))
                elif kind == "atto":
                    by_token(l, st, qT, made_by=("aT",))
                elif kind == "mgT":
                    drained(pe, l, JOB[(("atto", 1), 1)])
                    transposes(l, JOB[(st, 0)], pairs(xn, st[1]))
                elif kind == "wo":
                    by_token(l, st, hT, made_by=("mgT",))
                elif kind == "memT":
                    pe.wait_ge(mem_rdy, l + 1)
                    transposes(l, JOB[(st, 0)], pairs(memx, st[1]))
                elif kind == "ck":
                    by_channel(l, st, memT, made_by=("memT",))
                elif kind == "cv":
                    by_token(l, st, memT)
                elif kind == "cq":
                    by_channel(l, st, hT, made_by=("hT", 1))
                elif kind == "xscore":
                    t, pr = divmod(st[1], 2)
                    drained(pe, l, JOB[(("cq", 1), 1)])
                    job = JOB[(st, 0)]
                    free(l, job)
                    for j in range(2):
                        for k in range(2):
                            blk = 2 * (2 * pr + j) + k
                            ins = nc.tensor.matmul(bank[job % 8][:, j * SEQ:(j + 1) * SEQ],
                                                   qT[:, blk, t * P:(t + 1) * P], ckT[:, blk, :],
                                                   start=k == 0, stop=k == 1)
                    ins.then_inc(filled_s, 1)
                elif kind == "xpv":
                    n = st[1]
                    t, pr = divmod(n, 2)
                    drained(pe, l, JOB[(("xprobT", n), 0)])
                    job = JOB[(st, 0)]
                    free(l, job)
                    for j in range(2):
                        hd = 2 * pr + j
                        for s in range(2):
                            ins = nc.tensor.matmul(bank[job % 8][:, j * XD:(j + 1) * XD],
                                                   pT[:, n % 2, (2 * j + s) * P:(2 * j + s + 1) * P],
                                                   cv[:, s, hd * XD:(hd + 1) * XD], start=s == 0, stop=s == 1)
                    ins.then_inc(filled_s, 1)
                elif kind == "xoT":
                    drained(pe, l, JOB[(("xpv", 3), 0)])
                    transposes(l, JOB[(st, 0)], pairs(qbuf, st[1]))
                elif kind == "co":
                    by_token(l, st, qT, made_by=("xoT",))
                elif kind == "router":
                    pe.wait_ge(router_in, l * 32 + 32)
                    job = JOB[(st, 0)]
                    free(l, job, [JOB[(("hT", 2, 0), 0)]])
                    for t in range(TT):
                        for k in range(KC):
                            if t == 0 and k in (2, 4, 6):
                                drained(pe, l, JOB[(("hT", 2, k // 2), 0)])
                            ins = nc.tensor.matmul(bank[job % 8][:, t * 64:t * 64 + G + G * E],
                                                   hT[:, k, t * P:(t + 1) * P], rw[:, k, :],
                                                   start=k == 0, stop=k == KC - 1)
                    ins.then_inc(filled_s, 1)
                elif kind == "rank":
                    pe.wait_ge(oh_rdy, l + 1)
                    job = JOB[(st, 0)]
                    free(l, job)
                    b = bank[job % 8]
                    us = cols(rt, R_US, TT, G * E)
                    w = G * E
                    nc.tensor.matmul(b[:, 0:w], tris, us[:, 0, :], start=True, stop=True)
                    nc.tensor.matmul(b[:, w:2 * w], tris, us[:, 1, :], start=True, stop=False)
                    nc.tensor.matmul(b[:, w:2 * w], ones, us[:, 0, :], start=False, stop=True)
                    nc.tensor.matmul(b[:, 2 * w:3 * w], ones, us[:, 0, :], start=True, stop=False)
                    nc.tensor.matmul(b[:, 2 * w:3 * w], ones, us[:, 1, :], start=False,
                                     stop=True).then_inc(filled_s, 1)

            def expert_pass(u):
                pe.wait_ge(sel_rdy, u * 2 + 1)
                for c in range(KC):
                    b = bank[GATHER[c // 2]]
                    for k in range(TT):
                        ins = nc.tensor.matmul(b[:, (c % 2) * E * S:(c % 2 + 1) * E * S], xn_eighth[:, k, c, :],
                                               sel[:, k, :], start=k == 0, stop=k == TT - 1)
                    if c % 2:
                        ins.then_inc(gat_s, 1)
                pe.wait_ge(sel_rdy, u * 2 + 2)
                for b in range(NB):
                    for k in range(TT):
                        ins = nc.tensor.transpose(bank[2][:, b * SEQ + k * P:b * SEQ + (k + 1) * P],
                                                  selw[:, k, b * P:(b + 1) * P], ident)
                ins.then_inc(gat_s, 1)
                for b in range(NB):
                    for i in range(W_SLOTS):
                        if b == 0 and i % 2 == 0:
                            pe.wait_ge(xgv_rdy, u * 2 + (i // 2 + 1))
                            pe.wait_ge(xga_rdy, u * 2 + (i // 2 + 1))
                        pe.wait_ge(up_part_in[i], (u * NB + (b + 1)) * 32)
                        for k in range(KC // W_SLOTS):
                            for j in range(BE):
                                e = (b * BE + j) * S
                                kk = i * (KC // W_SLOTS) + k
                                ins = nc.tensor.matmul(bank[b][j * S:(j + 1) * S, :], xg[:, kk, e:e + S],
                                                       up_part[i][:, :, j, k * F:(k + 1) * F], start=kk == 0, stop=kk == KC - 1)
                        ins.then_inc(gu_s, 1)
                    pe.wait_ge(hid_s, u * NB + (b + 1))
                    for k in range(2):
                        ins = nc.tensor.transpose(bank[3][:, k * P:(k + 1) * P], hid[:, b, k * P:(k + 1) * P], ident)
                    ins.then_inc(hT_s, 1)
                    pe.wait_ge(hTc_s, u * NB + (b + 1))
                    for n in range(2):
                        pe.wait_ge(d_in_sem[2 * b + n], (u + 1) * (BE * 16))
                        for k in range(2):
                            for j in range(BE):
                                ins = nc.tensor.matmul(bank[4 + n][j * S:(j + 1) * S, :],
                                                       hidT[:, b, k * P + j * S:k * P + (j + 1) * S],
                                                       dquad[2 * b + n][:, j, k, :], start=k == 0, stop=k == 1)
                        ins.then_inc(dn_s, 1)
                    if b == 0:
                        pe.wait_ge(st_rdy, u + 1)
                    for k in range(TT):
                        for n in range(2):
                            if k == 0:
                                pe.wait_ge(yg_s, u * (2 * NB) + (2 * b + n + 1))
                            if b or k:
                                pe.wait_ge(add_s, u * (4 * NB) + (4 * b + 2 * k + n - 1))
                            nc.tensor.matmul(bank[6 + n][:, :], selT[:, b, k * P:(k + 1) * P],
                                             yg[:, n * NCOL:(n + 1) * NCOL], start=True, stop=True).then_inc(sct_s, 1)

            pe.wait_ge(cst_in, 16)
            with pe.Fori(0, DEPTH) as l:
                before = passes_before(pe, PE, l)
                for st in ORDER:
                    stage(l, st)
                drained(pe, l, max(k for k in range(NJ) if OWNER[k] == "dve"))
                drained(pe, l, max(k for k in range(NJ) if OWNER[k] == "act"))
                settle(pe)
                with pe.Fori(0, G) as g:
                    expert_pass(before + g)
                more_passes(pe, PE, l, lambda u, g: expert_pass(u))

        @block.scalar
        def _(act):
            steps = Steps(act, a_step)

            def stage(l, st):
                kind = st[0]
                job = JOB.get((st, 0))
                if kind == "norm" and st[1] != 1:
                    if st[1] == 0:
                        act.wait_ge(h_rdy, l + 1)
                        nc.scalar.activation(xn[:, 1, :], h[:, 1, :], ACT.Square,
                                             accum_out=st_[:, 17:18]).then_inc(sq_rdy, 1)
                    act.wait_ge(rstd_rdy, l * NORMS + (5 if st[1] else 1))
                    nc.scalar.activation(xn[:, 1, :], h[:, 1, :], ACT.Copy, scale=st_[:, 19:20]).then_inc(norm1_rdy, 1)
                elif kind == "xbc":
                    for j in range(2):
                        m = 2 * st[1] + j
                        filled(act, l, JOB[(st, j)])
                        if m >= 2:
                            act.wait_ge(silu_rdy, l * 12 + (m - 1))
                        for i in range(2):
                            ch = 2 * m + i
                            ins = nc.scalar.activation(conv[:, m % 2, i, :], bank[JOB[(st, j)] % 8][:, i * SEQ:(i + 1) * SEQ],
                                                       ACT.Identity, bias=prm[:, P_CB + ch:P_CB + ch + 1],
                                                       scale=prm[:, P_CW + 3 * CC + ch:P_CW + 3 * CC + ch + 1])
                        ins.then_inc(conv0_rdy, 1)
                    for j in range(2):
                        m = 2 * st[1] + j
                        act.wait_ge(conv_rdy, l * 12 + (m + 1))
                        nc.scalar.activation(xbcT[:, 2 * m:2 * m + 2, :], conv[:, m % 2, :, :],
                                             ACT.Silu).then_inc(silu_rdy, 1)
                elif kind == "dt":
                    act.wait_ge(dt_abs, l + 1)
                    steps.link(nc.scalar.activation(ex32, tmp32[:, 0, :], ACT.Exp, scale=-1.0))
                    steps.link(nc.scalar.activation(tmp32[:, 0, :], ex32, ACT.Ln, bias=1.0))
                    nc.scalar.activation(eac[:, :], prm[:, P_AL:P_AL + SH], ACT.Exp).then_inc(dt_log, 1)
                elif kind == "acum":
                    act.wait_ge(ac_rdy, l + 1)
                    nc.scalar.activation(eac[:, :], acum[:, 1, :], ACT.Exp)
                    nc.scalar.activation(tail[:, :], tail[:, :], ACT.Exp).then_inc(eac_rdy, 1)
                elif kind in ("qiT", "xT", "qT", "bT") or kind in SHARED and OWNER[job] == "act":
                    filled(act, l, job)
                    b = bank[job % 8][:, :]
                    if kind == "bT":
                        dst = btok[:, :]
                    elif kind == "xT":
                        t, q = divmod(st[1], 4)
                        dst = xs[:, t, q * NCOL:(q + 1) * NCOL]
                    else:
                        to, gain = TRANSPOSED[kind], gain_of(st)
                        i = st[-1]
                        if gain is not None:
                            for j in range(2):
                                ins = nc.scalar.activation(to[:, 2 * i + j, :], b[:, j * SEQ:(j + 1) * SEQ], ACT.Copy,
                                                           scale=prm[:, gain + 2 * i + j:gain + 2 * i + j + 1])
                            drain_inc(ins, job)
                            return
                        dst = to[:, 2 * i:2 * i + 2, :].rearrange("p c t -> p (c t)")
                    drain_inc(nc.scalar.activation(dst, b, ACT.Copy), job)
                elif kind == "idx":
                    filled(act, l, job)
                    n = IDX.index(st)
                    if n >= 2:
                        act.wait_ge(rel_used, l * len(IDX) + (n - 1))
                    drain_inc(nc.scalar.activation(rel[:, n % 2, :], bank[job % 8][:, :], ACT.Relu), job)
                elif kind in ("part", "gate", "cv"):
                    tiles = range(TT)
                    if kind == "part":
                        _, st, t = st
                        kind, tiles = st[0], [t]
                    for t in tiles:
                        job = JOB[(st, t)]
                        filled(act, l, job)
                        n = st[-1] * NCOL
                        if kind == "gate" and st[1] == 1:
                            drained(act, l, JOB[(("ssdo", 1), 1)])
                        dst = {"z": zt, "gate": gate, "cv": cv}[kind][:, t, n:n + NCOL]
                        func = {"z": ACT.Silu, "gate": ACT.Sigmoid, "cv": ACT.Copy}[kind]
                        drain_inc(nc.scalar.activation(dst, bank[job % 8][:, :], func), job)
                elif kind in ("ck", "cq"):
                    to = {"ck": ckT, "cq": qT}[kind]
                    for j in range(2):
                        job = JOB[(st, j)]
                        filled(act, l, job)
                        blk = 4 * st[1] + 2 * j
                        drain_inc(nc.scalar.activation(to[:, blk:blk + 2, :].rearrange("p c t -> p (c t)"),
                                                       bank[job % 8][:, :], ACT.Copy), job)
                elif kind == "decay":
                    n = st[1]
                    act.wait_ge(seg_rdy, l * len(SSD) + (n + 1))
                    nc.scalar.activation(mm_[:, n % 2, :], mm_[:, n % 2, :], ACT.Exp).then_inc(dec_rdy, 1)
                elif kind == "ssd":
                    t, g = SSD[st[1]]
                    if t == 0:
                        job = JOB[(st, 1)]
                        filled(act, l, job)
                        drain_inc(nc.scalar.activation(state[:, g, :], bank[job % 8][:, :], ACT.Copy), job)
                elif kind == "ygate":
                    t, g = SSD[st[1]]
                    act.wait_ge(y_rdy, l * len(SSD) + (st[1] + 1))
                    nc.scalar.activation(zt[:, t, g * NCOL:(g + 1) * NCOL], xs[:, t, g * NCOL:(g + 1) * NCOL], ACT.Square,
                                         accum_out=st_[:, st[1]:st[1] + 1]).then_inc(ssq_rdy, 1)
                elif kind == "score":
                    n = st[1]
                    t, r, i = ATT[n]
                    nk = (t + 1) * P
                    act.wait_ge(sc_rdy, l * (len(ATT) + 4) + (n + 1))
                    for j in range(NCOL // nk):
                        ins = nc.scalar.activation(sco[:, n % 2, j * nk:(j + 1) * nk], sco[:, n % 2, j * nk:(j + 1) * nk],
                                                   ACT.Exp, bias=nmx[:, n % 4, j:j + 1], scale=HD ** -0.5,
                                                   accum_out=sm[:, n % 4, j:j + 1])
                    ins.then_inc(pr_rdy, 1)
                elif kind == "xscore":
                    n = st[1]
                    act.wait_ge(sc_rdy, l * (len(ATT) + 4) + (len(ATT) + n + 1))
                    if n >= 2:
                        filled(act, l, JOB[(("xprobT", n - 2), 0)])
                    for j in range(2):
                        ins = nc.scalar.activation(sco[:, n % 2, j * SEQ:(j + 1) * SEQ], bank[job % 8][:, j * SEQ:(j + 1) * SEQ],
                                                   ACT.Exp, bias=nmx[:, n % 4, j:j + 1], scale=XD ** -0.5,
                                                   accum_out=sm[:, n % 4, j:j + 1])
                    ins.then_inc(pr_rdy, 1)
                    act.wait_ge(pr_rdy, l * (len(ATT) + 4) + (len(ATT) + n + 1))
                    drain_inc(act.nop(), job)
                elif kind in ("probT", "xprobT"):
                    filled(act, l, job)
                    n = st[1]
                    if n >= 2:
                        filled(act, l, JOB[("pv" if kind == "probT" else "xpv", n - 2), 0])
                    drain_inc(nc.scalar.activation(pT[:, n % 2, :], bank[job % 8][:, :], ACT.Copy), job)
                elif kind == "router":
                    act.wait_ge(rt_in, l + 1)
                    gd = cols(rt, R_GD, TT * G)
                    nc.scalar.activation(cols(rt, R_GE, TT * G), gd, ACT.Exp).then_inc(rt_exp, 1)
                    act.wait_ge(r2_in, l + 1)
                    nc.scalar.activation(cols(rt, R_TW, TT), cols(rt, R_DL, TT), ACT.Exp).then_inc(r2_exp, 1)

            def expert_pass(u):
                for i in (1, 3):
                    act.wait_ge(gat_s, u * 5 + (i + 1))
                    for c in (2 * i, 2 * i + 1):
                        ins = nc.scalar.activation(xg[:, c, :], bank[GATHER[i]][:, (c % 2) * E * S:(c % 2 + 1) * E * S],
                                                   ACT.Copy, scale=prm_ffn[:, c:c + 1])
                    ins.then_inc(xga_rdy, 1)
                for b in range(NB):
                    act.wait_ge(gu_s, u * (W_SLOTS * NB) + (W_SLOTS * b + 2 * W_SLOTS))
                    nc.scalar.activation(sil[:, b, :], bank[b][:, 0:F], ACT.Silu).then_inc(sil_s, 1)
                    act.wait_ge(hT_s, u * NB + (b + 1))
                    nc.scalar.activation(hidT[:, b, :], bank[3][:, 0:F], ACT.Copy).then_inc(hTc_s, 1)
                    for n in range(2):
                        act.wait_ge(dn_s, u * (2 * NB) + (2 * b + n + 1 + 2 * NB))
                        if b:
                            act.wait_ge(sct_s, u * (4 * NB) + (n + 3))
                        nc.scalar.activation(yg[:, n * NCOL:(n + 1) * NCOL], bank[4 + n][:, :],
                                             ACT.Copy).then_inc(yg_s, 1)

            with act.Fori(0, DEPTH) as l:
                before = passes_before(act, AC, l)
                steps.at(l * A_LAYER)
                for st in ORDER:
                    if st == ("hT", 0, 0):
                        act.wait_ge(prm_in, l * 16 + 16)
                    stage(l, st)
                assert steps.n == A_LAYER, f"A_LAYER = {steps.n}"
                with act.Fori(0, G) as g:
                    expert_pass(before + g)
                more_passes(act, AC, l, lambda u, g: expert_pass(u))

        @block.vector
        def _(dve):
            steps = Steps(dve, v_step)
            link = steps.link
            V = nc.vector

            def rms(at, ss, r, n):
                V.tensor_scalar(r, ss, 1.0 / n, EPS, ALU.mult, ALU.add).then_inc(var_rdy, 1)
                dve.wait_ge(rstd_rdy, at)

            def squares(src, scratch, tiles=range(TT)):
                for t in tiles:
                    ins = V.scalar_tensor_tensor(scratch[:, t, :], src[:, t, :], 1.0, src[:, t, :], ALU.mult, ALU.mult,
                                                 accum_out=st_[:, 16 + t:17 + t])
                return ins

            def normalise(at, src, dst, scratch):
                link(squares(src, scratch))
                return scale(at, src, dst)

            def scale(at, src, dst, tiles=range(TT)):
                rms(at, st_[:, 16:18], st_[:, 18:20], D)
                for t in tiles:
                    ins = V.tensor_scalar(dst[:, t, :], src[:, t, :], st_[:, 18 + t:19 + t], None, ALU.mult)
                return ins

            def rope(src, nh, t, dst):
                a = ropeA[:, 0:nh * HD].rearrange("p (h d) -> p h d", d=HD)
                b = ropeB[:, 0:nh * HD].rearrange("p (h d) -> p h d", d=HD)
                s = src.rearrange("p (h d) -> p h d", d=HD)
                cos = bc(cst[:, C_COS + t * HD:C_COS + (t + 1) * HD], 1, nh)
                sin = bc(cst[:, C_SIN + t * HD:C_SIN + (t + 1) * HD], 1, nh)
                V.tensor_tensor(a, s, cos, ALU.mult)
                link(V.tensor_tensor(b, s, sin, ALU.mult))
                hf = HD // 2
                V.tensor_tensor(dst[:, :, 0:hf], a[:, :, 0:hf], b[:, :, hf:HD], ALU.subtract)
                return V.tensor_tensor(dst[:, :, hf:HD], a[:, :, hf:HD], b[:, :, 0:hf], ALU.add)

            def first_max(src, prio, m, eq, oh, n):
                link(V.tensor_reduce(m, src, AX_X, ALU.max))
                link(V.tensor_tensor(eq, src, bc(m, 2, n), ALU.is_equal))
                link(V.tensor_tensor(eq, eq, bc(prio, 1, TT), ALU.mult))
                link(V.tensor_reduce(cols(rt, R_T2, TT), eq, AX_X, ALU.max))
                link(V.tensor_tensor(oh, eq, bc(cols(rt, R_T2, TT), 2, n), ALU.is_equal))

            def stage(l, st):
                kind = st[0]
                job = JOB.get((st, 0))
                b = bank[job % 8][:, :] if job is not None else None
                if kind == "norm" and st[1] == 0:
                    dve.nop().then_inc(h_rdy, 1)
                    link(squares(h, xn, [0]))
                    dve.wait_ge(sq_rdy, l + 1)
                    scale(l * NORMS + 1, h, xn, [0]).then_inc(norm_rdy, 1)
                elif kind == "norm":
                    link(V.tensor_reduce(st_[:, 16:18], st_[:, 0:4].rearrange("p (t n) -> p t n", n=2), AX_X, ALU.add))
                    scale(l * NORMS + 3 + st[1], h, xn, range(TT) if st[1] == 1 else [0]).then_inc(norm_rdy, 1)
                elif kind in SHARED:
                    if OWNER[job] == "dve":
                        filled(dve, l, job)
                        i, to, gain = st[-1], TRANSPOSED[kind], gain_of(st)
                        if gain is None:
                            drain_inc(V.tensor_copy(to[:, 2 * i:2 * i + 2, :].rearrange("p c t -> p (c t)"), b), job)
                        else:
                            for j in range(2):
                                ins = V.tensor_scalar(to[:, 2 * i + j, :], b[:, j * SEQ:(j + 1) * SEQ],
                                                      prm[:, gain + 2 * i + j:gain + 2 * i + j + 1], None, ALU.mult)
                            drain_inc(ins, job)
                elif kind == "small":
                    for t in range(TT):
                        job = JOB[(st, t)]
                        b = bank[job % 8]
                        filled(dve, l, job)
                        V.tensor_tensor(dtb[:, t, :], b[:, 0:SH], prm[:, P_DTB:P_DTB + SH], ALU.add)
                        V.tensor_scalar(wis[:, t, :], b[:, SH + HD:SH + HD + IH], IDX_SCALE, None, ALU.mult)
                        link(rope(b[:, SH:SH + HD], 1, t, ktok[:, t, 2:3, 0, :]))
                        drain_inc(dve.nop(), job)
                    dts = dtb[:, :, :].rearrange("p t h -> p (t h)")
                    V.scalar_tensor_tensor(tmp32[:, 0, :], dts, -1.0, dts, ALU.mult, ALU.max).then_inc(dt_abs, 1)
                    link(V.tensor_scalar(tmp32[:, 1, :], dts, 0.0, None, ALU.max))
                elif kind == "kv":
                    for t in range(TT):
                        job = JOB[(st, t)]
                        b = bank[job % 8]
                        filled(dve, l, job)
                        V.tensor_copy(vtok[:, t, :], b[:, AKV * HD:2 * AKV * HD])
                        link(rope(b[:, 0:AKV * HD], AKV, t, ktok[:, t, 0:AKV, 0, :]))
                        drain_inc(dve.nop(), job)
                    dve.nop().then_inc(ka_rdy, 1)
                elif kind in ("qi", "q"):
                    for t in range(TT):
                        job = JOB[(st, t)]
                        filled(dve, l, job)
                        n = NCOL * st[1] if kind == "q" else 0
                        if kind == "q" and st[1] == 0 and t == 0:
                            filled(dve, l, JOB[(("qiT", 1), 0)])
                        dst = qbuf[:, t, n:n + NCOL].rearrange("p (h d) -> p h d", d=HD)
                        link(rope(bank[job % 8][:, :], NCOL // HD, t, dst))
                        drain_inc(dve.nop(), job)
                elif kind == "xbc":
                    for j in range(2):
                        m = 2 * st[1] + j
                        job = JOB[(st, j)]
                        b = bank[job % 8]
                        dve.wait_ge(conv0_rdy, l * 12 + (m + 1))
                        for k in range(1, TAPS):
                            for i in range(2):
                                ch = 2 * m + i
                                w = P_CW + (TAPS - 1 - k) * CC + ch
                                ins = V.scalar_tensor_tensor(conv[:, m % 2, i, k:SEQ], b[:, i * SEQ:(i + 1) * SEQ - k],
                                                             prm[:, w:w + 1], conv[:, m % 2, i, k:SEQ], ALU.mult, ALU.add)
                            if k < TAPS - 1:
                                link(ins)
                            else:
                                ins.then_inc(conv_rdy, 1)
                                dve.wait_ge(conv_rdy, l * 12 + (m + 1))
                                drain_inc(dve.nop(), job)
                elif kind == "dt":
                    dve.wait_ge(dt_log, l + 1)
                    dts = dtb[:, :, :].rearrange("p t h -> p (t h)")
                    link(V.tensor_tensor(dts, tmp32[:, 0, :], tmp32[:, 1, :], ALU.add))
                    V.scalar_tensor_tensor(dta[:, :, :], dtb[:, :, :], -1.0, bc(eac[:, :], 1, TT),
                                           ALU.mult, ALU.mult).then_inc(dt_rdy, 1)
                elif kind == "acum":
                    filled(dve, l, job)
                    link(V.tensor_copy(acum[:, :, :].rearrange("p t h -> p (t h)"), b[:, 0:3 * SH]))
                    drain_inc(dve.nop(), job)
                    V.tensor_tensor(tail[:, :], acum[:, 2, :], acum[:, 0, :], ALU.subtract).then_inc(ac_rdy, 1)
                elif kind in ("kT", "kiT"):
                    filled(dve, l, job)
                    if kind == "kT":
                        dst = kT[:, 0:AKV, :]
                        src = b.rearrange("p (a t) -> p a t", a=AKV)
                    else:
                        dst, src = kT[:, AKV, :], b[:, 0:SEQ]
                    drain_inc(V.tensor_copy(dst, src), job)
                elif kind == "idx":
                    _, t, r, i = st
                    nk = (t + 1) * P
                    n = IDX.index(st)
                    drained(dve, l, job)
                    for j in range(NCOL // nk):
                        hd = 2 * (i * (NCOL // nk) + j) + r
                        src = rel[:, n % 2, j * nk:(j + 1) * nk]
                        if r == 0 and i == 0 and j == 0:
                            ins = V.tensor_scalar(isc[:, 0:nk], src, wis[:, t, hd:hd + 1], None, ALU.mult)
                        else:
                            ins = V.scalar_tensor_tensor(isc[:, 0:nk], src, wis[:, t, hd:hd + 1], isc[:, 0:nk],
                                                         ALU.mult, ALU.add)
                        link(ins)
                    dve.nop().then_inc(rel_used, 1)
                elif kind == "topk":
                    t = st[1]
                    nk = (t + 1) * P
                    s = isc[:, 0:nk]
                    link(V.tensor_tensor(isc[:, t * P:nk], isc[:, t * P:nk], caus, ALU.add))
                    for _ in range(TOPK // 8):
                        settle(dve)
                        link(V.max(top8[:, :], s))
                        settle(dve)
                        link(V.match_replace(s, top8[:, :], s, TAKEN))
                    link(V.tensor_scalar(pen[:, t, 0:nk], s, TAKEN / 2, NEG, ALU.is_gt, ALU.mult))
                    link(V.tensor_tensor(pen[:, t, t * P:nk], pen[:, t, t * P:nk], caus, ALU.add))
                elif kind == "cb":
                    filled(dve, l, job)
                    if st[1] == 0:
                        filled(dve, l, JOB[(IDX[-1], 0)])
                    drain_inc(V.tensor_tensor(cbm[:, st[1], :].rearrange("p (g t) -> p g t", g=SG),
                                              b.rearrange("p (g t) -> p g t", g=SG), bc(tri, 1, SG), ALU.mult), job)
                elif kind == "decay":
                    n = st[1]
                    t, g = SSD[n]
                    if n == 0:
                        dve.wait_ge(silu_rdy, l * 12 + 12)
                    if n >= 2:
                        filled(dve, l, JOB[(("ssd", n - 2), 0)])
                    for j in range(2):
                        job = JOB[(st, j)]
                        filled(dve, l, job)
                        for i in range(4):
                            hd = 4 * j + i
                            ins = V.tensor_scalar(mm_[:, n % 2, hd * P:(hd + 1) * P], bank[job % 8][:, i * P:(i + 1) * P],
                                                  acum[:, t, g * HG + hd:g * HG + hd + 1], 0.0, ALU.subtract, ALU.min)
                        drain_inc(ins, job)
                    drained(dve, l, job)
                    dve.nop().then_inc(seg_rdy, 1)
                    dve.wait_ge(dec_rdy, l * len(SSD) + (n + 1))
                    m3 = mm_[:, n % 2, :].rearrange("p (h t) -> p h t", h=HG)
                    V.tensor_tensor(m3, m3, bc(cbm[:, t, g * P:(g + 1) * P], 1, HG), ALU.mult).then_inc(m_rdy, 1)
                elif kind == "ssd":
                    n = st[1]
                    t, g = SSD[n]
                    y = xs[:, t, g * NCOL:(g + 1) * NCOL]
                    filled(dve, l, job)
                    dve.wait_ge(x_scaled, l * len(SSD) + (n + 1))
                    link(V.tensor_tensor(y, b, y, ALU.add))
                    drain_inc(dve.nop(), job)
                    if t == 1:
                        job = JOB[(st, 1)]
                        filled(dve, l, job)
                        link(V.tensor_tensor(ytmp.rearrange("p (h d) -> p h d", d=SP_),
                                             bank[job % 8][:, :].rearrange("p (h d) -> p h d", d=SP_),
                                             bc(eac[:, g * HG:(g + 1) * HG], 2, SP_), ALU.mult))
                        drain_inc(dve.nop(), job)
                        link(V.tensor_tensor(y, y, ytmp, ALU.add))
                elif kind == "ygate":
                    t, g = SSD[st[1]]
                    drained(dve, l, JOB[(("z", 3), 1)])
                    y = xs[:, t, g * NCOL:(g + 1) * NCOL]
                    V.tensor_tensor(y, y, zt[:, t, g * NCOL:(g + 1) * NCOL], ALU.mult).then_inc(y_rdy, 1)
                elif kind == "ynorm":
                    dve.wait_ge(ssq_rdy, (l + 1) * len(SSD))
                    rms(l * NORMS + 2, st_[:, 0:8], st_[:, 8:16], NCOL)
                    for t in range(TT):
                        for g in range(SG):
                            y = xs[:, t, g * NCOL:(g + 1) * NCOL]
                            ins = V.tensor_scalar(y, y, st_[:, 8 + t * SG + g:9 + t * SG + g], None, ALU.mult)
                    ins.then_inc(yn_rdy, 1)
                elif kind == "score":
                    n = st[1]
                    t, r, i = ATT[n]
                    nk = (t + 1) * P
                    nh = NCOL // nk
                    filled(dve, l, job)
                    if n == 0:
                        filled(dve, l, JOB[(("ssd", len(SSD) - 1), 1)])
                    if n >= 2:
                        filled(dve, l, JOB[(("probT", n - 2), 0)])
                    s3 = sco[:, n % 2, :].rearrange("p (h s) -> p h s", h=nh)
                    link(V.tensor_tensor(s3, b.rearrange("p (h s) -> p h s", h=nh), bc(pen[:, t, 0:nk], 1, nh), ALU.add))
                    drain_inc(dve.nop(), job)
                    link(V.tensor_reduce(mx[:, n % 4, 0:nh], s3, AX_X, ALU.max))
                    V.tensor_scalar(nmx[:, n % 4, 0:nh], mx[:, n % 4, 0:nh], -(HD ** -0.5), None,
                                    ALU.mult).then_inc(sc_rdy, 1)
                elif kind == "xscore":
                    n = st[1]
                    filled(dve, l, job)
                    if n >= 2:
                        dve.wait_ge(pr_rdy, l * (len(ATT) + 4) + (len(ATT) + n - 1))
                    link(V.tensor_reduce(mx[:, n % 4, 0:2], b.rearrange("p (h s) -> p h s", h=2), AX_X, ALU.max))
                    V.tensor_scalar(nmx[:, n % 4, 0:2], mx[:, n % 4, 0:2], -(XD ** -0.5), None,
                                    ALU.mult).then_inc(sc_rdy, 1)
                elif kind in ("pv", "xpv"):
                    n = st[1]
                    if kind == "pv":
                        t, r, i = ATT[n]
                        nh, w = 4 // (t + 1), HD
                        dst = qbuf[:, t, :].rearrange("p (a r d) -> p a r d", r=2, d=HD)[:, i * nh:(i + 1) * nh, r, :]
                    else:
                        t, pr = divmod(n, 2)
                        nh, w = 2, XD
                        dst = qbuf[:, t, pr * NCOL:(pr + 1) * NCOL].rearrange("p (a d) -> p a d", a=2)
                    filled(dve, l, job)
                    link(V.reciprocal(rs[:, n % 4, 0:nh], sm[:, n % 4, 0:nh]))
                    drain_inc(V.tensor_tensor(dst, b[:, 0:nh * w].rearrange("p (h d) -> p h d", h=nh),
                                              bc(rs[:, n % 4, 0:nh], 2, w), ALU.mult), job)
                elif kind == "ssdo":
                    n = st[1] * NCOL
                    for t in range(TT):
                        job = JOB[(st, t)]
                        filled(dve, l, job)
                        drained(dve, l, JOB[(("gate", 0, 1), 1)])
                        drain_inc(V.tensor_tensor(xn[:, t, n:n + NCOL], bank[job % 8][:, :], gate[:, t, n:n + NCOL], ALU.mult), job)
                elif kind == "atto":
                    n = st[1] * NCOL
                    for t in range(TT):
                        job = JOB[(st, t)]
                        filled(dve, l, job)
                        drained(dve, l, JOB[(("gate", 1, 1), 1)])
                        g_ = gate[:, t, n:n + NCOL]
                        link(V.tensor_tensor(g_, bank[job % 8][:, :], g_, ALU.mult))
                        drain_inc(V.tensor_tensor(xn[:, t, n:n + NCOL], xn[:, t, n:n + NCOL], g_, ALU.add), job)
                elif kind in ("wo", "co"):
                    n = st[1] * NCOL
                    if kind == "wo" and st[1] == 0:
                        dve.wait_ge(mem_in, l * 16 + 16)
                        normalise(l * NORMS + 3, memx, memx, cols(big, 2048, TT, D)).then_inc(mem_rdy, 1)
                    for t in range(TT):
                        job = JOB[(st, t)]
                        filled(dve, l, job)
                        hh = h[:, t, n:n + NCOL]
                        drain_inc(V.tensor_tensor(hh, bank[job % 8][:, :], hh, ALU.add), job)
                        drained(dve, l, job)
                        at = 2 * t + st[1]
                        link(V.scalar_tensor_tensor(xn[:, t, n:n + NCOL], hh, 1.0, hh, ALU.mult, ALU.mult,
                                                    accum_out=st_[:, at:at + 1]))
                elif kind == "router":
                    route(l, st, job, b)
                elif kind == "rank":
                    rank(l, job, b)

            def route(l, st, job, b):
                lg = cols(rt, R_LG, TT, G + G * E)
                filled(dve, l, job)
                link(V.tensor_tensor(lg, b.rearrange("p (a n) -> p a n", n=64)[:, 0:TT, 0:G + G * E],
                                     bc(prm[:, P_BR:P_BR + G + G * E], 1, TT), ALU.add))
                drain_inc(dve.nop(), job)
                dve.nop().then_inc(prm_used, 1)
                gm, oh = cols(rt, R_GM, TT), cols(rt, R_OH, TT, G)
                eq4 = cols(rt, R_EQ, TT, G)
                gd = cols(rt, R_GD, TT, G)
                prio = cst[:, C_PRIO:C_PRIO + E]
                first_max(lg[:, :, 0:G], prio[:, 0:G], gm, eq4, oh, G)
                V.tensor_tensor(gd, lg[:, :, 0:G], bc(gm, 2, G), ALU.subtract).then_inc(rt_in, 1)
                lge = lg[:, :, G:G + G * E].rearrange("p t (g e) -> p t g e", g=G)
                pick = rt[:, R_PK:R_PK + TT * G * E].rearrange("p (t g e) -> p t g e", t=TT, g=G)
                for t in range(TT):
                    ins = V.tensor_tensor(pick[:, t], lge[:, t], bc(oh[:, t, :], 2, E), ALU.mult)
                link(ins)
                ein = cols(rt, R_EI, TT, E)
                for t in range(TT):
                    ins = V.tensor_reduce(ein[:, t, :], pick[:, t].rearrange("p g e -> p e g"), AX_X, ALU.add)
                link(ins)
                v1, v2 = cols(rt, R_V1, TT), cols(rt, R_V2, TT)
                oh1, oh2 = cols(rt, R_O1, TT, E), cols(rt, R_O2, TT, E)
                eq8 = cols(rt, R_EQ, TT, E)
                first_max(ein, prio, v1, eq8, oh1, E)
                link(V.scalar_tensor_tensor(ein, oh1, TAKEN, ein, ALU.mult, ALU.add))
                first_max(ein, prio, v2, eq8, oh2, E)
                V.tensor_tensor(cols(rt, R_DL, TT), v2, v1, ALU.subtract).then_inc(r2_in, 1)
                link(V.tensor_tensor(eq8, oh1, oh2, ALU.add))
                us = rt[:, R_US:R_US + TT * G * E].rearrange("p (t g e) -> p t g e", t=TT, g=G)
                for t in range(TT):
                    ins = V.tensor_tensor(us[:, t], bc(oh[:, t, :], 2, E), bc(eq8[:, t, :], 1, G), ALU.mult)
                ins.then_inc(oh_rdy, 1)
                dve.wait_ge(oh_rdy, l + 1)
                dve.wait_ge(rt_exp, l + 1)
                gs = cols(rt, R_GS, TT)
                link(V.tensor_reduce(gs, cols(rt, R_GE, TT, G), AX_X, ALU.add))
                dve.wait_ge(r2_exp, l + 1)
                tw, den = cols(rt, R_TW, TT), cols(rt, R_DN, TT)
                link(V.scalar_tensor_tensor(den, tw, 1.0, gs, ALU.add, ALU.mult))
                link(V.reciprocal(den, den))
                link(V.tensor_tensor(tw, tw, den, ALU.mult))
                wi_ = cols(rt, R_WI, TT, E)
                V.tensor_tensor(oh2, oh2, bc(tw, 2, E), ALU.mult)
                link(V.tensor_tensor(wi_, oh1, bc(den, 2, E), ALU.mult))
                link(V.tensor_tensor(wi_, wi_, oh2, ALU.add))

            def rank(l, job, b):
                filled(dve, l, job)
                us, key = cols(rt, R_US, TT * G * E), cols(rt, R_KY, TT * G * E)
                w = G * E
                link(V.tensor_scalar(key, us, -16.0 * SEQ, 16.0 * SEQ, ALU.mult, ALU.add))
                V.tensor_tensor(key, b[:, 0:TT * w], key, ALU.add)
                cnt = cols(rt, R_CN, G)
                link(V.tensor_reduce(cnt, b[:, 2 * w:3 * w].rearrange("p (g e) -> p g e", g=G), AX_X, ALU.max))
                drain_inc(dve.nop(), job)

            def count_passes(l):
                cnt, nr, ps, tg = cols(rt, R_CN, G), cols(rt, R_NR, G), cols(rt, R_PS, G), cols(rt, R_TG, G)
                full = cols(rt, R_CR, G, ROUNDS)
                link(V.tensor_tensor(full, bc(cnt, 2, ROUNDS), bc(cst[:, C_FULL:C_FULL + ROUNDS], 1, G), ALU.is_gt))
                link(V.tensor_reduce(nr, full, AX_X, ALU.add))
                link(V.tensor_scalar(nr, nr, 1.0, None, ALU.max))
                link(V.tensor_scalar(ps, nr, -1.0, None, ALU.add))
                link(V.tensor_scalar(tg[:, 0:1], ub[:, :], G - 1.0, None, ALU.add))
                for g in range(1, G):
                    link(V.tensor_tensor(tg[:, g:g + 1], tg[:, g - 1:g], ps[:, g - 1:g], ALU.add))
                V.scalar_tensor_tensor(ub[:, :], ps[:, G - 1:G], 1.0, tg[:, G - 1:G], ALU.add, ALU.add)
                link(V.tensor_reduce(cnt[:, 0:1], ps, AX_X, ALU.add))
                V.tensor_copy(itab[0:1, 0:G], nr[0:1, :])
                V.tensor_copy(itab[0:1, G:2 * G], tg[0:1, :])
                V.tensor_copy(itab[0:1, 8:9], ub[0:1, :])
                V.tensor_copy(itab[0:1, 9:10], cnt[0:1, 0:1]).then_inc(keys_rdy, 1)
                dve.wait_ge(keys_rdy, l + 2)

            def expert_pass(u, g, meanwhile=None):
                kt = cols(rt, R_KT, TT, E)
                keys = cols(rt, R_KY, TT, G * E)[:, :, bass.ds(g * E, E)]
                V.tensor_copy(kt, keys).then_inc(kt_rdy, 1)
                dve.wait_ge(kt_rdy, u + 1)
                V.tensor_scalar(keys, keys, -float(S), None, ALU.add)
                within = cols(rt, R_WI, TT, E)

                def slots(m):
                    return m.rearrange("p (e s) -> p e s", e=E)

                for k in range(TT):
                    ins = V.tensor_tensor(slots(sel[:, k, :]), bc(iota[:, 0:S], 1, E), bc(kt[:, k, :], 2, S), ALU.is_equal)
                ins.then_inc(sel_rdy, 1)
                dve.wait_ge(sel_rdy, u * 2 + 1)
                for k in range(TT):
                    ins = V.tensor_tensor(slots(selw[:, k, :]), slots(sel[:, k, :]), bc(within[:, k, :], 2, S), ALU.mult)
                ins.then_inc(sel_rdy, 1)
                if meanwhile:
                    meanwhile()
                for i in (0, 2):
                    dve.wait_ge(gat_s, u * 5 + (i + 1))
                    for c in (2 * i, 2 * i + 1):
                        ins = V.tensor_scalar(xg[:, c, :], bank[GATHER[i]][:, (c % 2) * E * S:(c % 2 + 1) * E * S],
                                              prm_ffn[:, c:c + 1], None, ALU.mult)
                    ins.then_inc(xgv_rdy, 1)
                dve.wait_ge(gat_s, u * 5 + 5)
                V.tensor_copy(selT, bank[2][:, :].rearrange("p (b s) -> p b s", b=NB)).then_inc(st_rdy, 1)
                for b in range(NB):
                    dve.wait_ge(sil_s, u * NB + (b + 1))
                    V.tensor_tensor(hid[:, b, :], bank[b][:, F:2 * F], sil[:, b, :], ALU.mult).then_inc(hid_s, 1)
                    for k in range(TT):
                        for n in range(2):
                            dve.wait_ge(sct_s, u * (4 * NB) + (4 * b + 2 * k + n + 1))
                            if b:
                                dve.wait_ge(add_s, u * (4 * NB) + (2 * k + n + 1))
                            hh = h[:, k, n * NCOL:(n + 1) * NCOL]
                            V.tensor_tensor(hh, bank[6 + n][:, :], hh, ALU.add).then_inc(add_s, 1)
                dve.wait_ge(add_s, u * (4 * NB) + 4 * NB)

            V.memset(ub[:, :], 0.0)
            V.memset(itab[:, :], 0).then_inc(keys_rdy, 1)
            dve.wait_ge(keys_rdy, 1)
            dve.wait_ge(x_in, 16)
            with dve.Fori(0, DEPTH) as l:
                before = passes_before(dve, VE, l)
                steps.at(l * V_LAYER)
                for st in ORDER:
                    if st == ("hT", 0, 0):
                        dve.wait_ge(cst_in, 16)
                        dve.wait_ge(prm_in, l * 16 + 16)
                    if st[0] == "router":
                        link(V.tensor_copy(prm_ffn[:, :], prm[:, P_NFR:P_NFR + KC]))
                    stage(l, st)
                expert_pass(before, 0, meanwhile=lambda: count_passes(l))
                assert steps.n == V_LAYER, f"V_LAYER = {steps.n}"
                settle(dve)
                with dve.Fori(1, G) as g:
                    expert_pass(before + g, g)
                more_passes(dve, VE, l, expert_pass)
            steps.at(DEPTH * V_LAYER)
            link(squares(h, xn))
            rms(DEPTH * NORMS + 1, st_[:, 16:18], st_[:, 18:20], D)
            dve.wait_ge(fin_in, 16)
            for t in range(TT):
                V.scalar_tensor_tensor(xn[:, t, :], h[:, t, :], st_[:, 18 + t:19 + t], fgain,
                                       ALU.mult, ALU.mult).then_inc(fin_s, 1)


_NAMES = ["x", "mem", "w_in", "w_ssd_o", "w_attn_o", "w_out", "w_cq", "w_ckv", "w_co", "w_group", "w_router",
          "w_gate_e", "w_up_e", "w_down_e"]


def constants():
    import numpy as np
    i = np.arange(P)
    c = np.zeros((P, C_W), np.float32)
    c[:, C_ID:C_ID + P] = np.eye(P)
    c[:, C_TRI:C_TRI + P] = i[:, None] <= i[None, :]
    c[:, C_TRIS:C_TRIS + P] = i[:, None] < i[None, :]
    c[:, C_ONE:C_ONE + P] = 1.0
    c[:, C_IOTA:C_IOTA + P] = i[None, :]
    c[:, C_CAUS:C_CAUS + P] = np.where(i[None, :] <= i[:, None], 0.0, NEG)
    inv = (1.0 / (np.float32(10000.0) ** (np.arange(0, HD, 2, dtype=np.float32) / np.float32(HD)))).astype(np.float32)
    for t in range(TT):
        ang = (t * P + i).astype(np.float32)[:, None] * inv[None, :]
        c[:, C_COS + t * HD:C_COS + (t + 1) * HD] = np.tile(np.cos(ang), (1, 2))
        c[:, C_SIN + t * HD:C_SIN + (t + 1) * HD] = np.tile(np.sin(ang), (1, 2))
    c[:, C_PRIO:C_PRIO + E] = E - np.arange(E)
    c[:, C_FULL:C_FULL + ROUNDS] = np.arange(ROUNDS) * S
    c[:, C_MH:C_MH + E] = -0.5
    return c


def small_params(a):
    import numpy as np

    def by_block(v):
        return np.moveaxis(v.reshape(DEPTH, -1, P), 2, 1)

    def repeated(v):
        return np.broadcast_to(v[:, None, :], (DEPTH, P, v.shape[-1]))

    parts = [by_block(a[n].reshape(DEPTH, -1)) for n in
             ("conv_w", "conv_b", "norm_mix", "norm_xattn", "norm_mem", "norm_ffn", "ssd_norm")]
    parts += [repeated(a[n]) for n in ("dt_bias", "a_log", "d_skip", "b_group", "b_router")]
    parts.append(a["norm_ffn"].reshape(DEPTH, P, KC))
    return np.ascontiguousarray(np.concatenate(parts, axis=2))


def kernel(**inputs):
    import numpy as np
    import concourse.bacc as _bacc
    from concourse.bass_utils import run_bass_kernel_spmd as _run

    a = {k: np.asarray(v) for k, v in inputs.items()}
    arrays = {n: np.ascontiguousarray(a[n]) for n in _NAMES}
    arrays["x"] = arrays["x"].reshape(SEQ, D)
    arrays["mem"] = arrays["mem"].reshape(SEQ, D)
    arrays["params"] = small_params(a)
    arrays["consts"] = constants()
    arrays["gain_final"] = np.ascontiguousarray(np.broadcast_to(a["norm_final"][None, :], (P, D)))
    nc = _bacc.Bacc("TRN2", target_bir_lowering=False, num_devices=1)
    args = [nc.dram_tensor(f"in_{n}", v.shape, F32, kind="ExternalInput").ap() for n, v in arrays.items()]
    out = nc.dram_tensor("out_0", (SEQ, D), F32, kind="ExternalOutput").ap()
    trunk(nc, *args, out)
    r = _run(nc, [{f"in_{n}": v for n, v in arrays.items()}], core_ids=[0])
    return r.results[0]["out_0"].reshape(1, SEQ, D)
```
